# Optimizing a Trainium2 kernel written in Bass

```python
import math
import jax, jax.numpy as jnp
from jax import lax
import numpy as np
import jax
import jax.numpy as jnp

D_MODEL = 1024
BATCH = 1
SEQ = 512
DEPTH = 1

MLSTM_HEADS = 4
MLSTM_HEAD_DIM = D_MODEL // MLSTM_HEADS
MLSTM_WIDTH = MLSTM_HEADS * MLSTM_HEAD_DIM
MLSTM_CONV = 4
MLSTM_CHUNK = 128

ATTN_GROUPS = ((128, 1), (512, 4), (2048, 16))
ATTN_HEADS_PER_GROUP = 8
ATTN_HEAD_DIM = 64
ATTN_N_GROUPS = len(ATTN_GROUPS)
ATTN_HEADS = ATTN_N_GROUPS * ATTN_HEADS_PER_GROUP
ATTN_WIDTH = ATTN_HEADS * ATTN_HEAD_DIM
ATTN_OUT = ATTN_HEADS_PER_GROUP * ATTN_HEAD_DIM
ATTN_BLOCK = 128

N_BUCKETS = 32
MAX_DISTANCE = 2048

D_FF = -(-8 * D_MODEL // (3 * 256)) * 256

EPS = 1e-6

IN_SIZES = (MLSTM_WIDTH, MLSTM_WIDTH, MLSTM_WIDTH, 2 * MLSTM_HEADS, MLSTM_WIDTH,
            ATTN_WIDTH, ATTN_WIDTH, ATTN_WIDTH, 2 * D_MODEL)
IN_WIDTH = sum(IN_SIZES)


def _split_points(sizes):
    pts, acc = [], 0
    for s in sizes[:-1]:
        acc += s
        pts.append(acc)
    return pts

def rmsnorm(x, g):
    xf = x.astype(jnp.float32)
    r = lax.rsqrt(jnp.mean(xf * xf, axis=-1, keepdims=True) + EPS)
    return (xf * r * g.astype(jnp.float32)).astype(x.dtype)

def rel_bucket(n):
    max_exact = N_BUCKETS // 2
    nf = jnp.maximum(n, 1).astype(jnp.float32)
    large = max_exact + (jnp.log(nf / max_exact) / math.log(MAX_DISTANCE / max_exact)
                         * (N_BUCKETS - max_exact)).astype(jnp.int32)
    large = jnp.minimum(large, N_BUCKETS - 1)
    return jnp.where(n < max_exact, n, large)

def causal_depthwise_conv(x, w, b):
    c = x.shape[-1]
    y = lax.conv_general_dilated(x, w[:, None, :].astype(x.dtype), window_strides=(1,),
                                 padding=[(MLSTM_CONV - 1, 0)],
                                 dimension_numbers=('NWC', 'WIO', 'NWC'),
                                 feature_group_count=c)
    return y + b.astype(x.dtype)

def _mlstm_chunk_step(carry, inp):
    C, n, m = carry
    q, k, v, ig, lf = inp
    L = q.shape[-2]
    b = jnp.cumsum(lf, axis=-1)
    causal = jnp.tril(jnp.ones((L, L), dtype=bool))
    dmat = jnp.where(causal, b[..., :, None] - b[..., None, :] + ig[..., None, :], -jnp.inf)
    inter = b + m[..., None]
    m_t = jnp.maximum(inter, jnp.max(dmat, axis=-1))
    w_intra = jnp.exp(dmat - m_t[..., None]) * jnp.einsum('bhtd,bhsd->bhts', q, k)
    w_inter = jnp.exp(inter - m_t)
    num = (w_inter[..., None] * jnp.einsum('bhtd,bhde->bhte', q, C)
           + jnp.einsum('bhts,bhse->bhte', w_intra, v))
    den = w_inter * jnp.einsum('bhtd,bhd->bht', q, n) + jnp.sum(w_intra, axis=-1)
    h = num / jnp.maximum(jnp.abs(den), jnp.exp(-m_t))[..., None]
    b_last = b[..., -1]
    a = b_last[..., None] - b + ig
    m_new = jnp.maximum(b_last + m, jnp.max(a, axis=-1))
    decay = jnp.exp(b_last + m - m_new)
    wk = jnp.exp(a - m_new[..., None])
    C_new = decay[..., None, None] * C + jnp.einsum('bhs,bhsd,bhse->bhde', wk, k, v)
    n_new = decay[..., None] * n + jnp.einsum('bhs,bhsd->bhd', wk, k)
    return (C_new, n_new, m_new), h

def mlstm_cell(q, k, v, ig, lf):
    B, S, H, d = q.shape
    nc = S // MLSTM_CHUNK
    to_c = lambda t: t.reshape(B, nc, MLSTM_CHUNK, H, d).transpose(1, 0, 3, 2, 4)
    to_cg = lambda t: t.reshape(B, nc, MLSTM_CHUNK, H).transpose(1, 0, 3, 2)
    init = (jnp.zeros((B, H, d, d), jnp.float32), jnp.zeros((B, H, d), jnp.float32),
            jnp.zeros((B, H), jnp.float32))
    _, hs = lax.scan(_mlstm_chunk_step, init, (to_c(q), to_c(k), to_c(v), to_cg(ig), to_cg(lf)))
    return hs.transpose(1, 0, 3, 2, 4).reshape(B, S, H, d)

def dilated_window_attention(q, k, v, bias_tab, window, dilation):
    B, S, Hg, dh = q.shape
    span = window // dilation
    blk = ATTN_BLOCK
    sd = S // dilation
    nb = -(-sd // blk)
    pad = nb * blk - sd

    def to_blocks(t):
        t = t.reshape(B, sd, dilation, Hg, dh).transpose(0, 2, 3, 1, 4)
        t = jnp.pad(t, ((0, 0), (0, 0), (0, 0), (0, pad), (0, 0)))
        return t.reshape(B, dilation, Hg, nb, blk, dh)

    def with_prev(t):
        prev = jnp.pad(t, ((0, 0), (0, 0), (0, 0), (1, 0), (0, 0), (0, 0)))[:, :, :, :-1]
        return jnp.concatenate([prev, t], axis=-2)

    qb = to_blocks(q)
    kk = with_prev(to_blocks(k))
    vv = with_prev(to_blocks(v))

    q_pos = jnp.arange(blk)[:, None] + blk
    k_pos = jnp.arange(2 * blk)[None, :]
    dist = q_pos - k_pos
    key_idx = jnp.arange(nb)[:, None, None] * blk - blk + k_pos[None]
    valid = (dist >= 0) & (dist <= span) & (key_idx >= 0)
    bias = bias_tab[rel_bucket(jnp.maximum(dist, 0) * dilation)]
    bias = jnp.moveaxis(bias, -1, 0).astype(jnp.float32)[:, None]

    s = jnp.einsum('brhnqd,brhnkd->brhnqk', qb, kk) * (dh ** -0.5) + bias
    s = jnp.where(valid, s, -jnp.inf)
    mx = jnp.max(s, axis=-1, keepdims=True)
    p = jnp.exp(s - mx)
    l = jnp.sum(p, axis=-1)
    o = jnp.einsum('brhnqk,brhnkd->brhnqd', p, vv) / l[..., None]
    lse = mx[..., 0] + jnp.log(l)

    o = o.reshape(B, dilation, Hg, nb * blk, dh)[:, :, :, :sd]
    o = o.transpose(0, 3, 1, 2, 4).reshape(B, S, Hg, dh)
    lse = lse.reshape(B, dilation, Hg, nb * blk)[:, :, :, :sd]
    lse = lse.transpose(0, 3, 1, 2).reshape(B, S, Hg)
    return o, lse

def hybrid_layer(x, rel_bias, norm_mix_g, w_in, b_gate_if, conv_w, conv_b, mlstm_norm_g,
                 w_proj_a, w_proj_b, w_out, norm_ffn_g, w_gate, w_up, w_down):
    B, S, _ = x.shape
    f32 = jnp.float32
    h = rmsnorm(x, norm_mix_g)
    proj = h @ w_in
    q_m, k_m, v_m, if_pre, o_pre, q_a, k_a, v_a, gate_pre = jnp.split(
        proj, _split_points(IN_SIZES), axis=-1)

    qk = jax.nn.silu(causal_depthwise_conv(jnp.concatenate([q_m, k_m], axis=-1), conv_w, conv_b))
    q_m, k_m = jnp.split(qk.astype(f32), 2, axis=-1)
    q_m = q_m.reshape(B, S, MLSTM_HEADS, MLSTM_HEAD_DIM) * (MLSTM_HEAD_DIM ** -0.5)
    k_m = k_m.reshape(B, S, MLSTM_HEADS, MLSTM_HEAD_DIM)
    v_m = v_m.astype(f32).reshape(B, S, MLSTM_HEADS, MLSTM_HEAD_DIM)
    if_pre = if_pre.astype(f32) + b_gate_if.astype(f32)
    ig = if_pre[..., :MLSTM_HEADS]
    lf = jax.nn.log_sigmoid(if_pre[..., MLSTM_HEADS:])
    hm = mlstm_cell(q_m, k_m, v_m, ig, lf)
    mu = jnp.mean(hm, axis=-1, keepdims=True)
    var = jnp.mean(jnp.square(hm - mu), axis=-1, keepdims=True)
    hm = (hm - mu) * lax.rsqrt(var + EPS)
    hm = hm.reshape(B, S, MLSTM_WIDTH) * mlstm_norm_g.astype(f32)
    y_a = (jax.nn.sigmoid(o_pre.astype(f32)) * hm).astype(x.dtype)

    shp = (B, S, ATTN_N_GROUPS, ATTN_HEADS_PER_GROUP, ATTN_HEAD_DIM)
    q_a = q_a.astype(f32).reshape(shp)
    k_a = k_a.astype(f32).reshape(shp)
    v_a = v_a.astype(f32).reshape(shp)
    outs, lses = [], []
    for g, (window, dilation) in enumerate(ATTN_GROUPS):
        tab = rel_bias[:, g * ATTN_HEADS_PER_GROUP:(g + 1) * ATTN_HEADS_PER_GROUP]
        o_g, lse_g = dilated_window_attention(q_a[:, :, g], k_a[:, :, g], v_a[:, :, g],
                                              tab, window, dilation)
        outs.append(o_g)
        lses.append(lse_g)
    wts = jax.nn.softmax(jnp.stack(lses, axis=0), axis=0)
    y_b = jnp.sum(wts[..., None] * jnp.stack(outs, axis=0), axis=0)
    y_b = y_b.reshape(B, S, ATTN_OUT).astype(x.dtype)

    g_a, g_b = jnp.split(jax.nn.sigmoid(gate_pre), 2, axis=-1)
    merged = g_a * (y_a @ w_proj_a) + g_b * (y_b @ w_proj_b)
    x = x + merged @ w_out

    hf = rmsnorm(x, norm_ffn_g)
    x = x + (jax.nn.silu(hf @ w_gate) * (hf @ w_up)) @ w_down
    return x

def first_inputs(seed: int = 0) -> dict:
    key = jax.random.key(seed)
    ks = jax.random.split(key, 20)
    nrm = lambda k, shape, scale: jax.random.normal(k, shape, jnp.float32) * scale
    x = jax.random.normal(ks[0], (BATCH, SEQ, D_MODEL), jnp.float32)
    norm_mix_g = 1.0 + nrm(ks[1], (DEPTH, D_MODEL), 0.02)
    w_in = nrm(ks[2], (DEPTH, D_MODEL, IN_WIDTH), D_MODEL ** -0.5)
    ig_bias = nrm(ks[3], (DEPTH, MLSTM_HEADS), 0.1)
    fg_bias = jnp.linspace(3.0, 6.0, MLSTM_HEADS, dtype=jnp.float32)[None] + nrm(ks[4], (DEPTH, MLSTM_HEADS), 0.1)
    b_gate_if = jnp.concatenate([ig_bias, fg_bias], axis=-1)
    conv_w = nrm(ks[5], (DEPTH, MLSTM_CONV, 2 * MLSTM_WIDTH), MLSTM_CONV ** -0.5)
    conv_b = nrm(ks[6], (DEPTH, 2 * MLSTM_WIDTH), 0.02)
    mlstm_norm_g = 1.0 + nrm(ks[7], (DEPTH, MLSTM_WIDTH), 0.02)
    w_proj_a = nrm(ks[8], (DEPTH, MLSTM_WIDTH, D_MODEL), MLSTM_WIDTH ** -0.5)
    w_proj_b = nrm(ks[9], (DEPTH, ATTN_OUT, D_MODEL), ATTN_OUT ** -0.5)
    w_out = nrm(ks[10], (DEPTH, D_MODEL, D_MODEL), D_MODEL ** -0.5)
    norm_ffn_g = 1.0 + nrm(ks[11], (DEPTH, D_MODEL), 0.02)
    w_gate = nrm(ks[12], (DEPTH, D_MODEL, D_FF), D_MODEL ** -0.5)
    w_up = nrm(ks[13], (DEPTH, D_MODEL, D_FF), D_MODEL ** -0.5)
    w_down = nrm(ks[14], (DEPTH, D_FF, D_MODEL), D_FF ** -0.5)
    rel_bias = nrm(ks[15], (N_BUCKETS, ATTN_HEADS), 0.5)
    norm_final_g = 1.0 + nrm(ks[16], (D_MODEL,), 0.02)
    return {"x": x, "norm_mix_g": norm_mix_g, "w_in": w_in, "b_gate_if": b_gate_if,
            "conv_w": conv_w, "conv_b": conv_b, "mlstm_norm_g": mlstm_norm_g,
            "w_proj_a": w_proj_a, "w_proj_b": w_proj_b, "w_out": w_out,
            "norm_ffn_g": norm_ffn_g, "w_gate": w_gate, "w_up": w_up, "w_down": w_down,
            "rel_bias": rel_bias, "norm_final_g": norm_final_g}

def first_block(x, norm_mix_g, w_in, b_gate_if, conv_w, conv_b, mlstm_norm_g, w_proj_a,
              w_proj_b, w_out, norm_ffn_g, w_gate, w_up, w_down, rel_bias, norm_final_g):
    for layer in range(DEPTH):
        x = hybrid_layer(x, rel_bias, norm_mix_g[layer], w_in[layer], b_gate_if[layer],
                         conv_w[layer], conv_b[layer], mlstm_norm_g[layer], w_proj_a[layer],
                         w_proj_b[layer], w_out[layer], norm_ffn_g[layer], w_gate[layer],
                         w_up[layer], w_down[layer])
    return rmsnorm(x, norm_final_g)


GLA_HEADS = 4
GLA_DK = 128
GLA_DV = 256
GLA_GATE_RANK = 16
GLA_TAU = 16.0
GLA_CHUNK = 64
NSA_HEADS = 8
NSA_GROUPS = 2
NSA_REP = NSA_HEADS // NSA_GROUPS
NSA_DH = 64
NSA_CMP_LEN = 32
NSA_CMP_STRIDE = 16
NSA_SLC_LEN = 64
NSA_N_SEL = 16
NSA_WINDOW = 512
NSA_Q_BLOCK = 128
D_FF_2 = 2816
RMS_EPS = 1e-6
NEG = -1e30

GLA_QK_W = GLA_HEADS * GLA_DK
GLA_V_W = GLA_HEADS * GLA_DV
NSA_Q_W = NSA_HEADS * NSA_DH
NSA_KV_W = NSA_GROUPS * NSA_DH
NSA_GATE_W = NSA_HEADS * 3
IN_SPLITS = (GLA_QK_W, GLA_QK_W, GLA_V_W, GLA_V_W, GLA_GATE_RANK,
             NSA_Q_W, NSA_KV_W, NSA_KV_W, NSA_KV_W, NSA_KV_W, NSA_KV_W, NSA_KV_W,
             NSA_GATE_W, D_MODEL, D_MODEL)
IN_WIDTH_2 = 4 * GLA_QK_W // 2 + 2 * GLA_V_W + GLA_GATE_RANK + NSA_Q_W + 6 * NSA_KV_W + NSA_GATE_W + 2 * D_MODEL


def rms_norm(x, g):
    xf = x.astype(jnp.float32)
    y = xf * lax.rsqrt(jnp.mean(xf * xf, axis=-1, keepdims=True) + RMS_EPS)
    return (y * g.astype(jnp.float32)).astype(x.dtype)

def masked_softmax(s, mask):
    s = jnp.where(mask, s, NEG)
    p = jax.nn.softmax(s, axis=-1)
    return jnp.where(mask, p, 0.0)

def gla_mixer(q, k, v, r, a_lr, w_alpha2, b_alpha, norm_g):
    B, S = q.shape[0], q.shape[1]
    C = GLA_CHUNK
    nc = S // C

    def heads(t, d):
        return t.reshape(B, nc, C, GLA_HEADS, d).transpose(0, 3, 1, 2, 4).astype(jnp.float32)

    qh = heads(q, GLA_DK) * (GLA_DK ** -0.5)
    kh = heads(k, GLA_DK)
    vh = heads(v, GLA_DV)
    log_a = jax.nn.log_sigmoid((a_lr @ w_alpha2 + b_alpha).astype(jnp.float32)) / GLA_TAU
    b = jnp.cumsum(heads(log_a, GLA_DK), axis=3)
    b_last = b[:, :, :, -1:, :]
    qe = qh * jnp.exp(b)
    ke = kh * jnp.exp(-b)
    kd = kh * jnp.exp(b_last - b)
    causal = jnp.tril(jnp.ones((C, C), dtype=bool))
    attn = jnp.where(causal, jnp.einsum('bhncd,bhnsd->bhncs', qe, ke), 0.0)
    o = jnp.einsum('bhncs,bhnse->bhnce', attn, vh)
    upd = jnp.einsum('bhncd,bhnce->nbhde', kd, vh)
    decay = jnp.exp(b_last[:, :, :, 0, :]).transpose(2, 0, 1, 3)

    def step(state, inp):
        dec, u = inp
        return dec[..., None] * state + u, state

    init = jnp.zeros((B, GLA_HEADS, GLA_DK, GLA_DV), jnp.float32)
    _, s_prev = lax.scan(step, init, (decay, upd))
    o = o + jnp.einsum('bhncd,nbhde->bhnce', qe, s_prev)
    o = o * lax.rsqrt(jnp.mean(o * o, axis=-1, keepdims=True) + RMS_EPS) * norm_g.astype(jnp.float32)
    o = o.reshape(B, GLA_HEADS, S, GLA_DV).transpose(0, 2, 1, 3).reshape(B, S, GLA_V_W)
    return (o * jax.nn.silu(r.astype(jnp.float32))).astype(r.dtype)

def nsa_mixer(q, k_c, v_c, k_s, v_s, k_w, v_w, gate_logits, pe_k, w1_k, w2_k, pe_v, w1_v, w2_v):
    B, S = q.shape[0], q.shape[1]
    G, R, DH = NSA_GROUPS, NSA_REP, NSA_DH
    L, ST, SL, QB, W = NSA_CMP_LEN, NSA_CMP_STRIDE, NSA_SLC_LEN, NSA_Q_BLOCK, NSA_WINDOW
    qh = q.reshape(B, S, G, R, DH).transpose(0, 2, 3, 1, 4).astype(jnp.float32) * (DH ** -0.5)

    def kv_heads(t):
        return t.reshape(B, S, G, DH).transpose(0, 2, 1, 3).astype(jnp.float32)

    gates = jax.nn.sigmoid(gate_logits.astype(jnp.float32)).reshape(B, S, G, R, 3).transpose(0, 2, 3, 1, 4)
    h_idx = jnp.arange(NSA_HEADS, dtype=jnp.float32)
    slopes = jnp.exp2(-8.0 * (h_idx + 1.0) / NSA_HEADS).reshape(1, G, R, 1, 1)

    n_cmp = (S - L) // ST + 1
    starts_c = ST * jnp.arange(n_cmp)
    idx_c = starts_c[:, None] + jnp.arange(L)[None, :]

    def compress(t, pe, w1, w2):
        blocks = t[:, :, idx_c] + pe
        flat = blocks.reshape(B, G, n_cmp, L * DH)
        return jax.nn.silu(flat @ w1) @ w2

    kc = compress(kv_heads(k_c), pe_k, w1_k, w2_k).astype(jnp.float32)
    vc = compress(kv_heads(v_c), pe_v, w1_v, w2_v).astype(jnp.float32)
    end_c = starts_c + L - 1

    n_slc = S // SL
    n_sel = min(NSA_N_SEL, n_slc)
    starts_s = SL * jnp.arange(n_slc)
    ov = jnp.clip(jnp.minimum(starts_c[:, None] + L, starts_s[None, :] + SL)
                  - jnp.maximum(starts_c[:, None], starts_s[None, :]), 0, None).astype(jnp.float32) / L
    ks_blocks = kv_heads(k_s).reshape(B, G, n_slc, SL, DH)
    vs_blocks = kv_heads(v_s).reshape(B, G, n_slc, SL, DH)
    gather = jax.vmap(jax.vmap(lambda blk, ix: blk[ix]))

    kw_pad = jnp.pad(kv_heads(k_w), ((0, 0), (0, 0), (W, 0), (0, 0)))
    vw_pad = jnp.pad(kv_heads(v_w), ((0, 0), (0, 0), (W, 0), (0, 0)))

    nq = S // QB
    q_blocks = qh.reshape(B, G, R, nq, QB, DH).transpose(3, 0, 1, 2, 4, 5)
    g_blocks = gates.reshape(B, G, R, nq, QB, 3).transpose(3, 0, 1, 2, 4, 5)
    jb = jnp.arange(n_slc)
    r_w = jnp.arange(W + QB)

    def attend_block(args):
        i, qb, gb = args
        q0 = i * QB
        t = q0 + jnp.arange(QB)
        tf = t.astype(jnp.float32)
        dist_c = tf[:, None] - end_c[None, :].astype(jnp.float32)
        s_c = jnp.einsum('bgrqd,bgnd->bgrqn', qb, kc) - slopes * dist_c
        p_c = masked_softmax(s_c, end_c[None, :] <= t[:, None])
        o_c = jnp.einsum('bgrqn,bgnd->bgrqd', p_c, vc)
        imp = jnp.einsum('bgrqn,nj->bgqj', p_c, ov)
        cur = t // SL
        forced = (jb[None, :] == 0) | (jb[None, :] == cur[:, None]) | (jb[None, :] == cur[:, None] - 1)
        score = jnp.where(jb[None, :] > cur[:, None], NEG, jnp.where(forced, -NEG, imp))
        _, sel = lax.top_k(score, n_sel)
        ks = gather(ks_blocks, sel).reshape(B, G, QB, n_sel * SL, DH)
        vs = gather(vs_blocks, sel).reshape(B, G, QB, n_sel * SL, DH)
        pos_s = (sel[..., None] * SL + jnp.arange(SL)).reshape(B, G, QB, n_sel * SL)
        dist_s = (tf[None, None, :, None] - pos_s.astype(jnp.float32))[:, :, None]
        s_s = jnp.einsum('bgrqd,bgqkd->bgrqk', qb, ks) - slopes * dist_s
        p_s = masked_softmax(s_s, (pos_s <= t[None, None, :, None])[:, :, None])
        o_s = jnp.einsum('bgrqk,bgqkd->bgrqd', p_s, vs)
        kw = lax.dynamic_slice_in_dim(kw_pad, q0, W + QB, axis=2)
        vw = lax.dynamic_slice_in_dim(vw_pad, q0, W + QB, axis=2)
        pos_w = q0 - W + r_w
        dist_w = t[:, None] - pos_w[None, :]
        mask_w = (pos_w[None, :] >= 0) & (dist_w >= 0) & (dist_w < W)
        s_w = jnp.einsum('bgrqd,bgkd->bgrqk', qb, kw) - slopes * dist_w.astype(jnp.float32)
        p_w = masked_softmax(s_w, mask_w)
        o_w = jnp.einsum('bgrqk,bgkd->bgrqd', p_w, vw)
        return gb[..., 0:1] * o_c + gb[..., 1:2] * o_s + gb[..., 2:3] * o_w

    o = lax.map(attend_block, (jnp.arange(nq), q_blocks, g_blocks))
    return o.transpose(1, 0, 4, 2, 3, 5).reshape(B, S, NSA_Q_W).astype(q.dtype)

def second_inputs(seed: int = 0) -> dict:
    key = jax.random.key(seed)
    ks = jax.random.split(key, 24)
    f32 = jnp.float32

    def normal(k, shape, fan_in):
        return jax.random.normal(k, shape, f32) * (fan_in ** -0.5)

    def gain(k, shape):
        return 1.0 + 0.1 * jax.random.normal(k, shape, f32)

    Ld = DEPTH
    return {
        'x': jax.random.normal(ks[0], (BATCH, SEQ, D_MODEL), f32),
        'norm_mix_pre': gain(ks[1], (Ld, D_MODEL)),
        'norm_mix_post': gain(ks[2], (Ld, D_MODEL)),
        'norm_ffn_pre': gain(ks[3], (Ld, D_MODEL)),
        'norm_ffn_post': gain(ks[4], (Ld, D_MODEL)),
        'w_in': normal(ks[5], (Ld, D_MODEL, IN_WIDTH_2), D_MODEL),
        'gla_w_alpha2': normal(ks[6], (Ld, GLA_GATE_RANK, GLA_QK_W), GLA_GATE_RANK),
        'gla_b_alpha': 0.1 * jax.random.normal(ks[7], (Ld, GLA_QK_W), f32),
        'gla_norm_g': gain(ks[8], (Ld, GLA_DV)),
        'nsa_cmp_pe_k': 0.1 * jax.random.normal(ks[9], (Ld, NSA_CMP_LEN, NSA_DH), f32),
        'nsa_cmp_w1_k': normal(ks[10], (Ld, NSA_CMP_LEN * NSA_DH, NSA_DH), NSA_CMP_LEN * NSA_DH),
        'nsa_cmp_w2_k': normal(ks[11], (Ld, NSA_DH, NSA_DH), NSA_DH),
        'nsa_cmp_pe_v': 0.1 * jax.random.normal(ks[12], (Ld, NSA_CMP_LEN, NSA_DH), f32),
        'nsa_cmp_w1_v': normal(ks[13], (Ld, NSA_CMP_LEN * NSA_DH, NSA_DH), NSA_CMP_LEN * NSA_DH),
        'nsa_cmp_w2_v': normal(ks[14], (Ld, NSA_DH, NSA_DH), NSA_DH),
        'w_proj_gla': normal(ks[15], (Ld, GLA_V_W, D_MODEL), GLA_V_W),
        'w_proj_nsa': normal(ks[16], (Ld, NSA_Q_W, D_MODEL), NSA_Q_W),
        'w_out': normal(ks[17], (Ld, D_MODEL, D_MODEL), D_MODEL),
        'w_ffn_gate': normal(ks[18], (Ld, D_MODEL, D_FF_2), D_MODEL),
        'w_ffn_up': normal(ks[19], (Ld, D_MODEL, D_FF_2), D_MODEL),
        'w_ffn_down': normal(ks[20], (Ld, D_FF_2, D_MODEL), D_FF_2),
    }

def second_block(x, norm_mix_pre, norm_mix_post, norm_ffn_pre, norm_ffn_post, w_in,
              gla_w_alpha2, gla_b_alpha, gla_norm_g,
              nsa_cmp_pe_k, nsa_cmp_w1_k, nsa_cmp_w2_k, nsa_cmp_pe_v, nsa_cmp_w1_v, nsa_cmp_w2_v,
              w_proj_gla, w_proj_nsa, w_out, w_ffn_gate, w_ffn_up, w_ffn_down):
    split_points = [int(c) for c in np.cumsum(IN_SPLITS)[:-1]]
    for l in range(DEPTH):
        h = rms_norm(x, norm_mix_pre[l])
        proj = h @ w_in[l]
        (g_q, g_k, g_v, g_r, g_a, n_q, n_kc, n_vc, n_ks, n_vs, n_kw, n_vw,
         n_gate, merge_gla, merge_nsa) = jnp.split(proj, split_points, axis=-1)
        o_gla = gla_mixer(g_q, g_k, g_v, g_r, g_a, gla_w_alpha2[l], gla_b_alpha[l], gla_norm_g[l])
        o_nsa = nsa_mixer(n_q, n_kc, n_vc, n_ks, n_vs, n_kw, n_vw, n_gate,
                          nsa_cmp_pe_k[l], nsa_cmp_w1_k[l], nsa_cmp_w2_k[l],
                          nsa_cmp_pe_v[l], nsa_cmp_w1_v[l], nsa_cmp_w2_v[l])
        mixed = (jax.nn.sigmoid(merge_gla) * (o_gla @ w_proj_gla[l])
                 + jax.nn.sigmoid(merge_nsa) * (o_nsa @ w_proj_nsa[l]))
        x = x + rms_norm(mixed @ w_out[l], norm_mix_post[l])
        h = rms_norm(x, norm_ffn_pre[l])
        f = (jax.nn.silu(h @ w_ffn_gate[l]) * (h @ w_ffn_up[l])) @ w_ffn_down[l]
        x = x + rms_norm(f, norm_ffn_post[l])
    return x


def setup_inputs(seed=0):
    out = dict(first_inputs(seed))
    for name, value in second_inputs(seed + 1).items():
        if name != "x":
            out[name + "_2"] = value
    return out


def reference(
    x, norm_mix_g, w_in, b_gate_if, conv_w, conv_b, mlstm_norm_g, w_proj_a, w_proj_b, w_out,
    norm_ffn_g, w_gate, w_up, w_down, rel_bias, norm_final_g, norm_mix_pre_2, norm_mix_post_2,
    norm_ffn_pre_2, norm_ffn_post_2, w_in_2, gla_w_alpha2_2, gla_b_alpha_2, gla_norm_g_2,
    nsa_cmp_pe_k_2, nsa_cmp_w1_k_2, nsa_cmp_w2_k_2, nsa_cmp_pe_v_2, nsa_cmp_w1_v_2,
    nsa_cmp_w2_v_2, w_proj_gla_2, w_proj_nsa_2, w_out_2, w_ffn_gate_2, w_ffn_up_2, w_ffn_down_2,
):
    x = first_block(
        x, norm_mix_g, w_in, b_gate_if, conv_w, conv_b, mlstm_norm_g, w_proj_a, w_proj_b, w_out,
        norm_ffn_g, w_gate, w_up, w_down, rel_bias, norm_final_g,
    )
    return second_block(
        x, norm_mix_pre_2, norm_mix_post_2, norm_ffn_pre_2, norm_ffn_post_2, w_in_2,
        gla_w_alpha2_2, gla_b_alpha_2, gla_norm_g_2, nsa_cmp_pe_k_2, nsa_cmp_w1_k_2,
        nsa_cmp_w2_k_2, nsa_cmp_pe_v_2, nsa_cmp_w1_v_2, nsa_cmp_w2_v_2, w_proj_gla_2,
        w_proj_nsa_2, w_out_2, w_ffn_gate_2, w_ffn_up_2, w_ffn_down_2,
    )


_drawn_inputs = setup_inputs


def setup_inputs(seed=0):
    import zlib

    import numpy as np

    out = dict(_drawn_inputs(seed))
    spreads = {}
    factors = {'conv_b': 5.586, 'mlstm_norm_g': 4.632, 'nsa_cmp_pe_k_2': 29.98, 'norm_ffn_g': 3.435}
    for name, (base, spread) in spreads.items():
        noise = np.random.default_rng([zlib.crc32(name.encode()), seed]).standard_normal(out[name].shape)
        drawn = base * np.exp(spread * noise) if base else spread * noise
        out[name] = jnp.asarray(drawn.astype(out[name].dtype))
    for name, factor in factors.items():
        out[name] = (out[name] * factor).astype(out[name].dtype)
    return out
```

```python
import numpy as np
import concourse.bass as bass
from concourse import mybir
from contextlib import ExitStack

D = 1024
S = 512
DFF = 2816
NR = 3
NW = 3
FFN_PARTS = [(0, 8), (8, 16), (16, 22)]
EPS = 1e-6
NEG = -1e30

COLS = {}
_at = 0
for _name, _n in [("mix_g", 8), ("conv_w", 64), ("conv_b", 16), ("mnorm", 8), ("ffn_g", 8), ("final_g", 8),
                  ("pre2", 8), ("post2", 8), ("fpre2", 8), ("fpost2", 8), ("balpha", 4), ("glag", 2),
                  ("bif", 2), ("eps", 1), ("one", 1), ("pek", 32), ("pev", 32)]:
    COLS[_name] = _at
    _at += _n
NCOL = _at

CON = {}
_at = 0
for _name, _n in [("ident", 128), ("big", 128), ("mean", 128), ("sel", 512), ("ba", 512), ("bc", 124),
                  ("m01", 124), ("glam", 64), ("reset", 512)]:
    CON[_name] = _at
    _at += _n
NCON = _at


def unit_order():
    u = []

    def add(name, j, k0=0, k=8):
        u.append((name, j, k0, k))

    def ffn(sfx):
        for a, b in FFN_PARTS:
            for t in range(a, b):
                add("gate" + sfx, t)
                add("up" + sfx, t)
            for j in range(8):
                add("down" + sfx, j, a, b - a)

    def head(h):
        for n in ("qm", "km", "vm"):
            for j in (0, 1):
                add(n, 2 * h + j)

    def pair(hp):
        for g in range(3):
            for n in ("qa", "ka", "va"):
                add(n, 4 * g + hp)

    add("if", 0)
    head(0)
    for h in range(4):
        add("om", 2 * h)
        add("om", 2 * h + 1)
        if h < 3:
            head(h + 1)
    pair(0)
    for j in range(8):
        add("ga", j)
        add("pa", j)
    for hp in range(3):
        pair(hp + 1)
    for j in range(8):
        add("gb", j)
    for j in range(8):
        add("pb", j, 0, 4)
    for j in range(8):
        add("out", j)
    ffn("")

    add("small2", 0)
    for h in range(4):
        for n, j in (("gq", h), ("gk", h), ("gv", 2 * h), ("gv", 2 * h + 1)):
            add(n, j)
        add("gr", 2 * h)
        add("gr", 2 * h + 1)
    v = u[-24:]
    del u[-24:]
    u += v[0:4]
    for h in range(4):
        u += v[6 * h + 4:6 * h + 6]
        if h < 3:
            u += v[6 * h + 6:6 * h + 10]
    for i in range(4):
        add("nq", i)
    for n in ("kc", "vc", "ks", "kw", "vs", "vw"):
        add(n, 0)
    for j in range(8):
        add("mg", j)
        add("pg", j)
        add("mn", j)
    for j in range(8):
        add("pn", j, 0, 4)
    for j in range(8):
        add("out2", j)
    ffn("2")
    return u


class Queue:

    def __init__(self, sem):
        self.sem, self.n, self.items, self.seen = sem, 0, [], {}

    def wait(self, *tokens):
        for t in tokens:
            if t is None:
                continue
            if isinstance(t, list):
                self.wait(*t)
                continue
            sem, v = t
            if self.seen.get(id(sem), 0) < v:
                self.seen[id(sem)] = v
                self.items.append((None, sem, v))

    def op(self, fn, *tokens):
        self.wait(*tokens)
        self.n += 1
        self.items.append((fn, self.sem, 1))
        return (self.sem, self.n)

    def quiet(self, fn, *tokens):
        self.wait(*tokens)
        self.items.append((fn, None, 0))

    def dma(self, fn, chan, *tokens):
        self.wait(*tokens)
        chan[1] += 16
        self.items.append((fn, chan[0], 16))
        return (chan[0], chan[1])

    def last(self):
        return (self.sem, self.n) if self.n else None

    def replay(self, eng):
        for fn, sem, v in self.items:
            if fn is None:
                eng.wait_ge(sem, v)
            elif sem is None:
                fn()
            else:
                fn().then_inc(sem, v)


def build(nc, xT_d, wst_d, con_d, col_d, relb_d, oh_d, wa2_d, w1k_d, w1v_d, w2_d, out_d, scr_d):
    f32 = mybir.dt.float32
    r32 = mybir.dt.float32r
    i32 = mybir.dt.int32
    ALU = mybir.AluOpType
    ACT = mybir.ActivationFunctionType
    AX = mybir.AxisListType.X
    ctx = ExitStack()
    with ctx:
        def sb(name, shape, dt=f32):
            return ctx.enter_context(nc.sbuf_tensor(name, shape, dt))

        def sem(name):
            return ctx.enter_context(nc.semaphore(name))

        ARN = 20288
        XT = sb("XT", [128, 8, 512])
        HH = sb("HH", [128, 8, 512], r32)
        HL = sb("HL", [128, 8, 512], r32)
        AH = sb("AH", [128, 8, 512], r32)
        AL = sb("AL", [128, 8, 512], r32)
        RAW = sb("RAW", [128, NR, 1024])
        WH = sb("WH", [128, NW, 1024], r32)
        WL = sb("WL", [128, NW, 1024], r32)
        C = sb("C", [128, NCON])
        COL = sb("COL", [128, NCOL])
        AR = sb("AR", [128, ARN])
        PS = ctx.enter_context(nc.psum_tensor("PS", [128, 8, 512], f32))

        PE = Queue(sem("s_pe"))
        AC = Queue(sem("s_act"))
        DV = Queue(sem("s_dve"))
        GP = Queue(sem("s_pool"))
        SP = Queue(sem("s_sp"))
        s_raw = [[sem(f"s_raw{i}"), 0] for i in range(NR)]
        d_con = [sem("d_con"), 0]
        d_x = [sem("d_x"), 0]
        d_vec = [sem("d_vec"), 0]
        d_bias = [[sem(f"d_bias{i}"), 0] for i in range(2)]
        d_b2 = [sem("d_b2"), 0]
        d_out = [sem("d_out"), 0]
        V, A, T = nc.vector, nc.scalar, nc.tensor

        def f(ap):
            return ap.bitcast(f32)

        def col(name, j=0, p0=0, p1=128):
            return COL[p0:p1, COLS[name] + j:COLS[name] + j + 1]

        def con(name, a=0, b=None, p0=0, p1=128):
            n = {"ident": 128, "big": 128, "mean": 128, "sel": 512, "ba": 512, "bc": 124, "m01": 124, "glam": 64,
                 "reset": 512}[name]
            return C[p0:p1, CON[name] + a:CON[name] + (n if b is None else b)]

        class Arena:
            def __init__(self, at):
                self.at = at

            def __call__(self, n):
                o = self.at
                self.at += n
                assert self.at <= ARN, self.at
                return AR[:, o:o + n]

        def ident(n=128):
            return con("ident", 0, n, 0, n)

        def act(out, in_, func, *tok, **kw):
            return AC.op(lambda: A.activation(out, in_, func, **kw), *tok)

        def acopy(out, in_, *tok, scale=1.0):
            return AC.op(lambda: A.activation(out, in_, ACT.Copy, scale=scale), *tok)

        def tt(out, a, b, op, *tok):
            return DV.op(lambda: V.tensor_tensor(out, a, b, op), *tok)

        def ts(out, a, s1, s2, op0, op1, *tok):
            return DV.op(lambda: V.tensor_scalar(out, a, s1, s2, op0, op1), *tok)

        def stt(out, a, s, b, op0, op1, *tok):
            return DV.op(lambda: V.scalar_tensor_tensor(out=out, in0=a, scalar=s, in1=b, op0=op0, op1=op1), *tok)

        def vcopy(out, in_, *tok):
            return DV.op(lambda: V.tensor_copy(out, in_), *tok)

        def mm(out, l, r, start, stop, *tok, inc=False):
            fn = lambda: T.matmul(out, l, r, start=start, stop=stop)
            return PE.op(fn, *tok) if inc else PE.quiet(fn, *tok)

        def tp(out, in_, idn, *tok, inc=False):
            fn = lambda: T.transpose(out, in_, idn)
            return PE.op(fn, *tok) if inc else PE.quiet(fn, *tok)

        free = [None] * 8

        class Ring:
            def __init__(self, banks):
                self.banks, self.i = banks, 0

            def take(self):
                b = self.banks[self.i % len(self.banks)]
                self.i += 1
                return b, free[b]

        PR = Ring([0, 1])
        TR = Ring([5, 6])
        SB = [2, 3, 4]
        OB = 7

        order = unit_order()
        loaded, split_done, used = [], [], []

        def load_next():
            i = len(loaded)
            if i >= len(order):
                return
            k = order[i][3]
            waits = split_done[i - NR] if i >= NR else []
            loaded.append(SP.dma(lambda: nc.sync.dma_start(RAW[:, i % NR, 0:k * 128], wst_d[i, :, 0:k * 128]),
                                 s_raw[i % NR], *waits))

        def split_next():
            i = len(split_done)
            if i >= len(order):
                return
            k = order[i][3]
            raw, hi, lo = RAW[:, i % NR, 0:k * 128], WH[:, i % NW, 0:k * 128], WL[:, i % NW, 0:k * 128]
            gone = used[i - NW] if i >= NW else None
            th = acopy(hi, raw, loaded[i], gone)
            tl = tt(lo, raw, f(hi), ALU.subtract, loaded[i], th, gone)
            split_done.append([th, tl])
            load_next()

        def proj(name, j, X, xtok, k0=0, nk=8):
            i = len(used)
            assert order[i] == (name, j, k0, nk), (order[i], name, j, k0, nk)
            if len(split_done) < i + NW:
                split_next()
            b, fr = PR.take()
            XH, XL = X
            PE.wait(fr, split_done[i])
            t = None
            for k in range(nk):
                wh, wl = WH[:, i % NW, k * 128:(k + 1) * 128], WL[:, i % NW, k * 128:(k + 1) * 128]
                mm(PS[:, b, :], wh, XH[:, k, :], k == 0, False, xtok[k])
                mm(PS[:, b, :], wh, XL[:, k, :], False, False)
                t = mm(PS[:, b, :], wl, XH[:, k, :], False, k == nk - 1, inc=(k == nk - 1))
            used.append(t)
            return b, t

        def split_from(bank_or_sb, XH, XL, j, *tok):
            th = acopy(XH[:, j, :], bank_or_sb, *tok)
            tl = tt(XL[:, j, :], bank_or_sb, f(XH[:, j, :]), ALU.subtract, th, *tok)
            return [th, tl]

        s_c = [AC.dma(lambda: nc.scalar.dma_start(C[:, :], con_d), d_con),
               AC.dma(lambda: nc.scalar.dma_start(COL[:, :], col_d), d_con)][-1]
        tx = [SP.dma(lambda j=j: nc.sync.dma_start(XT[:, j:j + 4, :], xT_d[:, j:j + 4, :]), d_x) for j in (0, 4)][-1]
        for _ in range(NR):
            load_next()

        def fence():
            F = [PE.last(), AC.last(), DV.last()]
            AC.wait(*F)
            DV.wait(*F)
            return F

        def rms_rows(src, toks, ar):
            sq = [ar(512), ar(512)]
            acc, rb = ar(512), ar(512)
            last = [None, None]
            ta = None
            for j in range(8):
                t1 = act(sq[j % 2], src[:, j, :], ACT.Square, toks[j], last[j % 2])
                if j == 0:
                    ta = vcopy(acc, sq[0], t1)
                else:
                    ta = tt(acc, acc, sq[j % 2], ALU.add, t1, ta)
                last[j % 2] = ta
            b, fr = TR.take()
            tm = mm(PS[:, b, :], con("mean"), acc, True, True, ta, fr, s_c, inc=True)
            tl = act(rb, PS[:, b, :], ACT.Ln, tm, bias=col("eps"))
            free[b] = tl
            te = act(rb, rb, ACT.Exp, tl, scale=-0.5)
            return rb, te

        def norm_split(gname, toks, ar):
            rb, te = rms_rows(XT, toks, ar)
            tmp = [ar(512), ar(512)]
            last = [None, None]
            out = []
            for j in range(8):
                t = stt(tmp[j % 2], XT[:, j, :], col(gname, j), rb, ALU.mult, ALU.mult, te, last[j % 2])
                t2 = split_from(tmp[j % 2], HH, HL, j, t)
                last[j % 2] = t2
                out.append(t2)
            return out

        AC.wait(s_c)
        DV.wait(s_c)
        ar = Arena(0)
        tab, oh, vecs = ar(24), ar(1920), ar(1920)
        t0 = SP.dma(lambda: nc.sync.dma_start(tab[0:32, :], relb_d), d_vec)
        t0 = SP.dma(lambda: nc.sync.dma_start(oh[0:33, :], oh_d), d_vec)
        t1 = DV.op(lambda: V.memset(tab[32:33, :], NEG))
        tv = []
        for g in range(3):
            for a, n in ((0, 512), (512, 128)):
                b, fr = TR.take()
                tm = mm(PS[0:24, b, 0:n], tab[0:33, :], oh[0:33, g * 640 + a:g * 640 + a + n], True, True,
                        t0, t1, fr, inc=True)
                free[b] = acopy(vecs[0:24, g * 640 + a:g * 640 + a + n], PS[0:24, b, 0:n], tm)
                tv = free[b]
        tvec = SP.dma(lambda: nc.sync.dma_start(scr_d.rearrange("g h i -> h g i"),
                                                vecs[0:24, :].rearrange("p (g i) -> p g i", g=3)), d_vec, tv)
        split_next()
        split_next()
        htok = norm_split("mix_g", [tx] * 8, Arena(4000))
        HX = (HH, HL)
        F = fence()
        SP.wait(*F)
        SP.wait(tvec)
        AC.wait(tvec)
        DV.wait(tvec)

        SLOT = [AR[:, 4608 * i:4608 * (i + 1)] for i in range(2)]
        ar = Arena(4608)
        hq = [ar(1024), ar(1024)]
        hk = [ar(1024), ar(1024)]
        hv = [ar(1028), ar(1028)]
        so = ar(1024)
        xc = ar(516)
        yc = ar(512)
        th_ = ar(512)
        Mb = ar(512)
        Md = ar(128)
        Et = [ar(512), ar(512)]
        WT = ar(1280)
        hm = ar(1024)
        yf = ar(512)
        acol, ecol = ar(16), ar(16)
        stat = ar(64)
        g4 = [ar(512) for _ in range(4)]

        b, t = proj("if", 0, HX, htok)
        r = [x[0:4, :] for x in g4]
        t1 = ts(r[0], PS[0:4, b, :], col("bif", 0, 0, 4), None, ALU.add, ALU.bypass, t)
        t2 = ts(r[1], PS[32:36, b, :], col("bif", 1, 0, 4), None, ALU.add, ALU.bypass, t)
        free[b] = t2
        t3 = stt(r[2], r[1], -1.0, r[1], ALU.mult, ALU.max, t2)
        t4 = act(r[2], r[2], ACT.Exp, t3, scale=-1.0)
        t5 = act(r[2], r[2], ACT.Ln, t4, bias=col("one", 0, 0, 4))
        t6 = stt(r[1], r[1], 0.0, r[2], ALU.min, ALU.subtract, t5, t2)
        t7 = DV.op(lambda: V.memset(r[3], 1.0))
        t8 = DV.op(lambda: V.tensor_tensor_scan(r[2], r[3], r[1], 0.0, ALU.mult, ALU.add), t6, t7)
        t9 = tt(r[0], r[0], r[2], ALU.subtract, t8)
        t10 = DV.op(lambda: V.tensor_tensor_scan(r[1], r[3], r[0], 0.0, ALU.mult, ALU.max), t9)
        t11 = tt(r[2], r[2], r[1], ALU.add, t10)
        t12 = act(r[2], r[2], ACT.Exp, t11, scale=-1.0)
        b, fr = TR.take()
        for s in range(4):
            tp(PS[:, b, 4 * s:4 * s + 4], r[0][:, s * 128:(s + 1) * 128], ident(4), t9, fr)
            tc = tp(PS[:, b, 16 + 4 * s:20 + 4 * s], r[2][:, s * 128:(s + 1) * 128], ident(4), t12, inc=(s == 3))
        tcol = vcopy(acol, PS[:, b, 0:16], tc)
        tcol = vcopy(ecol, PS[:, b, 16:32], tc)
        free[b] = tcol
        tM = t10
        tone = [DV.op(lambda i=i: V.memset(hv[i][:, :].rearrange("p (t e) -> p t e", t=4)[:, :, 256:257], 1.0))
                for i in range(2)][-1]

        mq = {}
        last_att = {-2: None, -1: None}
        conv_free = [None, None]

        def conv(name, h, j):
            b, t = proj(name, 2 * h + j, HX, htok)
            c = (0 if name == "qm" else 8) + 2 * h + j
            dst = (hq if name == "qm" else hk)[h % 2][:, j * 512:(j + 1) * 512]
            t1 = acopy(xc[:, 4:516], PS[:, b, :], t, conv_free[0])
            free[b] = t1
            t2 = DV.op(lambda: V.memset(xc[:, 0:4], 0.0), conv_free[0])
            t3 = ts(yc, xc[:, 1:513], col("conv_w", 4 * c), col("conv_b", c), ALU.mult, ALU.add, t1, t2, conv_free[1])
            for q in range(1, 4):
                t3 = stt(yc, xc[:, 1 + q:513 + q], col("conv_w", 4 * c + q), yc, ALU.mult, ALU.add, t3)
            conv_free[0] = t3
            t4 = act(th_, yc, ACT.Tanh, t3, conv_free[1], scale=0.5)
            t5 = stt(dst, th_, 1.0, yc, ALU.add, ALU.mult, t4, last_att.get(h - 2))
            conv_free[1] = t5
            mq[(h, name, j)] = t5

        vt_free = [None]

        def to_tokens(src, dst3, tsrc, *tok):
            b, fr = TR.take()
            for t_ in range(4):
                x = tp(PS[:, b, t_ * 128:(t_ + 1) * 128], src[:, t_ * 128:(t_ + 1) * 128], ident(), tsrc, fr,
                       inc=(t_ == 3))
            free[b] = vcopy(dst3, PS[:, b, :].rearrange("p (t e) -> p t e", t=4), x, *tok)
            return x, free[b]

        def vproj(h, j):
            b, t = proj("vm", 2 * h + j, HX, htok)
            t1 = acopy(yf, PS[:, b, :], t, vt_free[0])
            free[b] = t1
            x, y = to_tokens(yf, hv[h % 2].rearrange("p (t e) -> p t e", t=4)[:, :, j * 128:(j + 1) * 128], t1,
                             last_att.get(h - 2))
            vt_free[0] = x
            mq[(h, "vm", j)] = y

        def sig_tile(dst, b, t, *tok):
            t1 = act(dst, PS[:, b, :], ACT.Tanh, t, *tok, scale=0.5)
            free[b] = t1
            return ts(dst, dst, 0.5, 0.5, ALU.mult, ALU.add, t1)

        so_free = [None, None]

        def oproj(h, j):
            b, t = proj("om", 2 * h + j, HX, htok)
            mq[(h, "om", j)] = sig_tile(so[:, j * 512:(j + 1) * 512], b, t, so_free[j])

        def head_units(h):
            return ([lambda j=j: conv("qm", h, j) for j in (0, 1)] + [lambda j=j: conv("km", h, j) for j in (0, 1)] +
                    [lambda j=j: vproj(h, j) for j in (0, 1)])

        pair_tok = {}
        pair_last = {}
        pv_free = [None]
        ptmp = xc[:, 0:512]

        def pair_units(hp, tmp, tmpfree):
            sl = SLOT[hp % 2]

            def one(g, kind):
                b, t = proj(("qa", "ka", "va")[kind], 4 * g + hp, HX, htok)
                o = (3 * g + kind) * 512
                gone = pair_last.get(hp - 2)
                if kind < 2:
                    tk = acopy(sl[:, o:o + 512], PS[:, b, :], t, gone, scale=0.125 if kind == 0 else 1.0)
                    free[b] = tk
                else:
                    t1 = acopy(tmp, PS[:, b, :], t, tmpfree[0])
                    free[b] = t1
                    x, tk = to_tokens(tmp, sl[:, o:o + 512].rearrange("p (t e) -> p t e", t=4), t1, gone)
                    tmpfree[0] = x
                pair_tok.setdefault(hp, []).append(tk)
            return [lambda g=g, k=k: one(g, k) for g in range(3) for k in range(3)]

        for u in head_units(0):
            u()
        ya_tok = [None] * 8
        mb_free = [None]
        e_free = [None, None]
        wt_free = [None]
        hm_free = [None]
        yf_free = vt_free
        for h in range(4):
            fill = [lambda j=j: oproj(h, j) for j in (0, 1)]
            fill += head_units(h + 1) if h < 3 else pair_units(0, ptmp, conv_free)

            def filler():
                if fill:
                    fill.pop(0)()

            q, k, v = hq[h % 2], hk[h % 2], hv[h % 2]
            b, fr = TR.take()
            t = mm(PS[:, b, :], con("sel", 128 * h, 128 * h + 128, 0, 4), r[1], True, True, tM, fr, inc=True)
            tmb = acopy(Mb, PS[:, b, :], t, mb_free[0])
            free[b] = tmb
            tw = []
            wo = [0, 512, 896, 1152]
            for s in range(4):
                n = 512 - 128 * s
                b = SB[s % 3]
                for c in (0, 1):
                    t = mm(PS[:, b, 0:n], k[:, c * 512 + s * 128:c * 512 + s * 128 + 128],
                           q[:, c * 512 + s * 128:c * 512 + 512], c == 0, c == 1,
                           mq[(h, "qm", c)], mq[(h, "km", c)], free[b], inc=(c == 1))
                E = Et[s % 2]
                t1 = tt(Md, Mb[:, s * 128:(s + 1) * 128], con("big"), ALU.add, tmb, e_free[0])
                t2 = act(E[:, 0:128], Md, ACT.Exp, t1, tcol, e_free[s % 2], scale=-1.0,
                         bias=acol[:, 4 * s + h:4 * s + h + 1])
                e_free[0] = t2 if s % 2 else e_free[0]
                md_free = t2
                if n > 128:
                    t2 = act(E[:, 128:n], Mb[:, (s + 1) * 128:512], ACT.Exp, tmb, scale=-1.0,
                             bias=acol[:, 4 * s + h:4 * s + h + 1])
                t3 = stt(WT[:, wo[s]:wo[s] + n], PS[:, b, 0:n], 1.0 / 64.0, E[:, 0:n], ALU.mult, ALU.mult, t, t2,
                         wt_free[0])
                e_free = [t3, t3]
                free[b] = t3
                tw.append(t3)
                filler()
                DV.wait(md_free)
            mb_free[0] = md_free if n <= 128 else t2
            mb_free[0] = AC.last()
            hv3 = v.rearrange("p (t e) -> p t e", t=4)
            hmt = []
            for t_ in range(4):
                b, fr = (OB, free[OB])
                for s in range(t_ + 1):
                    o = wo[s] + (t_ - s) * 128
                    t = mm(PS[:, b, 0:257], WT[:, o:o + 128], hv3[:, s, :], s == 0, s == t_, tw[s],
                           mq[(h, "vm", 0)], mq[(h, "vm", 1)], tone, fr, inc=(s == t_))
                d = stat[:, t_:t_ + 1]
                t1 = stt(d, PS[:, b, 256:257], -1.0, ecol[:, 4 * t_ + h:4 * t_ + h + 1], ALU.mult, ALU.max, t, tcol,
                         hm_free[0])
                t1 = tt(d, d, PS[:, b, 256:257], ALU.max, t1)
                t2 = DV.op(lambda d=d: V.reciprocal(d, d), t1)
                hmv = hm[:, t_ * 256:(t_ + 1) * 256]
                t3 = AC.op(lambda hmv=hmv, b=b, d=d: A.activation(hmv, PS[:, b, 0:256], ACT.Copy, scale=d),
                           t2, hm_free[0])
                free[b] = t3
                st6 = stat[:, 8 + 6 * t_:14 + 6 * t_]
                t4 = DV.op(lambda hmv=hmv, st6=st6: V.bn_stats(st6, hmv), t3)
                mv = stat[:, 32 + 2 * t_:34 + 2 * t_]
                t5 = DV.op(lambda mv=mv, st6=st6: V.bn_aggr(mv, st6), t4)
                hmt.append(t5)
                if t_ == 3:
                    wt_free[0] = t
                    last_att[h] = t
                filler()
            var = stat[:, 32:40].rearrange("p (t c) -> p t c", c=2)[:, :, 1:2]
            rs = stat[:, 40:44]
            t1 = act(rs, var, ACT.Ln, hmt[-1], bias=col("eps"))
            t1 = act(rs, rs, ACT.Exp, t1, scale=-0.5)
            for t_ in range(4):
                hmv = hm[:, t_ * 256:(t_ + 1) * 256]
                t2 = ts(hmv, hmv, stat[:, 32 + 2 * t_:33 + 2 * t_], rs[:, t_:t_ + 1], ALU.subtract, ALU.mult, t1,
                        hmt[t_])
            for j in (0, 1):
                b, fr = TR.take()
                for t_ in range(4):
                    t = tp(PS[:, b, t_ * 128:(t_ + 1) * 128], hm[:, t_ * 256 + j * 128:t_ * 256 + j * 128 + 128],
                           ident(), t2, fr, inc=(t_ == 3))
                t3 = stt(yf, PS[:, b, :], col("mnorm", 2 * h + j), so[:, j * 512:(j + 1) * 512], ALU.mult, ALU.mult,
                         t, mq[(h, "om", j)], yf_free[0])
                free[b] = t3
                so_free[j] = t3
                t4 = split_from(yf, AH, AL, 2 * h + j, t3)
                yf_free[0] = t4
                ya_tok[2 * h + j] = t4
                hm_free[0] = t
            while fill:
                filler()
        F = fence()
        SP.wait(*F)

        ar = Arena(9216)
        MG = ar(4096)
        MG3 = MG.rearrange("p (j t) -> p j t", j=8)
        BI = [ar(1280), ar(1280)]
        SS = [ar(1280), ar(1280)]
        PT = ar(1280)
        yb = ar(512)
        st = ar(32)
        AX_ = (AH, AL)

        bias_tok = {}
        bias_free = {-2: None, -1: None}

        def load_bias(h):
            t = BI[h % 2]
            SP.wait(bias_free[h - 2])
            for g in (1, 2):
                src = bass.AP(scr_d.tensor, scr_d.offset + (g * 24 + g * 8 + h) * 640, [[1, 128], [1, 512]])
                SP.dma(lambda g=g, src=src: nc.sync.dma_start(t[:, (g - 1) * 512:g * 512], src), d_bias[h % 2])
            src0 = bass.AP(scr_d.tensor, scr_d.offset + h * 640, [[1, 128], [1, 256]])
            bias_tok[h] = SP.dma(lambda: nc.sync.dma_start(t[:, 1024:1280], src0), d_bias[h % 2])

        load_bias(0)
        load_bias(1)

        def rev(ap, start, n, outer=None):
            dims = [list(ap.ap[0])] + ([list(outer)] if outer else []) + [[-1, n]]
            return bass.AP(ap.tensor, ap.offset + start, dims)

        sgt = SS[0][:, 0:512]
        sg_free = None
        mtok = []
        for j in range(8):
            b, t = proj("ga", j, HX, htok)
            t1 = sig_tile(sgt, b, t, sg_free)
            b, t = proj("pa", j, AX_, ya_tok)
            t2 = tt(MG3[:, j, :], sgt, PS[:, b, :], ALU.mult, t, t1)
            free[b] = t2
            sg_free = t2
            mtok.append(t2)
        ss_free = [sg_free, None]
        pt_free = [None]
        yb_free = [None]
        yb_tok = [None] * 4
        sc_free = [None, None]

        def att_a(it):
            hp, i, n = it
            h = 2 * hp + i
            par = (i * 4 + n) % 2
            sl = SLOT[hp % 2]
            W = 128 * (n + 1)
            k0 = max(0, n - 1)
            W0 = 128 * (n + 1 - k0)
            p = slice(64 * i, 64 * i + 64)
            toks = []
            for g, bnk, ka, w in ((1, SB[0], 0, W), (2, SB[1], 0, W), (0, SB[2], k0 * 128, W0)):
                o = 3 * g * 512
                toks.append(mm(PS[:, bnk, 0:w], sl[p, o + n * 128:o + n * 128 + 128],
                               sl[p, o + 512 + ka:o + 512 + ka + w], True, True, pair_tok[hp], free[bnk], inc=True))
            Sx = SS[par]
            bi = BI[h % 2]
            t1 = tt(Sx[:, 0:2 * W].rearrange("p (g k) -> p g k", g=2), PS[:, SB[0]:SB[0] + 2, 0:W],
                    rev(bi, W - 1, W, (512, 2)), ALU.add, toks[1], bias_tok[h], ss_free[par])
            free[SB[0]] = free[SB[1]] = t1
            t2 = tt(Sx[:, 2 * W:2 * W + W0], PS[:, SB[2], 0:W0], rev(bi, 1024 + W0 - 1, W0), ALU.add, toks[2])
            free[SB[2]] = t2
            if n == 3:
                bias_free[h] = t2
                if h + 2 < 8:
                    load_bias(h + 2)
            nm, l = st[:, par:par + 1], st[:, 2 + par:3 + par]
            N = 2 * W + W0
            t3 = DV.op(lambda: V.tensor_reduce(nm, Sx[:, 0:N], AX, ALU.max, negate=True), t1, t2, sc_free[par])
            t4 = AC.op(lambda: A.activation(Sx[:, 0:N], Sx[:, 0:N], ACT.Exp, bias=nm, accum_out=l), t3)
            return t4, (par, N, l)

        def transposes(Sx, nblk, tS, last_rows=128):
            out = []
            m = 0
            while m < nblk:
                c = min(4, nblk - m)
                b, fr = TR.take()
                for q in range(c):
                    t = tp(PS[:, b, q * 128:(q + 1) * 128], Sx[:, (m + q) * 128:(m + q + 1) * 128], ident(), tS, fr,
                           inc=(q == c - 1))
                e = acopy if (m // 4) % 2 else vcopy
                free[b] = e(PT[:, m * 128:(m + c) * 128], PS[:, b, 0:c * 128], t, pt_free[0])
                out.append(free[b])
                m += c
            return t, out

        def att_b(it, tS, info):
            hp, i, n = it
            par, N, l = info
            Sx = SS[par]
            sl = SLOT[hp % 2]
            nb = N // 128
            tl, ev = transposes(Sx, nb, tS)
            ss_free[par] = tl
            keys = [(1, j) for j in range(n + 1)] + [(2, j) for j in range(n + 1)] + \
                   [(0, j) for j in range(max(0, n - 1), n + 1)]
            for m, (g, j) in enumerate(keys):
                o = (3 * g + 2) * 512 + j * 128 + 64 * i
                t = mm(PS[:, OB, 0:64], PT[:, m * 128:(m + 1) * 128], sl[:, o:o + 64], m == 0, m == nb - 1,
                       ev, free[OB], inc=(m == nb - 1))
            pt_free[0] = t
            t1 = DV.op(lambda: V.reciprocal(l, l), tS)
            o = n * 128 + 64 * i
            t2 = ts(yb[:, o:o + 64], PS[:, OB, 0:64], l, None, ALU.mult, ALU.bypass, t, t1, yb_free[0])
            free[OB] = t2
            sc_free[par] = t2
            return t, t2

        def run_pair(hp, fill):
            items = [(hp, i, n) for i in (0, 1) for n in range(4)]
            nxt = att_a(items[0])
            for m, it in enumerate(items):
                if fill:
                    fill.pop(0)()
                cur = nxt
                if m + 1 < len(items):
                    nxt = att_a(items[m + 1])
                t, t2 = att_b(it, *cur)
            pair_last[hp] = t
            while fill:
                fill.pop(0)()
            b, fr = TR.take()
            for n in range(4):
                t = tp(PS[:, b, n * 128:(n + 1) * 128], yb[:, n * 128:(n + 1) * 128], ident(), t2, fr, inc=(n == 3))
            yb_free[0] = t
            yb_tok[hp] = split_from(PS[:, b, :], AH, AL, hp, t, pa_done)
            free[b] = yb_tok[hp]

        pa_done = used[-1]
        vt = AR[:, ar.at:ar.at]
        vtmp_free = [None]
        vtmp = yf2 = None
        VT = ctx.enter_context(nc.sbuf_tensor("VT", [128, 512], f32))
        for hp in range(3):
            run_pair(hp, pair_units(hp + 1, VT[:, :], vtmp_free))
        gb3 = SLOT[0][:, 0:4096].rearrange("p (j t) -> p j t", j=8)
        gtok = [None] * 8

        def gbu(j):
            b, t = proj("gb", j, HX, htok)
            gtok[j] = sig_tile(gb3[:, j, :], b, t, pair_last[2])
        run_pair(3, [lambda j=j: gbu(j) for j in range(8)])
        mt = []
        for j in range(8):
            b, t = proj("pb", j, AX_, yb_tok, 0, 4)
            t1 = tt(gb3[:, j, :], gb3[:, j, :], PS[:, b, :], ALU.mult, t, gtok[j])
            free[b] = t1
            t2 = tt(MG3[:, j, :], MG3[:, j, :], gb3[:, j, :], ALU.add, t1, mtok[j])
            mt.append(split_from(MG3[:, j, :], HH, HL, j, t2))
        xtok = []
        for j in range(8):
            b, t = proj("out", j, HX, mt)
            t1 = tt(XT[:, j, :], XT[:, j, :], PS[:, b, :], ALU.add, t, tx)
            free[b] = t1
            xtok.append(t1)

        def ffn(sfx, htok, ar, dst3, dtok, accumulate):
            sg = [ar(512), ar(512)]
            pf = [ar(512), ar(512)]
            sgf, pff = [None, None], [None, None]
            down_done = None
            out = list(dtok)
            for a, e in FFN_PARTS:
                tk = []
                for t_ in range(a, e):
                    q = t_ % 2
                    b, t = proj("gate" + sfx, t_, HX, htok)
                    t1 = act(sg[q], PS[:, b, :], ACT.Silu, t, sgf[q])
                    free[b] = t1
                    b, t = proj("up" + sfx, t_, HX, htok)
                    t2 = tt(pf[q], sg[q], PS[:, b, :], ALU.mult, t, t1, pff[q])
                    free[b] = t2
                    sgf[q] = t2
                    t3 = split_from(pf[q], AH, AL, t_ - a, t2, down_done)
                    pff[q] = t3
                    tk.append(t3)
                for j in range(8):
                    b, t = proj("down" + sfx, j, AX_, tk, a, e - a)
                    if accumulate or a > 0:
                        out[j] = tt(dst3[:, j, :], dst3[:, j, :], PS[:, b, :], ALU.add, t, out[j])
                    else:
                        out[j] = vcopy(dst3[:, j, :], PS[:, b, :], t)
                    free[b] = out[j]
                down_done = used[-1]
            return out

        fence()
        ar = Arena(0)
        htok = norm_split("ffn_g", xtok, ar)
        xtok = ffn("", htok, ar, XT, xtok, True)

        fence()
        ar = Arena(0)
        rb, te = rms_rows(XT, xtok, ar)
        xtok = [stt(XT[:, j, :], XT[:, j, :], col("final_g", j), rb, ALU.mult, ALU.mult, te, xtok[j])
                for j in range(8)]
        htok = norm_split("pre2", xtok, ar)
        F = fence()
        SP.wait(*F)

        ar = Arena(0)
        eb = [ar(512) for _ in range(4)]
        enb = [ar(512) for _ in range(4)]
        ekd = [ar(512) for _ in range(4)]
        qe = [ar(512), ar(512)]
        ke = [ar(512), ar(512)]
        kdt = [ar(512), ar(512)]
        gv = [ar(1024), ar(1024)]
        kd, vtm = ar(512), ar(512)
        rr = ar(1024)
        St = [ar(256), ar(256)]
        attn = ar(256)
        on = ar(1024)
        gst = ar(32)
        yf = ar(512)
        th2 = ar(512)
        wa2 = ar(512)
        alr = ar(512)
        dec = ar(32)
        keep = ar(96)
        gts = kd
        t0 = SP.dma(lambda: nc.sync.dma_start(wa2[0:16, :], wa2_d), d_b2)
        b, t = proj("small2", 0, HX, htok)
        t1 = acopy(alr[0:16, :], PS[0:16, b, :], t)
        t2 = act(gts[0:24, :], PS[32:56, b, :], ACT.Tanh, t, scale=0.5)
        free[b] = t2
        b, fr = TR.take()
        for n in range(4):
            t = tp(PS[:, b, 24 * n:24 * n + 24], gts[0:24, n * 128:(n + 1) * 128], ident(24), t2, fr, inc=(n == 3))
        tgate = ts(keep, PS[:, b, 0:96], 0.5, 0.5, ALU.mult, ALU.add, t)
        free[b] = tgate
        kd_free = [t]
        etok = []
        for h in range(4):
            b, fr = TR.take()
            t = mm(PS[:, b, :], wa2[0:16, h * 128:(h + 1) * 128], alr[0:16, :], True, True, t0, t1, fr, inc=True)
            z, e, w = eb[h], enb[h], ekd[h]
            t3 = ts(z, PS[:, b, :], col("balpha", h), None, ALU.add, ALU.bypass, t)
            free[b] = t3
            t4 = stt(e, z, -1.0, z, ALU.mult, ALU.max, t3)
            t5 = act(e, e, ACT.Exp, t4, scale=-1.0)
            t5 = act(e, e, ACT.Ln, t5, bias=col("one"))
            t6 = stt(z, z, 0.0, e, ALU.min, ALU.subtract, t5, t3)
            t7 = DV.op(lambda w=w, z=z: V.tensor_tensor_scan(w, con("reset"), z, 0.0, ALU.mult, ALU.add), t6)
            t8 = act(eb[h], w, ACT.Exp, t7, scale=1.0 / 16)
            t9 = act(enb[h], w, ACT.Exp, t7, scale=-1.0 / 16)
            w3 = w.rearrange("p (n c) -> p n c", c=64)
            vcopy(dec[:, 8 * h:8 * h + 8], eb[h].rearrange("p (n c) -> p n c", c=64)[:, :, 63:64], t8)
            t10 = tt(w3, w3[:, :, 63:64].to_broadcast([128, 8, 64]), w3, ALU.subtract, t8, t9, t7)
            t11 = act(w, w, ACT.Exp, t10, scale=1.0 / 16)
            etok.append([t8, t9, t11])
        t_at0 = DV.op(lambda: V.memset(attn, 0.0))
        gq = {}
        g_last = {-2: None, -1: None}
        vt_free = [None]

        def gla_unit(h, what):
            if what == 0:
                b, t = proj("gq", h, HX, htok)
                gq[(h, 0)] = free[b] = stt(qe[h % 2], PS[:, b, :], float(128 ** -0.5), eb[h], ALU.mult, ALU.mult, t,
                                           etok[h], g_last[h - 2])
            elif what == 1:
                b, t = proj("gk", h, HX, htok)
                gq[(h, 1)] = tt(ke[h % 2], PS[:, b, :], enb[h], ALU.mult, t, etok[h], g_last[h - 2])
                t2 = tt(kd, PS[:, b, :], ekd[h], ALU.mult, kd_free[0])
                free[b] = t2
                x, gq[(h, 2)] = to_tokens(kd, kdt[h % 2].rearrange("p (t e) -> p t e", t=4), t2, g_last[h - 2])
                kd_free[0] = x
            else:
                j = what - 2
                b, t = proj("gv", 2 * h + j, HX, htok)
                t1 = acopy(vtm, PS[:, b, :], t, vt_free[0])
                free[b] = t1
                x, gq[(h, 3 + j)] = to_tokens(vtm, gv[h % 2].rearrange("p (t e) -> p t e", t=4)
                                              [:, :, j * 128:(j + 1) * 128], t1, g_last[h - 2])
                vt_free[0] = x

        r_free = [None, None]
        th_free = [None]

        def gla_r(h, j):
            b, t = proj("gr", 2 * h + j, HX, htok)
            t1 = act(th2, PS[:, b, :], ACT.Tanh, t, th_free[0], scale=0.5)
            t2 = stt(rr[:, j * 512:(j + 1) * 512], th2, 1.0, PS[:, b, :], ALU.add, ALU.mult, t1, r_free[j])
            free[b] = t2
            th_free[0] = t2
            gq[(h, "r", j)] = t2

        NQ = [AR[:, 512 * i:512 * (i + 1)] for i in range(4)]
        NKC, NVC, NKS, NKW, NVS, NVW = [AR[:, 512 * i:512 * (i + 1)] for i in range(4, 10)]
        ntok = {}

        def nsa_unit(name, i):
            gone = gq[(3, 1)], DV_at[0]
            if name == "nq":
                b, t = proj("nq", i, HX, htok)
                ntok[("nq", i)] = free[b] = acopy(NQ[i], PS[:, b, :], t, *gone, scale=0.125)
                return
            b, t = proj(name, 0, HX, htok)
            if name in ("vs", "vw"):
                t1 = acopy(vtm, PS[:, b, :], t, vt_free[0])
                free[b] = t1
                x, ntok[name] = to_tokens(vtm, {"vs": NVS, "vw": NVW}[name].rearrange("p (t e) -> p t e", t=4), t1)
                vt_free[0] = x
            else:
                ntok[name] = free[b] = acopy({"kc": NKC, "vc": NVC, "ks": NKS, "kw": NKW}[name], PS[:, b, :], t,
                                             *gone)

        def gla_units(h):
            return [lambda w=w: gla_unit(h, w) for w in range(4)]

        for u in gla_units(0):
            u()
        att_free = [t_at0]
        st_free = [None, None]
        on_free = [None]
        yg_tok = [None] * 8
        yf_free = [None]
        DV_at = [None]
        glam = con("glam").bitcast(i32)
        for h in range(4):
            fill = [lambda j=j: gla_r(h, j) for j in (0, 1)]
            if h < 3:
                fill += gla_units(h + 1)
            else:
                DV_at[0] = DV.last()
                fill += [lambda i=i: nsa_unit("nq", i) for i in range(4)]
                fill += [lambda n=n: nsa_unit(n, 0) for n in ("kc", "vc", "ks", "kw", "vs", "vw")]
            q_, k_, kt_, v_ = qe[h % 2], ke[h % 2], kdt[h % 2], gv[h % 2]
            v3 = v_.rearrange("p (t e) -> p t e", t=4)
            b = SB[0]
            for n in range(8):
                pb, T_ = 64 * (n % 2), n // 2
                t = mm(PS[pb:pb + 64, b, T_ * 64:T_ * 64 + 64], k_[:, n * 64:n * 64 + 64], q_[:, n * 64:n * 64 + 64],
                       True, True, gq[(h, 0)], gq[(h, 1)], free[b], inc=(n == 7))
            mask3 = bass.AP(glam.tensor, glam.offset, [list(glam.ap[0]), [0, 4], [1, 64]])
            ta = DV.op(lambda b=b: V.copy_predicated(attn.rearrange("p (t c) -> p t c", t=4), mask3,
                                                     PS[:, b, 0:256].rearrange("p (t c) -> p t c", t=4)),
                       t, att_free[0])
            free[b] = ta
            tst = None
            for T_ in range(4):
                up = {}
                for n in (2 * T_, 2 * T_ + 1):
                    if n == 7:
                        continue
                    pb = 64 * (n % 2)
                    ub = SB[1 + n % 2]
                    up[n] = (ub, mm(PS[:, ub, 0:256], kt_[pb:pb + 64, T_ * 128:(T_ + 1) * 128], v3[pb:pb + 64, T_, :],
                                    True, True, gq[(h, 2)], gq[(h, 3)], gq[(h, 4)], free[ub], inc=True))
                for n in (2 * T_, 2 * T_ + 1):
                    pb = 64 * (n % 2)
                    t = mm(PS[pb:pb + 64, OB, 0:256], attn[pb:pb + 64, T_ * 64:T_ * 64 + 64], v3[pb:pb + 64, T_, :],
                           True, n == 0, ta, free[OB], inc=True)
                    if n > 0:
                        t = mm(PS[pb:pb + 64, OB, 0:256], q_[:, n * 64:n * 64 + 64], St[(n - 1) % 2], False, True,
                               tst, inc=True)
                        st_free[(n - 1) % 2] = t
                    if n < 7:
                        ub, tu = up[n]
                        if n == 0:
                            tst = vcopy(St[0], PS[:, ub, 0:256], tu, st_free[0])
                        else:
                            tst = stt(St[n % 2], St[(n - 1) % 2], dec[:, 8 * h + n:8 * h + n + 1],
                                      PS[:, ub, 0:256], ALU.mult, ALU.add, tu, tst, st_free[n % 2])
                        free[ub] = tst
                ss, rs = gst[:, T_:T_ + 1], gst[:, 8 + T_:9 + T_]
                onv = on[:, T_ * 256:(T_ + 1) * 256]
                t1 = AC.op(lambda onv=onv, ss=ss: A.activation(onv, PS[:, OB, 0:256], ACT.Square, accum_out=ss),
                           t, on_free[0])
                t2 = act(rs, ss, ACT.Ln, t1, scale=1.0 / 256, bias=col("eps"))
                t2 = act(rs, rs, ACT.Exp, t2, scale=-0.5)
                t3 = ts(onv, PS[:, OB, 0:256], rs, 0.5, ALU.mult, ALU.mult, t2)
                free[OB] = t3
                if fill:
                    fill.pop(0)()
                if fill:
                    fill.pop(0)()
            g_last[h] = t
            att_free[0] = t
            for j in (0, 1):
                b, fr = TR.take()
                for t_ in range(4):
                    t = tp(PS[:, b, t_ * 128:(t_ + 1) * 128], on[:, t_ * 256 + j * 128:t_ * 256 + j * 128 + 128],
                           ident(), t3, fr, inc=(t_ == 3))
                t4 = stt(yf, PS[:, b, :], col("glag", j), rr[:, j * 512:(j + 1) * 512], ALU.mult, ALU.mult, t,
                         gq[(h, "r", j)], yf_free[0])
                free[b] = t4
                r_free[j] = t4
                t5 = split_from(yf, AH, AL, 2 * h + j, t4)
                yf_free[0] = t5
                yg_tok[2 * h + j] = t5
                on_free[0] = t
            while fill:
                fill.pop(0)()
        keep2 = th2[:, 0:96]
        F = fence()
        GT = ctx.enter_context(nc.sbuf_tensor("GT", [128, 96], f32))
        tg2 = vcopy(GT[:, :], keep, tgate)
        F = fence()
        SP.wait(*F)
        ar = Arena(5120)
        MGN = ar(8192)
        MG3 = MGN[:, 0:4096].rearrange("p (j t) -> p j t", j=8)
        SN3 = MGN[:, 4096:8192].rearrange("p (j t) -> p j t", j=8)
        sz = ar(0).offset
        SS = [ar(1056), ar(1056)]
        PT = ar(1280)
        yb = ar(2048)
        yb3 = yb.rearrange("p (n c) -> p n c", n=4)
        w2s = ar(256)
        kcT = ar(32)
        vcs = ar(128)
        hid = ar(64)
        th3 = ar(64)
        st = ar(32)
        t0 = SP.dma(lambda: nc.sync.dma_start(MGN[:, 0:4096], w1k_d), d_b2)
        t0 = SP.dma(lambda: nc.sync.dma_start(MGN[:, 4096:8192], w1v_d), d_b2)
        t0 = SP.dma(lambda: nc.sync.dma_start(w2s, w2_d), d_b2)
        blk = [SS[0][:, 0:992], SS[1][:, 0:992]]
        for c, (src, pe_, nm_) in enumerate(((NKC, "pek", "kc"), (NVC, "pev", "vc"))):
            win = bass.AP(src.tensor, src.offset, [list(src.ap[0]), [1, 32], [16, 31]])
            pex = COL[:, COLS[pe_]:COLS[pe_] + 32]
            peb = bass.AP(pex.tensor, pex.offset, [list(pex.ap[0]), [1, 32], [0, 31]])
            t1 = tt(blk[c].rearrange("p (l n) -> p l n", l=32), win, peb, ALU.add, ntok[nm_])
            b, fr = TR.take()
            for l in range(32):
                t = mm(PS[:, b, 0:31], MGN[:, 4096 * c + l * 128:4096 * c + (l + 1) * 128],
                       blk[c][:, 31 * l:31 * l + 31], l == 0, l == 31, t0, t1, fr, inc=(l == 31))
            hv_ = hid[:, 32 * c:32 * c + 31]
            t2 = act(th3[:, 32 * c:32 * c + 31], PS[:, b, 0:31], ACT.Tanh, t, scale=0.5)
            t3 = ts(th3[:, 32 * c:32 * c + 31], th3[:, 32 * c:32 * c + 31], 0.5, 0.5, ALU.mult, ALU.add, t2)
            t3 = tt(hv_, th3[:, 32 * c:32 * c + 31], PS[:, b, 0:31], ALU.mult, t3)
            free[b] = t3
            comp_done = t
            b, fr = TR.take()
            if c == 0:
                t = mm(PS[:, b, 0:31], w2s[:, 0:128], hv_, True, True, t3, fr, inc=True)
                tkc = free[b] = vcopy(kcT[:, 0:31], PS[:, b, 0:31], t)
            else:
                t = mm(PS[0:31, b, 0:128], hv_, w2s[:, 128:256], True, True, t3, fr, inc=True)
                tvc = free[b] = vcopy(vcs[0:31, :], PS[0:31, b, 0:128], t)
        ss_free = [comp_done, comp_done]
        pt_free = [None]
        sc_free = [None, None]
        mtok, stok = [None] * 8, [None] * 8
        sgt_free = [None]
        SGT = VT[:, :]

        def merge_units(j):
            def a():
                b, t = proj("mg", j, HX, htok)
                sgt_free[0] = sig_tile(SGT, b, t, sgt_free[0])

            def c():
                b, t = proj("pg", j, AX_, yg_tok)
                mtok[j] = tt(MG3[:, j, :], SGT, PS[:, b, :], ALU.mult, t, sgt_free[0], comp_done)
                free[b] = mtok[j]
                sgt_free[0] = mtok[j]

            def d():
                b, t = proj("mn", j, HX, htok)
                stok[j] = sig_tile(SN3[:, j, :], b, t, comp_done)
            return [a, c, d]

        fill = []
        for j in range(8):
            fill += merge_units(j)

        def nsa_a(it):
            h, n = it
            par = (h * 4 + n) % 2
            i = h % 4
            p = slice(64 * (h // 4), 64 * (h // 4) + 64)
            W = 128 * (n + 1)
            slope = float(2.0 ** (-8.0 * (h + 1) / 8))
            qv = NQ[i][p, n * 128:(n + 1) * 128]
            ta_ = mm(PS[:, SB[0], 0:W], qv, NKS[p, 0:W], True, True, ntok[("nq", i)], ntok["ks"], free[SB[0]], inc=True)
            tb_ = mm(PS[:, SB[1], 0:W], qv, NKW[p, 0:W], True, True, ntok["kw"], free[SB[1]], inc=True)
            tc_ = mm(PS[:, SB[2], 0:31], qv, kcT[p, 0:31], True, True, tkc, free[SB[2]], inc=True)
            Sx = SS[par]
            ba = con("ba", 128 * (3 - n), 512)
            ba2 = bass.AP(ba.tensor, ba.offset, [list(ba.ap[0]), [0, 2], [1, W]])
            t1 = stt(Sx[:, 0:2 * W].rearrange("p (g k) -> p g k", g=2), ba2, slope, PS[:, SB[0]:SB[0] + 2, 0:W],
                     ALU.mult, ALU.add, tb_, ss_free[par])
            free[SB[0]] = free[SB[1]] = t1
            Sc = Sx[:, 1024:1055]
            t2 = stt(Sc, con("bc", 31 * n, 31 * n + 31), slope, PS[:, SB[2], 0:31], ALU.mult, ALU.add, tc_)
            free[SB[2]] = t2
            nm, l = st[:, 3 * par:3 * par + 3], st[:, 8 + 3 * par:11 + 3 * par]
            t3 = DV.op(lambda: V.tensor_reduce(nm[:, 1:3], Sx[:, 0:2 * W].rearrange("p (g k) -> p g k", g=2), AX,
                                               ALU.max, negate=True), t1, sc_free[par])
            t3 = DV.op(lambda: V.tensor_reduce(nm[:, 0:1], Sc, AX, ALU.max, negate=True), t2)
            AC.op(lambda: A.activation(Sc, Sc, ACT.Exp, bias=nm[:, 0:1], accum_out=l[:, 0:1]), t3)
            AC.op(lambda: A.activation(Sx[:, 0:W], Sx[:, 0:W], ACT.Exp, bias=nm[:, 1:2], accum_out=l[:, 1:2]))
            t4 = AC.op(lambda: A.activation(Sx[:, W:2 * W], Sx[:, W:2 * W], ACT.Exp, bias=nm[:, 2:3],
                                            accum_out=l[:, 2:3]))
            return t4, (par, l)

        def nsa_b(it, tS, info):
            h, n = it
            par, l = info
            Sx = SS[par]
            W = 128 * (n + 1)
            g_ = h // 4
            Sc = Sx[:, 1024:1055]
            t5 = tt(Sc, Sc, con("m01", 31 * n, 31 * n + 31), ALU.mult, tS)
            t6 = DV.op(lambda: V.reciprocal(l, l), tS)
            t6 = tt(l, l, GT[:, 24 * n + 3 * h:24 * n + 3 * h + 3], ALU.mult, t6, tg2)
            tl, ev = transposes2(Sx, 2 * (n + 1), tS, pt_free)
            b, fr = TR.take()
            tl = tp(PS[0:31, b, 0:128], Sc, ident(), t5, fr, inc=True)
            e2 = free[b] = acopy(PT[0:31, 1024:1152], PS[0:31, b, 0:128], tl, pt_free[0])
            ss_free[par] = tl
            for br, (vv, c0) in enumerate(((NVS, 64), (NVW, 128))):
                for j in range(n + 1):
                    m = br * (n + 1) + j
                    mm(PS[:, OB, c0:c0 + 64], PT[:, m * 128:(m + 1) * 128],
                       vv[:, j * 128 + 64 * g_:j * 128 + 64 * g_ + 64], j == 0, j == n, ev, ntok["vs"], ntok["vw"],
                       free[OB])
            t = mm(PS[:, OB, 0:64], PT[0:31, 1024:1152], vcs[0:31, 64 * g_:64 * g_ + 64], True, True, e2, tvc,
                   inc=True)
            pt_free[0] = t
            y = yb3[:, n, 64 * h:64 * h + 64]
            t7 = ts(y, PS[:, OB, 0:64], l[:, 0:1], None, ALU.mult, ALU.bypass, t, t6)
            t7 = stt(y, PS[:, OB, 64:128], l[:, 1:2], y, ALU.mult, ALU.add, t7)
            t7 = stt(y, PS[:, OB, 128:192], l[:, 2:3], y, ALU.mult, ALU.add, t7)
            free[OB] = t7
            sc_free[par] = t7
            return t7

        def transposes2(Sx, nblk, tS, ptf):
            out = []
            m = 0
            while m < nblk:
                c = min(4, nblk - m)
                b, fr = TR.take()
                for q in range(c):
                    t = tp(PS[:, b, q * 128:(q + 1) * 128], Sx[:, (m + q) * 128:(m + q + 1) * 128], ident(), tS, fr,
                           inc=(q == c - 1))
                e = acopy if (m // 4) % 2 == 0 else vcopy
                free[b] = e(PT[:, m * 128:(m + c) * 128], PS[:, b, 0:c * 128], t, ptf[0])
                out.append(free[b])
                m += c
            return t, out

        items = [(h, n) for h in range(8) for n in range(4)]
        nxt = nsa_a(items[0])
        for m, it in enumerate(items):
            if fill and m % 4 != 0:
                fill.pop(0)()
            cur = nxt
            if m + 1 < len(items):
                nxt = nsa_a(items[m + 1])
            t7 = nsa_b(it, *cur)
        while fill:
            fill.pop(0)()
        pg_done = used[-1]
        yn_tok = []
        for j in range(4):
            b, fr = TR.take()
            for n in range(4):
                t = tp(PS[:, b, n * 128:(n + 1) * 128], yb3[:, n, j * 128:(j + 1) * 128], ident(), t7, fr,
                       inc=(n == 3))
            x = split_from(PS[:, b, :], AH, AL, j, t, pg_done)
            free[b] = x
            yn_tok.append(x)
        mt = []
        for j in range(8):
            b, t = proj("pn", j, AX_, yn_tok, 0, 4)
            t1 = tt(SN3[:, j, :], SN3[:, j, :], PS[:, b, :], ALU.mult, t, stok[j])
            free[b] = t1
            t2 = tt(MG3[:, j, :], MG3[:, j, :], SN3[:, j, :], ALU.add, t1, mtok[j])
            mt.append(split_from(MG3[:, j, :], HH, HL, j, t2))
        F = fence()

        def post(name, src3, toks, ar):
            rb, te = rms_rows(src3, toks, ar)
            tmp = [ar(512), ar(512)]
            out = []
            for j in range(8):
                t = stt(tmp[j % 2], src3[:, j, :], col(name, j), rb, ALU.mult, ALU.mult, te)
                out.append(tt(XT[:, j, :], XT[:, j, :], tmp[j % 2], ALU.add, t))
            return out

        ar = Arena(0)
        OT = ar(4096).rearrange("p (j t) -> p j t", j=8)
        otok = []
        for j in range(8):
            b, t = proj("out2", j, HX, mt)
            free[b] = vcopy(OT[:, j, :], PS[:, b, :], t)
            otok.append(free[b])
        xtok = post("post2", OT, otok, ar)
        fence()
        ar = Arena(0)
        htok = norm_split("fpre2", xtok, ar)
        OT = ar(4096).rearrange("p (j t) -> p j t", j=8)
        otok = ffn("2", htok, ar, OT, [None] * 8, False)
        xtok = post("fpost2", OT, otok, ar)
        for j in range(8):
            to = SP.dma(lambda j=j: nc.sync.dma_start(out_d[:, j, :], XT[:, j, :]), d_out, xtok[j])
        SP.wait(to)

        assert len(used) == len(order)
        block = ctx.enter_context(nc.Block())

        @block.sync
        def _(eng):
            SP.replay(eng)

        @block.scalar
        def _(eng):
            AC.replay(eng)

        @block.vector
        def _(eng):
            DV.replay(eng)

        @block.tensor
        def _(eng):
            PE.replay(eng)


def constant_tables():
    con = np.zeros((128, NCON), np.float32)
    p = np.arange(128)
    con[:, CON["ident"]:CON["ident"] + 128] = np.eye(128)
    con[:, CON["big"]:CON["big"] + 128] = np.where(p[None, :] < p[:, None], 1e30, 0.0)
    con[:, CON["mean"]:CON["mean"] + 128] = 1.0 / 1024
    for h in range(4):
        con[h, CON["sel"] + 128 * h:CON["sel"] + 128 * h + 128] = 1.0
    dist = 384 + p[:, None] - np.arange(512)[None, :]
    con[:, CON["ba"]:CON["ba"] + 512] = np.where(dist >= 0, -dist, NEG)
    end = 16 * np.arange(31) + 31
    for n in range(4):
        t = 128 * n + p[:, None]
        ok = end[None, :] <= t
        con[:, CON["bc"] + 31 * n:CON["bc"] + 31 * n + 31] = np.where(ok, -(t - end[None, :]), NEG)
        con[:, CON["m01"] + 31 * n:CON["m01"] + 31 * n + 31] = ok
    con[:, CON["glam"]:CON["glam"] + 64] = (p[:, None] % 64) <= np.arange(64)[None, :]
    con[:, CON["reset"]:CON["reset"] + 512] = (np.arange(512) % 64 != 0)
    oh = np.zeros((33, 3, 640), np.float32)
    for g, (win, dil) in enumerate(((128, 1), (512, 4), (2048, 16))):
        for i in range(640):
            d = i - 127
            if d < 0 or d > win or d % dil:
                oh[32, g, i] = 1.0
                continue
            if d < 16:
                bkt = d
            else:
                bkt = min(31, 16 + int(np.float32(np.log(np.float32(d) / np.float32(16)) / np.float32(np.log(128.0))
                                                  * np.float32(16))))
            oh[bkt, g, i] = 1.0
    return con, oh.reshape(33, 1920)


def pack_units(inputs):
    w_in, w_in2 = inputs["w_in"][0], inputs["w_in_2"][0]
    pts = np.cumsum([0, 1024, 1024, 1024, 8, 1024, 1536, 1536, 1536, 1024, 1024])
    names = ["qm", "km", "vm", "if_", "om", "qa", "ka", "va", "ga", "gb"]
    m = {n: w_in[:, pts[i]:pts[i + 1]] for i, n in enumerate(names)}
    z = np.zeros((1024, 128), np.float32)
    z[:, 0:4] = m["if_"][:, 0:4]
    z[:, 32:36] = m["if_"][:, 4:8]
    m["if"] = z
    pts = np.cumsum([0, 512, 512, 1024, 1024, 16, 512, 128, 128, 128, 128, 128, 128, 24, 1024, 1024])
    names = ["gq", "gk", "gv", "gr", "al", "nq_", "kc", "vc", "ks", "vs", "kw", "vw", "gt", "mg", "mn"]
    m.update({n: w_in2[:, pts[i]:pts[i + 1]] for i, n in enumerate(names)})
    z = np.zeros((1024, 128), np.float32)
    z[:, 0:16] = m["al"]
    z[:, 32:56] = m["gt"]
    m["small2"] = z
    q = m["nq_"].reshape(1024, 2, 4, 64)
    m["nq"] = np.ascontiguousarray(q.transpose(0, 2, 1, 3)).reshape(1024, 512)
    m.update({"pa": inputs["w_proj_a"][0], "pb": inputs["w_proj_b"][0], "out": inputs["w_out"][0],
              "gate": inputs["w_gate"][0], "up": inputs["w_up"][0], "down": inputs["w_down"][0],
              "pg": inputs["w_proj_gla_2"][0], "pn": inputs["w_proj_nsa_2"][0], "out2": inputs["w_out_2"][0],
              "gate2": inputs["w_ffn_gate_2"][0], "up2": inputs["w_ffn_up_2"][0], "down2": inputs["w_ffn_down_2"][0]})
    order = unit_order()
    w = np.zeros((len(order), 128, 1024), np.float32)
    for i, (name, j, k0, nk) in enumerate(order):
        blk = m[name][k0 * 128:(k0 + nk) * 128, j * 128:(j + 1) * 128]
        w[i, :, 0:nk * 128] = blk.reshape(nk, 128, 128).transpose(1, 0, 2).reshape(128, nk * 128)
    return w


def pack_cols(inputs):
    c = np.zeros((128, NCOL), np.float32)

    def put(name, vec):
        v = vec.reshape(-1, 128).T
        c[:, COLS[name]:COLS[name] + v.shape[1]] = v

    put("mix_g", inputs["norm_mix_g"][0])
    cw = inputs["conv_w"][0]
    c[:, COLS["conv_w"]:COLS["conv_w"] + 64] = cw.reshape(4, 16, 128).transpose(2, 1, 0).reshape(128, 64)
    put("conv_b", inputs["conv_b"][0])
    put("mnorm", inputs["mlstm_norm_g"][0])
    put("ffn_g", inputs["norm_ffn_g"][0])
    put("final_g", inputs["norm_final_g"])
    put("pre2", inputs["norm_mix_pre_2"][0])
    put("post2", inputs["norm_mix_post_2"][0])
    put("fpre2", inputs["norm_ffn_pre_2"][0])
    put("fpost2", inputs["norm_ffn_post_2"][0])
    put("balpha", inputs["gla_b_alpha_2"][0])
    put("glag", inputs["gla_norm_g_2"][0])
    b = inputs["b_gate_if"][0]
    c[0:4, COLS["bif"]] = b[0:4]
    c[0:4, COLS["bif"] + 1] = b[4:8]
    c[:, COLS["eps"]] = EPS
    c[:, COLS["one"]] = 1.0
    for n, k in (("pek", "nsa_cmp_pe_k_2"), ("pev", "nsa_cmp_pe_v_2")):
        pe = inputs[k][0].T
        c[0:64, COLS[n]:COLS[n] + 32] = pe
        c[64:128, COLS[n]:COLS[n] + 32] = pe
    return c


def kernel(**inputs):
    import concourse.bacc as bacc
    from concourse.bass_utils import run_bass_kernel_spmd

    inputs = {k: np.asarray(v) for k, v in inputs.items()}
    con, oh = constant_tables()
    x = inputs["x"][0]
    arrays = {
        "xT": np.ascontiguousarray(x.T.reshape(8, 128, 512).transpose(1, 0, 2)),
        "wst": pack_units(inputs),
        "con": con,
        "col": pack_cols(inputs),
        "relb": np.ascontiguousarray(inputs["rel_bias"]),
        "oh": oh,
        "wa2": np.ascontiguousarray(inputs["gla_w_alpha2_2"][0]),
    }
    for n, k in (("w1k", "nsa_cmp_w1_k_2"), ("w1v", "nsa_cmp_w1_v_2")):
        w = inputs[k][0].reshape(32, 64, 64).transpose(1, 0, 2)
        bd = np.zeros((128, 32, 128), np.float32)
        bd[0:64, :, 0:64] = w
        bd[64:128, :, 64:128] = w
        arrays[n] = bd.reshape(128, 4096)
    w2 = np.zeros((128, 256), np.float32)
    for i, k in enumerate(("nsa_cmp_w2_k_2", "nsa_cmp_w2_v_2")):
        w2[0:64, 128 * i:128 * i + 64] = inputs[k][0]
        w2[64:128, 128 * i + 64:128 * i + 128] = inputs[k][0]
    arrays["w2"] = w2

    nc = bacc.Bacc("TRN2", target_bir_lowering=False, num_devices=1)
    f32 = mybir.dt.float32
    aps = [nc.dram_tensor(n, arrays[n].shape, f32, kind="ExternalInput").ap()
           for n in ("xT", "wst", "con", "col", "relb", "oh", "wa2", "w1k", "w1v", "w2")]
    out = nc.dram_tensor("out", (128, 8, 512), f32, kind="ExternalOutput").ap()
    scr = nc.dram_tensor("scr", (3, 24, 640), f32, kind="Internal").ap()
    build(nc, *aps, out, scr)
    r = run_bass_kernel_spmd(nc, [arrays], core_ids=[0])
    y = r.results[0]["out"]
    return np.ascontiguousarray(y.transpose(1, 0, 2).reshape(1024, 512).T)[None]
```

```python
import numpy as np
import concourse.bass as bass
from concourse import mybir
from contextlib import ExitStack

D = 1024
S = 512
DFF = 2816
NR = 3
NW = 3
FFN_PARTS = [(0, 8), (8, 16), (16, 22)]
EPS = 1e-6
NEG = -1e30

COLS = {}
_at = 0
for _name, _n in [("mix_g", 8), ("conv_w", 64), ("conv_b", 16), ("mnorm", 8), ("ffn_g", 8), ("final_g", 8),
                  ("pre2", 8), ("post2", 8), ("fpre2", 8), ("fpost2", 8), ("balpha", 4), ("glag", 2),
                  ("bif", 2), ("eps", 1), ("one", 1), ("nhalf", 4), ("pek", 32), ("pev", 32)]:
    COLS[_name] = _at
    _at += _n
NCOL = _at

CON = {}
_at = 0
for _name, _n in [("ident", 128), ("big", 128), ("mean", 128), ("sel", 512), ("ba", 512), ("bc", 124),
                  ("m01", 124), ("glam", 64)]:
    CON[_name] = _at
    _at += _n
NCON = _at


def unit_order():
    u = []

    def add(name, j, k0=0, k=8):
        u.append((name, j, k0, k))

    def ffn(sfx):
        for a, b in FFN_PARTS:
            for t in range(a, b):
                add("gate" + sfx, t)
                add("up" + sfx, t)
            for j in range(8):
                add("down" + sfx, j, a, b - a)

    def head(h):
        for n in ("qm", "km", "vm"):
            for j in (0, 1):
                add(n, 2 * h + j)

    def pair(hp):
        for g in range(3):
            for n in ("qa", "ka", "va"):
                add(n, 4 * g + hp)

    head(0)
    u.insert(2, ("if", 0, 0, 8))
    for h in range(4):
        add("om", 2 * h)
        add("om", 2 * h + 1)
        if h < 3:
            head(h + 1)
    pair(0)
    for j in range(8):
        add("ga", j)
        add("pa", j)
    for hp in range(3):
        pair(hp + 1)
    for j in range(8):
        add("gb", j)
    for j in range(8):
        add("pb", j, 0, 4)
    for j in range(8):
        add("out", j)
    ffn("")

    add("small2", 0)
    def ghead(h):
        for n, j in (("gv", 2 * h), ("gv", 2 * h + 1), ("gq", h), ("gk", h)):
            add(n, j)

    ghead(0)
    for h in range(4):
        add("gr", 2 * h)
        add("gr", 2 * h + 1)
        if h < 3:
            ghead(h + 1)
    for n in ("kc", "vc", "w1k", "nq", "w1v", "ks", "kw", "vs", "vw"):
        for i in range(4 if n in ("nq", "w1k", "w1v") else 1):
            add(n, i)
    for j in range(8):
        add("mg", j)
        add("pg", j)
        add("mn", j)
    for j in range(8):
        add("pn", j, 0, 4)
    for j in range(8):
        add("out2", j)
    ffn("2")
    return u


BUSY_DVE = ("qm", "km", "vm", "om", "qa", "ka", "va", "gb", "gv", "gr", "gq", "gk", "nq", "kc", "vc", "ks", "vs",
            "kw", "vw", "mg", "pg", "mn")


class Queue:

    def __init__(self, sem):
        self.sem, self.n, self.items, self.seen = sem, 0, [], {}

    def wait(self, *tokens):
        for t in tokens:
            if t is None:
                continue
            if isinstance(t, list):
                self.wait(*t)
                continue
            sem, v = t
            if self.seen.get(id(sem), 0) < v:
                self.seen[id(sem)] = v
                self.items.append((None, sem, v))

    def op(self, fn, *tokens):
        self.wait(*tokens)
        self.n += 1
        self.items.append((fn, self.sem, 1))
        return (self.sem, self.n)

    def quiet(self, fn, *tokens):
        self.wait(*tokens)
        self.items.append((fn, None, 0))

    def dma(self, fn, chan, *tokens):
        self.wait(*tokens)
        chan[1] += 16
        self.items.append((fn, chan[0], 16))
        return (chan[0], chan[1])

    def last(self):
        return (self.sem, self.n) if self.n else None

    def replay(self, eng):
        for fn, sem, v in self.items:
            if fn is None:
                eng.wait_ge(sem, v)
            elif sem is None:
                fn()
            else:
                fn().then_inc(sem, v)


def build(nc, xT_d, wst_d, con_d, col_d, relb_d, oh_d, wa2_d, w2_d, out_d, scr_d):
    f32 = mybir.dt.float32
    r32 = mybir.dt.float32r
    i32 = mybir.dt.int32
    ALU = mybir.AluOpType
    ACT = mybir.ActivationFunctionType
    AX = mybir.AxisListType.X
    ctx = ExitStack()
    with ctx:
        def sb(name, shape, dt=f32):
            return ctx.enter_context(nc.sbuf_tensor(name, shape, dt))

        def sem(name):
            return ctx.enter_context(nc.semaphore(name))

        ARN = 20288
        XT = sb("XT", [128, 8, 512])
        HH = sb("HH", [128, 8, 512], r32)
        HL = sb("HL", [128, 8, 512], r32)
        AH = sb("AH", [128, 8, 512], r32)
        AL = sb("AL", [128, 8, 512], r32)
        RAW = sb("RAW", [128, NR, 1024])
        WH = sb("WH", [128, NW, 1024], r32)
        WL = sb("WL", [128, NW, 1024], r32)
        C = sb("C", [128, NCON])
        COL = sb("COL", [128, NCOL])
        AR = sb("AR", [128, ARN])
        PS = ctx.enter_context(nc.psum_tensor("PS", [128, 8, 512], f32))

        PE = Queue(sem("s_pe"))
        AC = Queue(sem("s_act"))
        DV = Queue(sem("s_dve"))
        GP = Queue(sem("s_pool"))
        SP = Queue(sem("s_sp"))
        s_raw = [[sem(f"s_raw{i}"), 0] for i in range(NR)]
        d_con = [sem("d_con"), 0]
        d_x = [[sem(f"d_x{i}"), 0] for i in range(8)]
        d_col = [sem("d_col"), 0]
        d_vec = [sem("d_vec"), 0]
        d_bias = [[sem(f"d_bias{i}"), 0] for i in range(2)]
        d_b2 = [sem("d_b2"), 0]
        d_w2 = [sem("d_w2"), 0]
        d_out = [[sem(f"d_out{i}"), 0] for i in range(2)]
        V, A, T, G = nc.vector, nc.scalar, nc.tensor, nc.gpsimd
        RB = sb("RB", [128, 512])[:, :]
        VT = sb("VT", [128, 512])
        GT = sb("GT", [128, 96])
        HX, AX_ = (HH, HL), (AH, AL)

        def f(ap):
            return ap.bitcast(f32)

        def col(name, j=0, p0=0, p1=128, n=1):
            return COL[p0:p1, COLS[name] + j:COLS[name] + j + n]

        def con(name, a=0, b=None, p0=0, p1=128):
            n = {"ident": 128, "big": 128, "mean": 128, "sel": 512, "ba": 512, "bc": 124, "m01": 124, "glam": 64}[name]
            return C[p0:p1, CON[name] + a:CON[name] + (n if b is None else b)]

        class Arena:
            def __init__(self, at):
                self.at = at

            def __call__(self, n):
                o = self.at
                self.at += n
                assert self.at <= ARN, self.at
                return AR[:, o:o + n]

        def ident(n=128):
            return con("ident", 0, n, 0, n)

        def act(out, in_, func, *tok, **kw):
            return AC.op(lambda: A.activation(out, in_, func, **kw), *tok)

        def acopy(out, in_, *tok, scale=1.0):
            return AC.op(lambda: A.activation(out, in_, ACT.Copy, scale=scale), *tok)

        def tt(out, a, b, op, *tok):
            return DV.op(lambda: V.tensor_tensor(out, a, b, op), *tok)

        def ts(out, a, s1, s2, op0, op1, *tok):
            return DV.op(lambda: V.tensor_scalar(out, a, s1, s2, op0, op1), *tok)

        def stt(out, a, s, b, op0, op1, *tok):
            return DV.op(lambda: V.scalar_tensor_tensor(out=out, in0=a, scalar=s, in1=b, op0=op0, op1=op1), *tok)

        def ptt(out, a, b, op, *tok):
            return GP.op(lambda: G.tensor_tensor(out, a, b, op), *tok)

        def vcopy(out, in_, *tok):
            return DV.op(lambda: V.tensor_copy(out, in_), *tok)

        def mm(out, l, r, start, stop, *tok, inc=False):
            fn = lambda: T.matmul(out, l, r, start=start, stop=stop)
            return PE.op(fn, *tok) if inc else PE.quiet(fn, *tok)

        def tp(out, in_, idn, *tok, inc=False):
            fn = lambda: T.transpose(out, in_, idn)
            return PE.op(fn, *tok) if inc else PE.quiet(fn, *tok)

        free = [None] * 8

        class Ring:
            def __init__(self, banks):
                self.banks, self.i = banks, 0

            def take(self):
                b = self.banks[self.i % len(self.banks)]
                self.i += 1
                return b, free[b]

        PR = Ring([0, 1])
        TR = Ring([5, 6])
        SB = [2, 3, 4]
        OB = 7

        order = unit_order()
        loaded, split_done, used = [], [], {}
        started = [0]

        def raw_unit(i):
            return order[i][0] in ("w1k", "w1v")

        def load_more(most=1000):
            while len(loaded) < len(order) and most > 0:
                most -= 1
                i = len(loaded)
                if i < NR:
                    waits = []
                elif raw_unit(i - NR):
                    if i - NR not in used:
                        return
                    waits = [used[i - NR]]
                elif i - NR < len(split_done):
                    waits = split_done[i - NR]
                else:
                    return
                k = order[i][3]
                loaded.append(SP.dma(lambda i=i, k=k: nc.sync.dma_start(RAW[:, i % NR, 0:k * 128],
                                                                        wst_d[i, :, 0:k * 128]),
                                     s_raw[i % NR], *waits))

        def split_next():
            i = len(split_done)
            if i >= len(order):
                return
            if raw_unit(i):
                split_done.append([loaded[i]])
                return
            k = order[i][3]
            raw, hi, lo = RAW[:, i % NR, 0:k * 128], WH[:, i % NW, 0:k * 128], WL[:, i % NW, 0:k * 128]
            gone = used.get(i - NW)
            th = acopy(hi, raw, loaded[i], gone)
            low = ptt if i % 2 and order[i][0] in BUSY_DVE else tt
            tl = low(lo, raw, f(hi), ALU.subtract, loaded[i], th, gone)
            split_done.append([th, tl])
            load_more()

        def open_unit(key):
            i = started[0]
            started[0] += 1
            assert order[i] == key, (order[i], key)
            while len(split_done) < min(i + NW, len(order)) and len(split_done) - NW < len(used):
                split_next()
            return i

        class Filler:

            def __init__(self, gens, points):
                self.gens, self.total, self.points = list(gens), 4 * len(gens), points
                self.acc = self.done = 0

            def step(self):
                while self.gens:
                    try:
                        next(self.gens[0])
                        return
                    except StopIteration:
                        self.gens.pop(0)

            def __call__(self, w=1):
                self.acc += w * self.total / self.points
                while self.done < int(self.acc + 1e-6):
                    self.step()
                    self.done += 1

            def drain(self):
                while self.gens:
                    self.step()

        last_unit = [None]
        hooks = []

        def together(*gens):
            gens = list(gens)
            while gens:
                for g in list(gens):
                    try:
                        next(g)
                    except StopIteration:
                        gens.remove(g)

        def run(gen):
            try:
                while True:
                    next(gen)
            except StopIteration as e:
                return e.value

        def proj(*a):
            return run(gproj(*a))

        def gproj(name, j, X, xtok, k0=0, nk=8):
            i = open_unit((name, j, k0, nk))
            b, fr = PR.take()
            XH, XL = X
            PE.wait(fr, split_done[i])
            t = None
            for k in range(nk):
                wh, wl = WH[:, i % NW, k * 128:(k + 1) * 128], WL[:, i % NW, k * 128:(k + 1) * 128]
                mm(PS[:, b, :], wh, XH[:, k, :], k == 0, False, xtok[k])
                mm(PS[:, b, :], wh, XL[:, k, :], False, False)
                t = mm(PS[:, b, :], wl, XH[:, k, :], False, k == nk - 1, inc=(k == nk - 1))
                if k % 2 and k < nk - 1:
                    yield
            used[i] = t
            last_unit[0] = t
            while hooks:
                hooks.pop(0)()
            return b, t

        def split_from(bank_or_sb, XH, XL, j, *tok):
            th = acopy(XH[:, j, :], bank_or_sb, *tok)
            tl = tt(XL[:, j, :], bank_or_sb, f(XH[:, j, :]), ALU.subtract, th, *tok)
            return [th, tl]

        s_col = AC.dma(lambda: nc.scalar.dma_start(COL[:, :], col_d), d_col)
        s_c = AC.dma(lambda: nc.scalar.dma_start(C[:, :], con_d), d_con)
        xtok = []
        for j, n in ((0, 1), (1, 1), (2, 2), (4, 2), (6, 2)):
            t = SP.dma(lambda j=j, n=n: nc.sync.dma_start(XT[:, j:j + n, :], xT_d[:, j:j + n, :]), d_x[len(xtok)])
            xtok += [t] * n
            if j < 4:
                load_more(1)

        def fence():
            F = [PE.last(), AC.last(), DV.last(), GP.last()]
            GP.wait(*F)
            AC.wait(*F)
            DV.wait(*F)
            return F

        class Stats:

            def __init__(self, sq, acc):
                self.sq, self.acc, self.n, self.last, self.t = sq, acc, 0, [None, None], None

            def add(self, src, *tok, scale=1.0):
                q = self.n % 2
                dst = self.acc if self.n == 0 else self.sq[q]
                t1 = act(dst, src, ACT.Square, *tok, self.last[q], scale=scale)
                self.t = t1 if self.n == 0 else ptt(self.acc, self.acc, dst, ALU.add, t1, self.t)
                self.last[q] = None if self.n == 0 else self.t
                self.n += 1

            def fold(self):
                b, fr = TR.take()
                return b, mm(PS[:, b, :], con("mean"), self.acc, True, True, self.t, fr, s_c, inc=True)

        RBT = [None]

        def rms(stats, dst=None, *tok):
            b, tm = stats.fold()
            tmp = stats.sq[0]
            tl = act(tmp, PS[:, b, :], ACT.Ln, tm, stats.last[0], bias=col("eps"))
            free[b] = tl
            d = RB if dst is None else dst
            te = act(d, tmp, ACT.Exp, tl, *tok, scale=-0.5)
            if dst is None:
                RBT[0] = te
            return te

        def power(dst, src, scale, *tok, n=1):
            t = GP.op(lambda: G.tensor_scalar(dst, src, scale, EPS, ALU.mult, ALU.add), *tok)
            return ptt(dst, dst, col("nhalf", 0, n=n), ALU.pow, t)

        def scaled(dst, b, t, *tok, p0=0, p1=128, scale=None):
            if scale is None:
                return tt(dst, PS[p0:p1, b, :], RB[p0:p1, :], ALU.mult, t, RBT[0], *tok)
            return stt(dst, PS[p0:p1, b, :], scale, RB[p0:p1, :], ALU.mult, ALU.mult, t, RBT[0], *tok)

        def operand(j, src, g, X, *tok):
            th = act(X[0][:, j, :], src, ACT.Copy, *tok, scale=g)
            tl = stt(X[1][:, j, :], src, g, f(X[0][:, j, :]), ALU.mult, ALU.subtract, th, *tok)
            return [th, tl]

        st0 = Stats([AR[:, 0:512], AR[:, 512:1024]], AR[:, 1024:1536])
        GG = COL[:, COLS["pre2"]:COLS["pre2"] + 8]
        AC.wait(s_col)
        DV.wait(s_col)
        GP.wait(s_col)
        tgg = tt(GG, COL[:, COLS["final_g"]:COLS["final_g"] + 8], COL[:, COLS["pre2"]:COLS["pre2"] + 8], ALU.mult)
        htok = []
        for j in range(8):
            htok.append(operand(j, XT[:, j, :], col("mix_g", j), HX, xtok[j]))
            st0.add(XT[:, j, :], xtok[j])
            if j in (3, 5):
                split_next()
        AC.wait(s_c)
        DV.wait(s_c)
        hooks.append(lambda: rms(st0))
        SLOT = [AR[:, 4608 * i:4608 * (i + 1)] for i in range(2)]
        ar = Arena(4608)
        hq = [ar(1024), ar(1024)]
        hk = [ar(1024), ar(1024)]
        hv = [ar(1028), ar(1028)]
        so = ar(1024)
        xc = ar(516)
        yc = ar(512)
        th_ = ar(512)
        Mb = ar(512)
        Md = ar(128)
        Et = [ar(512), ar(512)]
        WT = ar(1280)
        hm = ar(1024)
        yf = ar(512)
        acol, ecol = ar(16), ar(16)
        stat = ar(64)
        g4 = [ar(512) for _ in range(4)]

        mq = {}
        last_att = {-2: None, -1: None}
        conv_free = [None, None]

        def conv(name, h, j):
            b, t = yield from gproj(name, 2 * h + j, HX, htok)
            c = (0 if name == "qm" else 8) + 2 * h + j
            dst = (hq if name == "qm" else hk)[h % 2][:, j * 512:(j + 1) * 512]
            t1 = scaled(xc[:, 4:516], b, t, conv_free[0])
            free[b] = t1
            t2 = DV.op(lambda: V.memset(xc[:, 0:4], 0.0), conv_free[0])
            t3 = ts(yc, xc[:, 1:513], col("conv_w", 4 * c), col("conv_b", c), ALU.mult, ALU.add, t1, t2, conv_free[1])
            for q in range(1, 4):
                t3 = stt(yc, xc[:, 1 + q:513 + q], col("conv_w", 4 * c + q), yc, ALU.mult, ALU.add, t3)
            conv_free[0] = t3
            t4 = act(th_, yc, ACT.Tanh, t3, conv_free[1], scale=0.5)
            t5 = stt(dst, th_, 1.0, yc, ALU.add, ALU.mult, t4, last_att.get(h - 2))
            conv_free[1] = t5
            mq[(h, name, j)] = t5
            yield

        vt_free = [None]

        def to_tokens(src, dst3, tsrc, *tok):
            b, fr = TR.take()
            for t_ in range(4):
                x = tp(PS[:, b, t_ * 128:(t_ + 1) * 128], src[:, t_ * 128:(t_ + 1) * 128], ident(), tsrc, fr,
                       inc=(t_ == 3))
            free[b] = vcopy(dst3, PS[:, b, :].rearrange("p (t e) -> p t e", t=4), x, *tok)
            return x, free[b]

        def vproj(h, j):
            b, t = yield from gproj("vm", 2 * h + j, HX, htok)
            t1 = scaled(yf, b, t, vt_free[0])
            free[b] = t1
            x, y = to_tokens(yf, hv[h % 2].rearrange("p (t e) -> p t e", t=4)[:, :, j * 128:(j + 1) * 128], t1,
                             last_att.get(h - 2))
            vt_free[0] = x
            mq[(h, "vm", j)] = y
            yield

        def sig_tile(dst, b, t, *tok):
            t0 = scaled(dst, b, t, *tok)
            free[b] = t0
            t1 = act(dst, dst, ACT.Tanh, t0, scale=0.5)
            return ts(dst, dst, 0.5, 0.5, ALU.mult, ALU.add, t1)

        so_free = [None, None]

        def oproj(h, j):
            b, t = yield from gproj("om", 2 * h + j, HX, htok)
            mq[(h, "om", j)] = sig_tile(so[:, j * 512:(j + 1) * 512], b, t, so_free[j])
            yield

        def head_units(h):
            return ([conv("qm", h, j) for j in (0, 1)] + [conv("km", h, j) for j in (0, 1)] +
                    [vproj(h, j) for j in (0, 1)])

        pair_tok = {}
        pair_last = {}
        pv_free = [None]
        ptmp = xc[:, 0:512]

        def pair_units(hp, tmp, tmpfree):
            sl = SLOT[hp % 2]

            def one(g, kind):
                b, t = yield from gproj(("qa", "ka", "va")[kind], 4 * g + hp, HX, htok)
                o = (3 * g + kind) * 512
                gone = pair_last.get(hp - 2)
                if kind < 2:
                    tk = scaled(sl[:, o:o + 512], b, t, gone, scale=0.125 if kind == 0 else None)
                    free[b] = tk
                else:
                    t1 = scaled(tmp, b, t, tmpfree[0])
                    free[b] = t1
                    x, tk = to_tokens(tmp, sl[:, o:o + 512].rearrange("p (t e) -> p t e", t=4), t1, gone)
                    tmpfree[0] = x
                pair_tok.setdefault(hp, []).append(tk)
                yield
            return [one(g, k) for g in range(3) for k in range(3)]

        hu = head_units(0)
        together(hu[0], hu[1])
        b, t = proj("if", 0, HX, htok)
        r = [x[0:4, :] for x in g4]
        t1 = scaled(r[0], b, t, p0=0, p1=4)
        t2 = scaled(r[1], b, t, p0=32, p1=36)
        free[b] = t2
        t1 = ts(r[0], r[0], col("bif", 0, 0, 4), None, ALU.add, ALU.bypass, t1)
        t2 = ts(r[1], r[1], col("bif", 1, 0, 4), None, ALU.add, ALU.bypass, t2)
        t3 = stt(r[2], r[1], -1.0, r[1], ALU.mult, ALU.max, t2)
        t4 = act(r[2], r[2], ACT.Exp, t3, scale=-1.0)
        t5 = act(r[2], r[2], ACT.Ln, t4, bias=col("one", 0, 0, 4))
        t6 = stt(r[1], r[1], 0.0, r[2], ALU.min, ALU.subtract, t5, t2)
        t7 = DV.op(lambda: V.memset(r[3], 1.0))
        t8 = DV.op(lambda: V.tensor_tensor_scan(r[2], r[3], r[1], 0.0, ALU.mult, ALU.add), t6, t7)
        t9 = tt(r[0], r[0], r[2], ALU.subtract, t8)
        t10 = DV.op(lambda: V.tensor_tensor_scan(r[1], r[3], r[0], 0.0, ALU.mult, ALU.max), t9)
        t11 = tt(r[2], r[2], r[1], ALU.add, t10)
        t12 = act(r[2], r[2], ACT.Exp, t11, scale=-1.0)
        tM = t10
        tone = [DV.op(lambda i=i: V.memset(hv[i][:, :].rearrange("p (t e) -> p t e", t=4)[:, :, 256:257], 1.0))
                for i in range(2)][-1]

        for u in hu[2:]:
            run(u)
        b, fr = TR.take()
        for s in range(4):
            tp(PS[:, b, 4 * s:4 * s + 4], r[0][:, s * 128:(s + 1) * 128], ident(4), t9, fr)
            tc = tp(PS[:, b, 16 + 4 * s:20 + 4 * s], r[2][:, s * 128:(s + 1) * 128], ident(4), t12, inc=(s == 3))
        tcol = vcopy(acol, PS[:, b, 0:16], tc)
        tcol = vcopy(ecol, PS[:, b, 16:32], tc)
        free[b] = tcol
        ar = Arena(0)
        SP.wait(GP.last(), AC.last(), DV.last())
        DV.wait(GP.last())
        tab, oh, vecs = ar(24), ar(1920), ar(1920)
        t0 = SP.dma(lambda: nc.sync.dma_start(tab[0:32, :], relb_d), d_vec)
        t0 = SP.dma(lambda: nc.sync.dma_start(oh[0:33, :], oh_d), d_vec)
        t1 = DV.op(lambda: V.memset(tab[32:33, :], NEG))
        tv = []
        for g in range(3):
            for a, n in ((0, 512), (512, 128)):
                b, fr = TR.take()
                tm = mm(PS[0:24, b, 0:n], tab[0:33, :], oh[0:33, g * 640 + a:g * 640 + a + n], True, True,
                        t0, t1, fr, inc=True)
                free[b] = acopy(vecs[0:24, g * 640 + a:g * 640 + a + n], PS[0:24, b, 0:n], tm)
                tv = free[b]
        tvec = SP.dma(lambda: nc.sync.dma_start(scr_d.rearrange("g h i -> h g i"),
                                                vecs[0:24, :].rearrange("p (g i) -> p g i", g=3)), d_vec, tv)
        AC.wait(tvec)
        DV.wait(tvec)
        ya_tok = [None] * 8
        mb_free = [None]
        e_free = [None, None]
        wt_free = [None]
        hm_free = [None]
        yf_free = vt_free
        for h in range(4):
            units = [oproj(h, j) for j in (0, 1)]
            units += head_units(h + 1) if h < 3 else pair_units(0, ptmp, conv_free)
            filler = Filler(units, 14)

            q, k, v = hq[h % 2], hk[h % 2], hv[h % 2]
            b, fr = TR.take()
            t = mm(PS[:, b, :], con("sel", 128 * h, 128 * h + 128, 0, 4), r[1], True, True, tM, fr, inc=True)
            tmb = acopy(Mb, PS[:, b, :], t, mb_free[0])
            free[b] = tmb
            filler()
            tw = []
            wo = [0, 512, 896, 1152]
            for s in range(4):
                n = 512 - 128 * s
                b = SB[s % 3]
                for c in (0, 1):
                    t = mm(PS[:, b, 0:n], k[:, c * 512 + s * 128:c * 512 + s * 128 + 128],
                           q[:, c * 512 + s * 128:c * 512 + 512], c == 0, c == 1,
                           mq[(h, "qm", c)], mq[(h, "km", c)], free[b], inc=(c == 1))
                E = Et[s % 2]
                t1 = tt(Md, Mb[:, s * 128:(s + 1) * 128], con("big"), ALU.add, tmb, e_free[0])
                t2 = act(E[:, 0:128], Md, ACT.Exp, t1, tcol, e_free[s % 2], scale=-1.0,
                         bias=acol[:, 4 * s + h:4 * s + h + 1])
                e_free[0] = t2 if s % 2 else e_free[0]
                md_free = t2
                if n > 128:
                    t2 = act(E[:, 128:n], Mb[:, (s + 1) * 128:512], ACT.Exp, tmb, scale=-1.0,
                             bias=acol[:, 4 * s + h:4 * s + h + 1])
                t3 = stt(WT[:, wo[s]:wo[s] + n], PS[:, b, 0:n], 1.0 / 64.0, E[:, 0:n], ALU.mult, ALU.mult, t, t2,
                         wt_free[0])
                e_free = [t3, t3]
                free[b] = t3
                tw.append(t3)
                filler()
                DV.wait(md_free)
            mb_free[0] = md_free if n <= 128 else t2
            mb_free[0] = AC.last()
            hv3 = v.rearrange("p (t e) -> p t e", t=4)
            hmt = []
            for t_ in range(4):
                b = (OB, SB[0], SB[1], SB[2])[t_]
                fr = free[b]
                for s in range(t_ + 1):
                    o = wo[s] + (t_ - s) * 128
                    t = mm(PS[:, b, 0:257], WT[:, o:o + 128], hv3[:, s, :], s == 0, s == t_, tw[s],
                           mq[(h, "vm", 0)], mq[(h, "vm", 1)], tone, fr, inc=(s == t_))
                d = stat[:, t_:t_ + 1]
                t1 = stt(d, PS[:, b, 256:257], -1.0, ecol[:, 4 * t_ + h:4 * t_ + h + 1], ALU.mult, ALU.max, t, tcol,
                         hm_free[0])
                t1 = tt(d, d, PS[:, b, 256:257], ALU.max, t1)
                t2 = DV.op(lambda d=d: V.reciprocal(d, d), t1)
                hmv = hm[:, t_ * 256:(t_ + 1) * 256]
                t3 = AC.op(lambda hmv=hmv, b=b, d=d: A.activation(hmv, PS[:, b, 0:256], ACT.Copy, scale=d),
                           t2, hm_free[0])
                free[b] = t3
                st6 = stat[:, 8 + 6 * t_:14 + 6 * t_]
                t4 = DV.op(lambda hmv=hmv, st6=st6: V.bn_stats(st6, hmv), t3)
                mv = stat[:, 32 + 2 * t_:34 + 2 * t_]
                t5 = DV.op(lambda mv=mv, st6=st6: V.bn_aggr(mv, st6), t4)
                hmt.append(t5)
                if t_ == 3:
                    wt_free[0] = t
                    last_att[h] = t
                filler()
            var = stat[:, 33:40:2]
            rs = stat[:, 40:44]
            t1 = power(rs, var, 1.0, hmt[-1], n=4)
            for t_ in range(4):
                hmv = hm[:, t_ * 256:(t_ + 1) * 256]
                t2 = ts(hmv, hmv, stat[:, 32 + 2 * t_:33 + 2 * t_], rs[:, t_:t_ + 1], ALU.subtract, ALU.mult, t1,
                        hmt[t_])
            filler(3)
            for j in (0, 1):
                b, fr = TR.take()
                for t_ in range(4):
                    t = tp(PS[:, b, t_ * 128:(t_ + 1) * 128], hm[:, t_ * 256 + j * 128:t_ * 256 + j * 128 + 128],
                           ident(), t2, fr, inc=(t_ == 3))
                t3 = stt(yf, PS[:, b, :], col("mnorm", 2 * h + j), so[:, j * 512:(j + 1) * 512], ALU.mult, ALU.mult,
                         t, mq[(h, "om", j)], yf_free[0])
                free[b] = t3
                so_free[j] = t3
                t4 = split_from(yf, AH, AL, 2 * h + j, t3)
                yf_free[0] = t4
                ya_tok[2 * h + j] = t4
                hm_free[0] = t
                filler()
            filler.drain()
        F = fence()
        SP.wait(*F)

        ar = Arena(9216)
        MG = ar(4096)
        MG3 = MG.rearrange("p (j t) -> p j t", j=8)
        BI = [ar(1280), ar(1280)]
        SS = [ar(1280), ar(1280)]
        PT = ar(1280)
        yb = ar(512)
        st = ar(32)

        bias_tok = {}
        bias_free = {-2: None, -1: None}

        def load_bias(h):
            t = BI[h % 2]
            SP.wait(bias_free[h - 2])
            for g in (1, 2):
                src = bass.AP(scr_d.tensor, scr_d.offset + (g * 24 + g * 8 + h) * 640, [[1, 128], [1, 512]])
                SP.dma(lambda g=g, src=src: nc.sync.dma_start(t[:, (g - 1) * 512:g * 512], src), d_bias[h % 2])
            src0 = bass.AP(scr_d.tensor, scr_d.offset + h * 640, [[1, 128], [1, 256]])
            bias_tok[h] = SP.dma(lambda: nc.sync.dma_start(t[:, 1024:1280], src0), d_bias[h % 2])

        load_bias(0)
        load_bias(1)

        def rev(ap, start, n, outer=None):
            dims = [list(ap.ap[0])] + ([list(outer)] if outer else []) + [[-1, n]]
            return bass.AP(ap.tensor, ap.offset + start, dims)

        sgt = SS[0][:, 0:512]
        sg_free = None
        mtok = []
        for j in range(8):
            b, t = proj("ga", j, HX, htok)
            t1 = sig_tile(sgt, b, t, sg_free)
            b, t = proj("pa", j, AX_, ya_tok)
            t2 = tt(MG3[:, j, :], sgt, PS[:, b, :], ALU.mult, t, t1)
            free[b] = t2
            sg_free = t2
            mtok.append(t2)
        ss_free = [sg_free, None]
        pt_free = [None]
        yb_free = [None]
        yb_tok = [None] * 4
        sc_free = [None, None]

        def att_a(it):
            hp, i, n = it
            h = 2 * hp + i
            par = ORD_N.index(n) % 2
            sl = SLOT[hp % 2]
            W = 128 * (n + 1)
            k0 = max(0, n - 1)
            W0 = 128 * (n + 1 - k0)
            p = slice(64 * i, 64 * i + 64)
            toks = []
            for g, bnk, ka, w in ((1, SB[0], 0, W), (2, SB[1], 0, W), (0, SB[2], k0 * 128, W0)):
                o = 3 * g * 512
                toks.append(mm(PS[:, bnk, 0:w], sl[p, o + n * 128:o + n * 128 + 128],
                               sl[p, o + 512 + ka:o + 512 + ka + w], True, True, pair_tok[hp], free[bnk], inc=True))
            return lambda: att_s(it, toks)

        def att_s(it, toks):
            hp, i, n = it
            h = 2 * hp + i
            par = ORD_N.index(n) % 2
            W = 128 * (n + 1)
            W0 = 128 * min(2, n + 1)
            Sx = SS[par]
            bi = BI[h % 2]
            t1 = tt(Sx[:, 0:2 * W].rearrange("p (g k) -> p g k", g=2), PS[:, SB[0]:SB[0] + 2, 0:W],
                    rev(bi, W - 1, W, (512, 2)), ALU.add, toks[1], bias_tok[h], ss_free[par])
            free[SB[0]] = free[SB[1]] = t1
            t2 = tt(Sx[:, 2 * W:2 * W + W0], PS[:, SB[2], 0:W0], rev(bi, 1024 + W0 - 1, W0), ALU.add, toks[2])
            free[SB[2]] = t2
            if n == LAST_N:
                bias_free[h] = t2
                if h + 2 < 8:
                    load_bias(h + 2)
            nm, l = st[:, par:par + 1], st[:, 2 + par:3 + par]
            N = 2 * W + W0
            t3 = DV.op(lambda: V.tensor_reduce(nm, Sx[:, 0:N], AX, ALU.max, negate=True), t1, t2, sc_free[par])
            t4 = AC.op(lambda: A.activation(Sx[:, 0:N], Sx[:, 0:N], ACT.Exp, bias=nm, accum_out=l), t3)
            return t4, (par, N, l)

        def transposes(Sx, nblk, tS, filler, first):
            out = []
            m = 0
            while m < nblk:
                if m == 8:
                    filler()
                c = min(4, nblk - m)
                b, fr = TR.take()
                for q in range(c):
                    t = tp(PS[:, b, q * 128:(q + 1) * 128], Sx[:, (m + q) * 128:(m + q + 1) * 128], ident(), tS, fr,
                           inc=(q == c - 1))
                e = acopy if (m // 4 + first) % 2 else vcopy
                free[b] = e(PT[:, m * 128:(m + c) * 128], PS[:, b, 0:c * 128], t, pt_free[0])
                out.append(free[b])
                m += c
            return t, out

        LAST_N = 1
        ORD_N = (3, 0, 2, 1)

        def att_b(it, tS, info, fill, softmax):
            hp, i, n = it
            par, N, l = info
            Sx = SS[par]
            sl = SLOT[hp % 2]
            nb = N // 128
            tl, ev = transposes(Sx, nb, tS, fill, 0)
            ss_free[par] = tl
            nxt = softmax() if softmax else None
            fill()
            keys = [(1, j) for j in range(n + 1)] + [(2, j) for j in range(n + 1)] + \
                   [(0, j) for j in range(max(0, n - 1), n + 1)]
            for m, (g, j) in enumerate(keys):
                o = (3 * g + 2) * 512 + j * 128 + 64 * i
                t = mm(PS[:, OB, 0:64], PT[:, m * 128:(m + 1) * 128], sl[:, o:o + 64], m == 0, m == nb - 1,
                       ev, free[OB], inc=(m == nb - 1))
            pt_free[0] = t
            t1 = DV.op(lambda: V.reciprocal(l, l), tS)
            o = n * 128 + 64 * i
            t2 = ts(yb[:, o:o + 64], PS[:, OB, 0:64], l, None, ALU.mult, ALU.bypass, t, t1, yb_free[0])
            free[OB] = t2
            sc_free[par] = t2
            return t, t2, nxt

        def run_pair(hp, units):
            items = [(hp, i, n) for i in (0, 1) for n in ORD_N]
            fill = Filler(units, 26)
            nxt = att_a(items[0])()
            for m, it in enumerate(items):
                fill()
                cur = nxt
                sm = att_a(items[m + 1]) if m + 1 < len(items) else None
                fill()
                t, t2, nxt = att_b(it, *cur, fill, sm)
            pair_last[hp] = t
            fill.drain()
            b, fr = TR.take()
            for n in range(4):
                t = tp(PS[:, b, n * 128:(n + 1) * 128], yb[:, n * 128:(n + 1) * 128], ident(), t2, fr, inc=(n == 3))
            yb_free[0] = t
            yb_tok[hp] = split_from(PS[:, b, :], AH, AL, hp, t, pa_done)
            free[b] = yb_tok[hp]

        pa_done = last_unit[0]
        vt = AR[:, ar.at:ar.at]
        vtmp_free = [None]
        vtmp = yf2 = None
        for hp in range(3):
            run_pair(hp, pair_units(hp + 1, VT[:, :], vtmp_free))
        gb3 = SLOT[0][:, 0:4096].rearrange("p (j t) -> p j t", j=8)
        gtok = [None] * 8

        def gbu(j):
            b, t = yield from gproj("gb", j, HX, htok)
            gtok[j] = sig_tile(gb3[:, j, :], b, t, pair_last[2])
            yield
        run_pair(3, [gbu(j) for j in range(8)])
        mt = []
        for j in range(8):
            b, t = proj("pb", j, AX_, yb_tok, 0, 4)
            t1 = tt(gb3[:, j, :], gb3[:, j, :], PS[:, b, :], ALU.mult, t, gtok[j])
            free[b] = t1
            t2 = tt(MG3[:, j, :], MG3[:, j, :], gb3[:, j, :], ALU.add, t1, mtok[j])
            mt.append(split_from(MG3[:, j, :], HH, HL, j, t2))
        xtok = []
        pb_done = last_unit[0]
        nst = Stats([SS[0][:, 0:512], SS[0][:, 512:1024]], SS[1][:, 0:512])
        GP.wait(DV.last(), AC.last(), PE.last())
        htok = []
        for j in range(8):
            b, t = proj("out", j, HX, mt)
            t1 = tt(XT[:, j, :], XT[:, j, :], PS[:, b, :], ALU.add, t)
            free[b] = t1
            xtok.append(t1)
            htok.append(operand(j, XT[:, j, :], col("ffn_g", j), AX_, t1, pb_done))
            nst.add(XT[:, j, :], t1)
        out_done = last_unit[0]
        hooks.append(lambda: rms(nst, None, DV.last()))

        def ffn(sfx, X, Y, htok, ar, dst3, dtok, accumulate, ydone, finished):
            sg = [ar(512), ar(512)]
            sr = [ar(512), ar(512)]
            pf = [ar(512), ar(512)]
            sgf, srf, pff = [None, None], [None, None], [None, None]
            down_done = ydone
            out = list(dtok)
            for a, e in FFN_PARTS:
                tk = []

                def gate(t_):
                    q = t_ % 2
                    b, t = yield from gproj("gate" + sfx, t_, X, htok)
                    t1 = scaled(sg[q], b, t, sgf[q])
                    free[b] = t1
                    t2 = act(sg[q], sg[q], ACT.Silu, t1)
                    sgf[q] = srf[q] = ptt(sr[q], sg[q], RB, ALU.mult, t2, RBT[0], pff[q])
                    yield

                def up(t_):
                    q = t_ % 2
                    b, t = yield from gproj("up" + sfx, t_, X, htok)
                    t2 = tt(pf[q], sr[q], PS[:, b, :], ALU.mult, t, srf[q], pff[q])
                    free[b] = t2
                    t3 = split_from(pf[q], Y[0], Y[1], t_ - a, t2, down_done)
                    pff[q] = t3
                    tk.append(t3)
                    yield

                for t_ in range(a, e):
                    if t_ == 0:
                        together(gate(t_), up(t_))
                    else:
                        run(gate(t_))
                        run(up(t_))
                up_done = last_unit[0]
                for j in range(8):
                    b, t = proj("down" + sfx, j, Y, tk, a, e - a)
                    if accumulate or a > 0:
                        out[j] = tt(dst3[:, j, :], dst3[:, j, :], PS[:, b, :], ALU.add, t, out[j])
                    else:
                        out[j] = vcopy(dst3[:, j, :], PS[:, b, :], t)
                    free[b] = out[j]
                    if e == 22:
                        finished(j, out[j], up_done)
                down_done = last_unit[0]
            return out

        arF = Arena(0)
        nst1 = Stats([arF(512), arF(512)], arF(512))
        nst2 = Stats([arF(512), arF(512)], arF(512))
        R1 = VT[:, :]
        htok2 = []
        fence()

        def end1(j, t, up_done):
            htok2.append(operand(j, XT[:, j, :], GG[:, j:j + 1], AX_, t, up_done, tgg))
            nst1.add(XT[:, j, :], t)
            nst2.add(XT[:, j, :], t, scale=col("final_g", j))

        xtok = ffn("", AX_, HX, htok, arF, XT, xtok, True, out_done, end1)
        def two_norms():
            t1 = rms(nst1, R1, DV.last())
            b, tm = nst2.fold()
            t2 = tt(nst2.sq[0], PS[:, b, :], R1, ALU.mult, tm, t1, nst2.last[0])
            free[b] = t2
            t2 = tt(nst2.sq[0], nst2.sq[0], R1, ALU.mult, t2)
            t3 = act(nst2.sq[1], nst2.sq[0], ACT.Ln, t2, nst2.last[1], bias=col("eps"))
            t3 = act(nst2.sq[1], nst2.sq[1], ACT.Exp, t3, scale=-0.5)
            RBT[0] = tt(RB, nst2.sq[1], R1, ALU.mult, t3, GP.last())

        hooks.append(two_norms)
        htok = htok2
        down_done = last_unit[0]
        F = fence()
        SP.wait(*F)

        ar = Arena(0)
        EB, ENB, EKD = [ar(512), ar(512)], [ar(512), ar(512)], [ar(512), ar(512)]
        BLK = [AR[:, 0:992], AR[:, 1024:2016]]
        NQ = [ar(512) for _ in range(4)]
        NKC, NVC, NKS, NKW, NVS, NVW = [ar(512) for _ in range(6)]
        nsa_at = ar.at
        qe = [ar(512), ar(512)]
        ke = [ar(512), ar(512)]
        kdt = [ar(512), ar(512)]
        gv = [ar(1024), ar(1024)]
        kd, vtm = ar(512), ar(512)
        rr = ar(1024)
        St = [ar(256), ar(256)]
        attn = ar(256)
        on = ar(1024)
        gst = ar(32)
        yf = ar(512)
        th2 = ar(512)
        wa2 = ar(512)
        alr = ar(512)
        dec = ar(32)
        reset = ar(512)
        CM = sb("CM", [128, 128])
        kcT, vcs = AR[:, 2080:2112], CM[:, 0:128]
        hid, th3, w2s = ar(64), ar(64), ar(256)
        gts = kd
        t0 = SP.dma(lambda: nc.sync.dma_start(wa2[0:16, :], wa2_d), d_b2)
        tw2 = SP.dma(lambda: nc.sync.dma_start(w2s, w2_d), d_w2)
        t_rs = DV.op(lambda: V.memset(reset, 1.0))
        t_rs = DV.op(lambda: V.memset(reset.rearrange("p (n c) -> p n c", c=64)[:, :, 0:1], 0.0), t_rs)
        t_at0 = DV.op(lambda: V.memset(attn, 0.0))
        gq = {}
        g_last = {-2: None, -1: None}
        vt_free = [None]
        kd_free = [None]
        small = {}
        XO = AX_

        def small_unit():
            b, t = yield from gproj("small2", 0, XO, htok)
            small["a"] = scaled(alr[0:16, :], b, t, p0=0, p1=16)
            t1 = scaled(gts[0:24, :], b, t, p0=32, p1=56)
            free[b] = t1
            t2 = act(gts[0:24, :], gts[0:24, :], ACT.Tanh, t1, scale=0.5)
            b, fr = TR.take()
            for n in range(4):
                t = tp(PS[:, b, 24 * n:24 * n + 24], gts[0:24, n * 128:(n + 1) * 128], ident(24), t2, fr,
                       inc=(n == 3))
            small["g"] = ts(GT[:, :], PS[:, b, 0:96], 0.5, 0.5, ALU.mult, ALU.add, t)
            free[b] = small["g"]
            kd_free[0] = t
            yield

        def decays(h):
            b, fr = TR.take()
            gone = gq.get((h - 2, "k"))
            t = mm(PS[:, b, :], wa2[0:16, h * 128:(h + 1) * 128], alr[0:16, :], True, True, t0, small["a"], fr,
                   inc=True)
            z, e, w = EB[h % 2], ENB[h % 2], EKD[h % 2]
            t3 = ts(z, PS[:, b, :], col("balpha", h), None, ALU.add, ALU.bypass, t, gone)
            free[b] = t3
            t4 = stt(e, z, -1.0, z, ALU.mult, ALU.max, t3)
            t5 = act(e, e, ACT.Exp, t4, scale=-1.0)
            t5 = act(e, e, ACT.Ln, t5, bias=col("one"))
            t6 = stt(z, z, 0.0, e, ALU.min, ALU.subtract, t5, t3)
            t7 = DV.op(lambda: V.tensor_tensor_scan(w, reset, z, 0.0, ALU.mult, ALU.add), t6, t_rs)
            t8 = act(z, w, ACT.Exp, t7, scale=1.0 / 16)
            t9 = act(e, w, ACT.Exp, t7, scale=-1.0 / 16)
            td = vcopy(dec[:, 8 * h:8 * h + 8], z.rearrange("p (n c) -> p n c", c=64)[:, :, 63:64], t8)
            w3 = w.rearrange("p (n c) -> p n c", c=64)
            t10 = tt(w3, w3[:, :, 63:64].to_broadcast([128, 8, 64]), w3, ALU.subtract, t8, t9, t7)
            t11 = act(w, w, ACT.Exp, t10, scale=1.0 / 16)
            small[("eb", h)] = ptt(z, z, RB, ALU.mult, t8, td, RBT[0])
            small[("enb", h)] = ptt(e, e, RB, ALU.mult, t9, RBT[0])
            small[("ekd", h)] = ptt(w, w, RB, ALU.mult, t11, RBT[0])

        def decay_unit(h):
            decays(h)
            return
            yield

        def gla_unit(h, what):
            if what == 0:
                b, t = yield from gproj("gq", h, XO, htok)
                gq[(h, 0)] = free[b] = stt(qe[h % 2], PS[:, b, :], float(128 ** -0.5), EB[h % 2], ALU.mult, ALU.mult,
                                           t, small[("eb", h)], g_last[h - 2])
            elif what == 1:
                b, t = yield from gproj("gk", h, XO, htok)
                gq[(h, 1)] = tt(ke[h % 2], PS[:, b, :], ENB[h % 2], ALU.mult, t, small[("enb", h)], g_last[h - 2])
                t2 = tt(kd, PS[:, b, :], EKD[h % 2], ALU.mult, small[("ekd", h)], kd_free[0])
                free[b] = gq[(h, "k")] = t2
                x, gq[(h, 2)] = to_tokens(kd, kdt[h % 2].rearrange("p (t e) -> p t e", t=4), t2, g_last[h - 2])
                kd_free[0] = x
            else:
                j = what - 2
                b, t = yield from gproj("gv", 2 * h + j, XO, htok)
                t1 = scaled(vtm, b, t, vt_free[0])
                free[b] = t1
                x, gq[(h, 3 + j)] = to_tokens(vtm, gv[h % 2].rearrange("p (t e) -> p t e", t=4)
                                              [:, :, j * 128:(j + 1) * 128], t1, g_last[h - 2])
                vt_free[0] = x
            yield

        r_free = [None, None]
        th_free = [None]

        def gla_r(h, j):
            b, t = yield from gproj("gr", 2 * h + j, XO, htok)
            rj = rr[:, j * 512:(j + 1) * 512]
            t0_ = scaled(rj, b, t, r_free[j])
            free[b] = t0_
            t1 = act(th2, rj, ACT.Tanh, t0_, th_free[0], scale=0.5)
            t2 = stt(rj, th2, 1.0, rj, ALU.add, ALU.mult, t1)
            th_free[0] = t2
            gq[(h, "r", j)] = t2
            yield

        ntok = {}

        def nsa_unit(name, i):
            b, t = yield from gproj(name, i, XO, htok)
            if name == "nq":
                ntok[("nq", i)] = free[b] = scaled(NQ[i], b, t, scale=0.125)
            elif name in ("vs", "vw"):
                t1 = scaled(vtm, b, t, vt_free[0])
                free[b] = t1
                x, ntok[name] = to_tokens(vtm, {"vs": NVS, "vw": NVW}[name].rearrange("p (t e) -> p t e", t=4), t1)
                vt_free[0] = x
            else:
                ntok[name] = free[b] = scaled({"kc": NKC, "vc": NVC, "ks": NKS, "kw": NKW}[name], b, t)
            yield

        def compress_blocks(c):
            src, pe_ = ((NKC, "pek"), (NVC, "pev"))[c]
            win = bass.AP(src.tensor, src.offset, [list(src.ap[0]), [1, 32], [16, 31]])
            pex = COL[:, COLS[pe_]:COLS[pe_] + 32]
            peb = bass.AP(pex.tensor, pex.offset, [list(pex.ap[0]), [1, 32], [0, 31]])
            ntok[("blk", c)] = tt(BLK[c].rearrange("p (l n) -> p l n", l=32), win, peb, ALU.add,
                                  ntok[("kc", "vc")[c]], gq[(3, 0)], gq[(3, 1)], gq[(3, "k")])
            return
            yield

        def compress_1(c):
            b, fr = PR.take()
            for m in range(4):
                i = open_unit((("w1k", "w1v")[c], m, 0, 8))
                for l in range(8):
                    L = 8 * m + l
                    t = mm(PS[:, b, 0:31], RAW[:, i % NR, l * 128:(l + 1) * 128], BLK[c][:, 31 * L:31 * L + 31],
                           L == 0, L == 31, split_done[i], ntok[("blk", c)], fr, inc=(l == 7))
                used[i] = t
                load_more()
                yield
            h_, x_ = hid[:, 32 * c:32 * c + 31], th3[:, 32 * c:32 * c + 31]
            t2 = act(x_, PS[:, b, 0:31], ACT.Tanh, t, scale=0.5)
            t3 = ts(x_, x_, 0.5, 0.5, ALU.mult, ALU.add, t2)
            free[b] = ntok[("hid", c)] = tt(h_, x_, PS[:, b, 0:31], ALU.mult, t3)

        def compress_2(c):
            h_ = hid[:, 32 * c:32 * c + 31]
            b, fr = TR.take()
            if c == 0:
                t = mm(PS[:, b, 0:31], w2s[:, 0:128], h_, True, True, ntok[("hid", 0)], tw2, fr, inc=True)
                ntok["kcT"] = free[b] = vcopy(kcT[:, 0:31], PS[:, b, 0:31], t)
            else:
                t = mm(PS[0:31, b, 0:128], h_, w2s[:, 128:256], True, True, ntok[("hid", 1)], tw2, fr, inc=True)
                ntok["vcs"] = free[b] = vcopy(vcs[0:31, :], PS[0:31, b, 0:128], t)
            return
            yield

        def gla_units(h):
            return [gla_unit(h, 2), gla_unit(h, 3), gla_unit(h, 0), gla_unit(h, 1)]

        gu = gla_units(0)
        together(small_unit(), gu[0])
        decays(0)
        for u in gu[1:]:
            run(u)
        for j in range(8):
            xtok[j] = stt(XT[:, j, :], XT[:, j, :], col("final_g", j), R1, ALU.mult, ALU.mult, xtok[j], htok2[j],
                          nst1.t, nst2.t)
        att_free = [t_at0]
        st_free = [None, None]
        on_free = [None]
        yg_tok = [None] * 8
        yf_free = [None]
        glam = con("glam").bitcast(i32)
        for h in range(4):
            units = [gla_r(h, j) for j in (0, 1)]
            if h < 3:
                units += [decay_unit(h + 1)] + gla_units(h + 1)
            else:
                units += [nsa_unit("kc", 0), nsa_unit("vc", 0), compress_blocks(0), compress_blocks(1),
                          compress_1(0)]
                units += [nsa_unit("nq", i) for i in range(4)] + [compress_1(1), compress_2(0)]
                units += [nsa_unit(n, 0) for n in ("ks", "kw", "vs", "vw")] + [compress_2(1)]
            fill = Filler(units, 18)
            q_, k_, kt_, v_ = qe[h % 2], ke[h % 2], kdt[h % 2], gv[h % 2]
            v3 = v_.rearrange("p (t e) -> p t e", t=4)
            b = SB[0]
            for n in range(8):
                pb, T_ = 64 * (n % 2), n // 2
                t = mm(PS[pb:pb + 64, b, T_ * 64:T_ * 64 + 64], k_[:, n * 64:n * 64 + 64], q_[:, n * 64:n * 64 + 64],
                       True, True, gq[(h, 0)], gq[(h, 1)], free[b], inc=(n == 7))
            mask3 = bass.AP(glam.tensor, glam.offset, [list(glam.ap[0]), [0, 4], [1, 64]])
            ta = DV.op(lambda b=b: V.copy_predicated(attn.rearrange("p (t c) -> p t c", t=4), mask3,
                                                     PS[:, b, 0:256].rearrange("p (t c) -> p t c", t=4)),
                       t, att_free[0])
            free[b] = ta
            tst = None
            for T_ in range(4):
                up_ = {}
                for n in (2 * T_, 2 * T_ + 1):
                    if n == 7:
                        continue
                    pb = 64 * (n % 2)
                    ub = SB[1 + n % 2]
                    up_[n] = (ub, mm(PS[:, ub, 0:256], kt_[pb:pb + 64, T_ * 128:(T_ + 1) * 128], v3[pb:pb + 64, T_, :],
                                     True, True, gq[(h, 2)], gq[(h, 3)], gq[(h, 4)], free[ub], inc=True))
                fill(1 if T_ else 2)
                for n in (2 * T_, 2 * T_ + 1):
                    pb = 64 * (n % 2)
                    t = mm(PS[pb:pb + 64, OB, 0:256], attn[pb:pb + 64, T_ * 64:T_ * 64 + 64], v3[pb:pb + 64, T_, :],
                           True, n == 0, ta, free[OB], inc=True)
                    if n > 0:
                        t = mm(PS[pb:pb + 64, OB, 0:256], q_[:, n * 64:n * 64 + 64], St[(n - 1) % 2], False, True,
                               tst, inc=True)
                        st_free[(n - 1) % 2] = t
                    if n < 7:
                        ub, tu = up_[n]
                        if n == 0:
                            tst = vcopy(St[0], PS[:, ub, 0:256], tu, st_free[0])
                        else:
                            tst = stt(St[n % 2], St[(n - 1) % 2], dec[:, 8 * h + n:8 * h + n + 1],
                                      PS[:, ub, 0:256], ALU.mult, ALU.add, tu, tst, st_free[n % 2])
                        free[ub] = tst
                    fill()
                ss, rs = gst[:, T_:T_ + 1], gst[:, 8 + T_:9 + T_]
                onv = on[:, T_ * 256:(T_ + 1) * 256]
                t1 = AC.op(lambda onv=onv, ss=ss: A.activation(onv, PS[:, OB, 0:256], ACT.Square, accum_out=ss),
                           t, on_free[0])
                t2 = power(rs, ss, 1.0 / 256, t1)
                t3 = ts(onv, PS[:, OB, 0:256], rs, 0.5, ALU.mult, ALU.mult, t2)
                free[OB] = t3
            g_last[h] = t
            att_free[0] = t
            fill(2)
            for j in (0, 1):
                b, fr = TR.take()
                for t_ in range(4):
                    t = tp(PS[:, b, t_ * 128:(t_ + 1) * 128], on[:, t_ * 256 + j * 128:t_ * 256 + j * 128 + 128],
                           ident(), t3, fr, inc=(t_ == 3))
                t4 = stt(yf, PS[:, b, :], col("glag", j), rr[:, j * 512:(j + 1) * 512], ALU.mult, ALU.mult, t,
                         gq[(h, "r", j)], yf_free[0])
                free[b] = t4
                r_free[j] = t4
                t5 = split_from(yf, HH, HL, 2 * h + j, t4, down_done)
                yf_free[0] = t5
                yg_tok[2 * h + j] = t5
                on_free[0] = t
            fill(2)
            fill.drain()
        F = fence()
        tkc, tvc, tg2 = ntok["kcT"], ntok["vcs"], small["g"]
        ar = Arena(0)
        yb = ar(2048)
        st = ar(32)
        ar = Arena(nsa_at)
        MGN = ar(8192)
        MG3 = MGN[:, 0:4096].rearrange("p (j t) -> p j t", j=8)
        SN3 = MGN[:, 4096:8192].rearrange("p (j t) -> p j t", j=8)
        SS = [ar(1056), ar(1056)]
        PT = ar(1280)
        yb3 = yb.rearrange("p (n c) -> p n c", n=4)
        ss_free = [None, None]
        pt_free = [None]
        sc_free = [None, None]
        mtok, stok = [None] * 8, [None] * 8
        sgt_free = [None]
        SGT = VT[:, :]
        comp_done = None

        def merge_units(j):
            def a():
                b, t = yield from gproj("mg", j, XO, htok)
                sgt_free[0] = sig_tile(SGT, b, t, sgt_free[0], xtok[7])
                yield

            def c():
                b, t = yield from gproj("pg", j, HX, yg_tok)
                mtok[j] = tt(MG3[:, j, :], SGT, PS[:, b, :], ALU.mult, t, sgt_free[0])
                free[b] = mtok[j]
                sgt_free[0] = mtok[j]
                yield

            def d():
                b, t = yield from gproj("mn", j, XO, htok)
                stok[j] = sig_tile(SN3[:, j, :], b, t)
                yield
            return [a(), c(), d()]

        fill = []
        for j in range(8):
            fill += merge_units(j)

        def nsa_a(it):
            h, n = it
            par = ORD_N.index(n) % 2
            i = h % 4
            p = slice(64 * (h // 4), 64 * (h // 4) + 64)
            W = 128 * (n + 1)
            qv = NQ[i][p, n * 128:(n + 1) * 128]
            ta_ = mm(PS[:, SB[0], 0:W], qv, NKS[p, 0:W], True, True, ntok[("nq", i)], ntok["ks"], free[SB[0]], inc=True)
            tb_ = mm(PS[:, SB[1], 0:W], qv, NKW[p, 0:W], True, True, ntok["kw"], free[SB[1]], inc=True)
            tc_ = mm(PS[:, SB[2], 0:31], qv, kcT[p, 0:31], True, True, tkc, free[SB[2]], inc=True)
            return lambda: nsa_s(it, tb_, tc_)

        def nsa_s(it, tb_, tc_):
            h, n = it
            par = ORD_N.index(n) % 2
            W = 128 * (n + 1)
            slope = float(2.0 ** (-8.0 * (h + 1) / 8))
            Sx = SS[par]
            ba = con("ba", 128 * (3 - n), 512)
            ba2 = bass.AP(ba.tensor, ba.offset, [list(ba.ap[0]), [0, 2], [1, W]])
            t1 = stt(Sx[:, 0:2 * W].rearrange("p (g k) -> p g k", g=2), ba2, slope, PS[:, SB[0]:SB[0] + 2, 0:W],
                     ALU.mult, ALU.add, tb_, ss_free[par])
            free[SB[0]] = free[SB[1]] = t1
            Sc = Sx[:, 1024:1055]
            t2 = stt(Sc, con("bc", 31 * n, 31 * n + 31), slope, PS[:, SB[2], 0:31], ALU.mult, ALU.add, tc_)
            free[SB[2]] = t2
            nm, l = st[:, 3 * par:3 * par + 3], st[:, 8 + 3 * par:11 + 3 * par]
            t3 = DV.op(lambda: V.tensor_reduce(nm[:, 1:3], Sx[:, 0:2 * W].rearrange("p (g k) -> p g k", g=2), AX,
                                               ALU.max, negate=True), t1, sc_free[par])
            t3 = DV.op(lambda: V.tensor_reduce(nm[:, 0:1], Sc, AX, ALU.max, negate=True), t2)
            AC.op(lambda: A.activation(Sc, Sc, ACT.Exp, bias=nm[:, 0:1], accum_out=l[:, 0:1]), t3)
            AC.op(lambda: A.activation(Sx[:, 0:W], Sx[:, 0:W], ACT.Exp, bias=nm[:, 1:2], accum_out=l[:, 1:2]))
            t4 = AC.op(lambda: A.activation(Sx[:, W:2 * W], Sx[:, W:2 * W], ACT.Exp, bias=nm[:, 2:3],
                                            accum_out=l[:, 2:3]))
            return t4, (par, l)

        def nsa_b(it, tS, info, fill, softmax):
            h, n = it
            par, l = info
            Sx = SS[par]
            W = 128 * (n + 1)
            g_ = h // 4
            Sc = Sx[:, 1024:1055]
            t5 = tt(Sc, Sc, con("m01", 31 * n, 31 * n + 31), ALU.mult, tS)
            tl, ev = transposes(Sx, 2 * (n + 1), tS, lambda: None, 1)
            b, fr = TR.take()
            tl = tp(PS[0:31, b, 0:128], Sc, ident(), t5, fr, inc=True)
            e2 = free[b] = acopy(PT[0:31, 1024:1152], PS[0:31, b, 0:128], tl, pt_free[0])
            ss_free[par] = tl
            t6 = DV.op(lambda: V.reciprocal(l, l), tS)
            t6 = tt(l, l, GT[:, 24 * n + 3 * h:24 * n + 3 * h + 3], ALU.mult, t6, tg2)
            nxt = softmax() if softmax else None
            fill()
            for br, (vv, c0) in enumerate(((NVS, 64), (NVW, 128))):
                for j in range(n + 1):
                    m = br * (n + 1) + j
                    mm(PS[:, OB, c0:c0 + 64], PT[:, m * 128:(m + 1) * 128],
                       vv[:, j * 128 + 64 * g_:j * 128 + 64 * g_ + 64], j == 0, j == n, ev, ntok["vs"], ntok["vw"],
                       free[OB])
            t = mm(PS[:, OB, 0:64], PT[0:31, 1024:1152], vcs[0:31, 64 * g_:64 * g_ + 64], True, True, e2, tvc,
                   inc=True)
            pt_free[0] = t
            y = yb3[:, n, 64 * h:64 * h + 64]
            t7 = ts(y, PS[:, OB, 0:64], l[:, 0:1], None, ALU.mult, ALU.bypass, t, t6)
            t7 = stt(y, PS[:, OB, 64:128], l[:, 1:2], y, ALU.mult, ALU.add, t7)
            t7 = stt(y, PS[:, OB, 128:192], l[:, 2:3], y, ALU.mult, ALU.add, t7)
            free[OB] = t7
            sc_free[par] = t7
            return t7, nxt

        items = [(h, n) for h in range(8) for n in ORD_N]
        fill = Filler(fill, 3 * len(items))
        nxt = nsa_a(items[0])()
        for m, it in enumerate(items):
            fill()
            cur = nxt
            sm = nsa_a(items[m + 1]) if m + 1 < len(items) else None
            fill()
            t7, nxt = nsa_b(it, *cur, fill, sm)
        fill.drain()
        pg_done = last_unit[0]
        yn_tok = []
        for j in range(4):
            b, fr = TR.take()
            for n in range(4):
                t = tp(PS[:, b, n * 128:(n + 1) * 128], yb3[:, n, j * 128:(j + 1) * 128], ident(), t7, fr,
                       inc=(n == 3))
            x = split_from(PS[:, b, :], HH, HL, j, t, pg_done)
            free[b] = x
            yn_tok.append(x)
        mt = []
        for j in range(8):
            b, t = proj("pn", j, HX, yn_tok, 0, 4)
            t1 = tt(SN3[:, j, :], SN3[:, j, :], PS[:, b, :], ALU.mult, t, stok[j])
            free[b] = t1
            t2 = tt(MG3[:, j, :], MG3[:, j, :], SN3[:, j, :], ALU.add, t1, mtok[j])
            mt.append(split_from(MG3[:, j, :], AH, AL, j, t2, pg_done))
        pn_done = last_unit[0]

        def post(name, src3, stats, ar, then):
            te = rms(stats, R1, DV.last(), GP.last())
            tmp = [ar(512), ar(512)]
            last = [None, None]
            for j in range(8):
                t = stt(tmp[j % 2], src3[:, j, :], col(name, j), R1, ALU.mult, ALU.mult, te, last[j % 2])
                last[j % 2] = ptt(XT[:, j, :], XT[:, j, :], tmp[j % 2], ALU.add, t, xtok[j])
                then(j, last[j % 2])

        ar = Arena(0)
        ost = Stats([ar(512), ar(512)], ar(512))
        F = [PE.last()]
        ar = Arena(nsa_at + 8192)
        ptm = ar
        nst = Stats([ar(512), ar(512)], ar(512))
        OT = MG3
        otok = []
        ost.last = [F, F]
        AC.wait(F)
        GP.wait(F)
        for j in range(8):
            b, t = proj("out2", j, AX_, mt)
            free[b] = acopy(OT[:, j, :], PS[:, b, :], t, mt[7])
            otok.append(free[b])
            ost.add(OT[:, j, :], free[b])
        out2_done = last_unit[0]
        htok = []
        def then2(j, t):
            htok.append(operand(j, XT[:, j, :], col("fpre2", j), HX, t, pn_done))
            nst.add(XT[:, j, :], t)
            xtok[j] = t

        post("post2", OT, ost, ptm, then2)
        hooks.append(lambda: rms(nst, None, DV.last(), GP.last()))
        ar = Arena(0)
        OT = ar(4096).rearrange("p (j t) -> p j t", j=8)
        fst = Stats([ar(512), ar(512)], ar(512))

        def end2(j, t, up_done):
            fst.add(OT[:, j, :], t)

        ffn("2", HX, AX_, htok, ar, OT, [None] * 8, False, out2_done, end2)

        def store(j, t):
            q, e = ((SP, nc.sync), (AC, nc.scalar))[j % 2]
            store.t.append(q.dma(lambda: e.dma_start(out_d[:, j, :], XT[:, j, :]), d_out[j % 2], t))

        store.t = []
        post("fpost2", OT, fst, ar, store)
        SP.wait(store.t[-2], store.t[-1])

        assert len(used) == len(order)
        block = ctx.enter_context(nc.Block())

        @block.sync
        def _(eng):
            SP.replay(eng)

        @block.scalar
        def _(eng):
            AC.replay(eng)

        @block.gpsimd
        def _(eng):
            GP.replay(eng)

        @block.vector
        def _(eng):
            DV.replay(eng)

        @block.tensor
        def _(eng):
            PE.replay(eng)


def constant_tables():
    con = np.zeros((128, NCON), np.float32)
    p = np.arange(128)
    con[:, CON["ident"]:CON["ident"] + 128] = np.eye(128)
    con[:, CON["big"]:CON["big"] + 128] = np.where(p[None, :] < p[:, None], 1e30, 0.0)
    con[:, CON["mean"]:CON["mean"] + 128] = 1.0 / 1024
    for h in range(4):
        con[h, CON["sel"] + 128 * h:CON["sel"] + 128 * h + 128] = 1.0
    dist = 384 + p[:, None] - np.arange(512)[None, :]
    con[:, CON["ba"]:CON["ba"] + 512] = np.where(dist >= 0, -dist, NEG)
    end = 16 * np.arange(31) + 31
    for n in range(4):
        t = 128 * n + p[:, None]
        ok = end[None, :] <= t
        con[:, CON["bc"] + 31 * n:CON["bc"] + 31 * n + 31] = np.where(ok, -(t - end[None, :]), NEG)
        con[:, CON["m01"] + 31 * n:CON["m01"] + 31 * n + 31] = ok
    con[:, CON["glam"]:CON["glam"] + 64] = (p[:, None] % 64) <= np.arange(64)[None, :]
    oh = np.zeros((33, 3, 640), np.float32)
    for g, (win, dil) in enumerate(((128, 1), (512, 4), (2048, 16))):
        for i in range(640):
            d = i - 127
            if d < 0 or d > win or d % dil:
                oh[32, g, i] = 1.0
                continue
            if d < 16:
                bkt = d
            else:
                bkt = min(31, 16 + int(np.float32(np.log(np.float32(d) / np.float32(16)) / np.float32(np.log(128.0))
                                                  * np.float32(16))))
            oh[bkt, g, i] = 1.0
    return con, oh.reshape(33, 1920)


def pack_units(inputs):
    w_in, w_in2 = inputs["w_in"][0], inputs["w_in_2"][0]
    pts = np.cumsum([0, 1024, 1024, 1024, 8, 1024, 1536, 1536, 1536, 1024, 1024])
    names = ["qm", "km", "vm", "if_", "om", "qa", "ka", "va", "ga", "gb"]
    m = {n: w_in[:, pts[i]:pts[i + 1]] for i, n in enumerate(names)}
    z = np.zeros((1024, 128), np.float32)
    z[:, 0:4] = m["if_"][:, 0:4]
    z[:, 32:36] = m["if_"][:, 4:8]
    m["if"] = z
    pts = np.cumsum([0, 512, 512, 1024, 1024, 16, 512, 128, 128, 128, 128, 128, 128, 24, 1024, 1024])
    names = ["gq", "gk", "gv", "gr", "al", "nq_", "kc", "vc", "ks", "vs", "kw", "vw", "gt", "mg", "mn"]
    m.update({n: w_in2[:, pts[i]:pts[i + 1]] for i, n in enumerate(names)})
    z = np.zeros((1024, 128), np.float32)
    z[:, 0:16] = m["al"]
    z[:, 32:56] = m["gt"]
    m["small2"] = z
    q = m["nq_"].reshape(1024, 2, 4, 64)
    m["nq"] = np.ascontiguousarray(q.transpose(0, 2, 1, 3)).reshape(1024, 512)
    m.update({"pa": inputs["w_proj_a"][0], "pb": inputs["w_proj_b"][0], "out": inputs["w_out"][0],
              "gate": inputs["w_gate"][0], "up": inputs["w_up"][0], "down": inputs["w_down"][0],
              "pg": inputs["w_proj_gla_2"][0], "pn": inputs["w_proj_nsa_2"][0], "out2": inputs["w_out_2"][0],
              "gate2": inputs["w_ffn_gate_2"][0], "up2": inputs["w_ffn_up_2"][0], "down2": inputs["w_ffn_down_2"][0]})
    order = unit_order()
    w = np.zeros((len(order), 128, 1024), np.float32)
    for n, k in (("w1k", "nsa_cmp_w1_k_2"), ("w1v", "nsa_cmp_w1_v_2")):
        x = inputs[k][0].reshape(32, 64, 64).transpose(1, 0, 2)
        bd = np.zeros((128, 32, 128), np.float32)
        bd[0:64, :, 0:64] = x
        bd[64:128, :, 64:128] = x
        m[n] = bd
    for i, (name, j, k0, nk) in enumerate(order):
        if name in ("w1k", "w1v"):
            w[i] = m[name][:, 8 * j:8 * j + 8, :].reshape(128, 1024)
            continue
        blk = m[name][k0 * 128:(k0 + nk) * 128, j * 128:(j + 1) * 128]
        w[i, :, 0:nk * 128] = blk.reshape(nk, 128, 128).transpose(1, 0, 2).reshape(128, nk * 128)
    return w


def pack_cols(inputs):
    c = np.zeros((128, NCOL), np.float32)

    def put(name, vec):
        v = vec.reshape(-1, 128).T
        c[:, COLS[name]:COLS[name] + v.shape[1]] = v

    put("mix_g", inputs["norm_mix_g"][0])
    cw = inputs["conv_w"][0]
    c[:, COLS["conv_w"]:COLS["conv_w"] + 64] = cw.reshape(4, 16, 128).transpose(2, 1, 0).reshape(128, 64)
    put("conv_b", inputs["conv_b"][0])
    put("mnorm", inputs["mlstm_norm_g"][0])
    put("ffn_g", inputs["norm_ffn_g"][0])
    put("final_g", inputs["norm_final_g"])
    put("pre2", inputs["norm_mix_pre_2"][0])
    put("post2", inputs["norm_mix_post_2"][0])
    put("fpre2", inputs["norm_ffn_pre_2"][0])
    put("fpost2", inputs["norm_ffn_post_2"][0])
    put("balpha", inputs["gla_b_alpha_2"][0])
    put("glag", inputs["gla_norm_g_2"][0])
    b = inputs["b_gate_if"][0]
    c[0:4, COLS["bif"]] = b[0:4]
    c[0:4, COLS["bif"] + 1] = b[4:8]
    c[:, COLS["eps"]] = EPS
    c[:, COLS["one"]] = 1.0
    c[:, COLS["nhalf"]:COLS["nhalf"] + 4] = -0.5
    for n, k in (("pek", "nsa_cmp_pe_k_2"), ("pev", "nsa_cmp_pe_v_2")):
        pe = inputs[k][0].T
        c[0:64, COLS[n]:COLS[n] + 32] = pe
        c[64:128, COLS[n]:COLS[n] + 32] = pe
    return c


def kernel(**inputs):
    import concourse.bacc as bacc
    from concourse.bass_utils import run_bass_kernel_spmd

    inputs = {k: np.asarray(v) for k, v in inputs.items()}
    con, oh = constant_tables()
    x = inputs["x"][0]
    arrays = {
        "xT": np.ascontiguousarray(x.T.reshape(8, 128, 512).transpose(1, 0, 2)),
        "wst": pack_units(inputs),
        "con": con,
        "col": pack_cols(inputs),
        "relb": np.ascontiguousarray(inputs["rel_bias"]),
        "oh": oh,
        "wa2": np.ascontiguousarray(inputs["gla_w_alpha2_2"][0]),
    }
    w2 = np.zeros((128, 256), np.float32)
    for i, k in enumerate(("nsa_cmp_w2_k_2", "nsa_cmp_w2_v_2")):
        w2[0:64, 128 * i:128 * i + 64] = inputs[k][0]
        w2[64:128, 128 * i + 64:128 * i + 128] = inputs[k][0]
    arrays["w2"] = w2

    nc = bacc.Bacc("TRN2", target_bir_lowering=False, num_devices=1)
    f32 = mybir.dt.float32
    aps = [nc.dram_tensor(n, arrays[n].shape, f32, kind="ExternalInput").ap()
           for n in ("xT", "wst", "con", "col", "relb", "oh", "wa2", "w2")]
    out = nc.dram_tensor("out", (128, 8, 512), f32, kind="ExternalOutput").ap()
    scr = nc.dram_tensor("scr", (3, 24, 640), f32, kind="Internal").ap()
    build(nc, *aps, out, scr)
    r = run_bass_kernel_spmd(nc, [arrays], core_ids=[0])
    y = r.results[0]["out"]
    return np.ascontiguousarray(y.transpose(1, 0, 2).reshape(1024, 512).T)[None]
```

```python
import numpy as np
import concourse.bass as bass
from concourse import mybir
from contextlib import ExitStack

D = 1024
S = 512
DFF = 2816
NR = 3
NW = 3
FFN_PARTS = [(0, 8), (8, 16), (16, 22)]
EPS = 1e-6
NEG = -1e30

COLS = {}
_at = 0
for _name, _n in [("mix_g", 8), ("conv_w", 64), ("conv_b", 16), ("mnorm", 8), ("ffn_g", 8), ("final_g", 8),
                  ("pre2", 8), ("post2", 8), ("fpre2", 8), ("fpost2", 8), ("balpha", 4), ("glag", 2),
                  ("bif", 2), ("eps", 1), ("one", 1), ("nhalf", 4), ("pek", 32), ("pev", 32)]:
    COLS[_name] = _at
    _at += _n
NCOL = _at

CON = {}
_at = 0
for _name, _n in [("ident", 128), ("big", 128), ("mean", 128), ("sel", 512), ("ba", 512), ("bc", 124),
                  ("m01", 124), ("glam", 128)]:
    CON[_name] = _at
    _at += _n
NCON = _at


def unit_order():
    u = []

    def add(name, j, k0=0, k=8):
        u.append((name, j, k0, k))

    def ffn(sfx):
        for a, b in FFN_PARTS:
            for t in range(a, b):
                add("gate" + sfx, t)
                add("up" + sfx, t)
            for j in range(8):
                add("down" + sfx, j, a, b - a)

    def head(h, between):
        own = [("qm", 0), ("qm", 1), ("vm", 0), ("km", 0), ("km", 1), ("vm", 1)]
        for i, (n, j) in enumerate(own):
            add(n, 2 * h + j)
            if i in between:
                u.append(between[i])

    def pair(hp):
        for g in range(3):
            for n in ("qa", "ka", "va"):
                add(n, 4 * g + hp)

    head(0, {1: ("if", 0, 0, 8)})
    for h in range(3):
        head(h + 1, {0: ("om", 2 * h, 0, 8), 3: ("om", 2 * h + 1, 0, 8)})
    add("om", 6)
    add("om", 7)
    pair(0)
    for j in range(8):
        add("ga", j)
        add("pa", j)
    for hp in range(3):
        pair(hp + 1)
    for j in range(8):
        add("gb", j)
    for j in range(8):
        add("pb", j, 0, 4)
    for j in range(8):
        add("out", j)
    ffn("")

    add("small2", 0)
    for h in range(4):
        g = [("gv", 2 * h), ("gv", 2 * h + 1), ("gq", h), ("gk", h)]
        if h == 0:
            g[2:2] = [("gr", 0), ("gr", 1)]
        if h > 1:
            g[0:0] = [("gr", 2 * h - 2), ("gr", 2 * h - 1)]
        for n, j in g:
            add(n, j)
    add("gr", 6)
    add("gr", 7)
    for n in ("kc", "vc", "w1k", "nq", "w1v", "ks", "kw", "vs", "vw"):
        for i in range(4 if n in ("nq", "w1k", "w1v") else 1):
            add(n, i)
    for j in range(8):
        add("mg", j)
        add("pg", j)
        add("mn", j)
    for j in range(8):
        add("pn", j, 0, 4)
    for j in range(8):
        add("out2", j)
    ffn("2")
    return u


BUSY_DVE = ("qm", "km", "vm", "om", "qa", "ka", "va", "gb", "nq", "kc", "vc", "ks", "vs",
            "kw", "vw", "mg", "pg", "mn", "pb", "pn")


class Queue:

    def __init__(self, sem):
        self.sem, self.n, self.items, self.seen = sem, 0, [], {}

    def wait(self, *tokens):
        for t in tokens:
            if t is None:
                continue
            if isinstance(t, list):
                self.wait(*t)
                continue
            sem, v = t
            if self.seen.get(id(sem), 0) < v:
                self.seen[id(sem)] = v
                self.items.append((None, sem, v))

    def op(self, fn, *tokens):
        self.wait(*tokens)
        self.n += 1
        self.items.append((fn, self.sem, 1))
        return (self.sem, self.n)

    def quiet(self, fn, *tokens):
        self.wait(*tokens)
        self.items.append((fn, None, 0))

    def dma(self, fn, chan, *tokens):
        self.wait(*tokens)
        chan[1] += 16
        self.items.append((fn, chan[0], 16))
        return (chan[0], chan[1])

    def last(self):
        return (self.sem, self.n) if self.n else None

    def replay(self, eng):
        for fn, sem, v in self.items:
            if fn is None:
                eng.wait_ge(sem, v)
            elif sem is None:
                fn()
            else:
                fn().then_inc(sem, v)


def build(nc, xT_d, wst_d, con_d, col_d, relb_d, oh_d, wa2_d, w2_d, out_d, scr_d):
    f32 = mybir.dt.float32
    r32 = mybir.dt.float32r
    i32 = mybir.dt.int32
    ALU = mybir.AluOpType
    ACT = mybir.ActivationFunctionType
    AX = mybir.AxisListType.X
    ctx = ExitStack()
    with ctx:
        def sb(name, shape, dt=f32):
            return ctx.enter_context(nc.sbuf_tensor(name, shape, dt))

        def sem(name):
            return ctx.enter_context(nc.semaphore(name))

        ARN = 20288
        XT = sb("XT", [128, 8, 512])
        HH = sb("HH", [128, 8, 512], r32)
        HL = sb("HL", [128, 8, 512], r32)
        AH = sb("AH", [128, 8, 512], r32)
        AL = sb("AL", [128, 8, 512], r32)
        RAW = sb("RAW", [128, NR, 1024])
        WH = sb("WH", [128, NW, 1024], r32)
        WL = sb("WL", [128, NW, 1024], r32)
        C = sb("C", [128, NCON])
        COL = sb("COL", [128, NCOL])
        AR = sb("AR", [128, ARN])
        PS = ctx.enter_context(nc.psum_tensor("PS", [128, 8, 512], f32))

        PE = Queue(sem("s_pe"))
        AC = Queue(sem("s_act"))
        DV = Queue(sem("s_dve"))
        GP = Queue(sem("s_pool"))
        SP = Queue(sem("s_sp"))
        s_raw = [[sem(f"s_raw{i}"), 0] for i in range(NR)]
        d_con = [sem("d_con"), 0]
        d_x = [[sem(f"d_x{i}"), 0] for i in range(8)]
        d_col = [sem("d_col"), 0]
        d_vec = [sem("d_vec"), 0]
        d_bias = [[sem(f"d_bias{i}"), 0] for i in range(2)]
        d_b2 = [sem("d_b2"), 0]
        d_w2 = [sem("d_w2"), 0]
        d_out = [[sem(f"d_out{i}"), 0] for i in range(2)]
        V, A, T, G = nc.vector, nc.scalar, nc.tensor, nc.gpsimd
        RB = sb("RB", [128, 512])[:, :]
        VT = sb("VT", [128, 512])
        GT = sb("GT", [128, 96])
        RC = sb("RC", [128, 16])
        HX, AX_ = (HH, HL), (AH, AL)

        def f(ap):
            return ap.bitcast(f32)

        def col(name, j=0, p0=0, p1=128, n=1):
            return COL[p0:p1, COLS[name] + j:COLS[name] + j + n]

        def con(name, a=0, b=None, p0=0, p1=128):
            n = {"ident": 128, "big": 128, "mean": 128, "sel": 512, "ba": 512, "bc": 124, "m01": 124, "glam": 128}[name]
            return C[p0:p1, CON[name] + a:CON[name] + (n if b is None else b)]

        class Arena:
            def __init__(self, at):
                self.at = at

            def __call__(self, n):
                o = self.at
                self.at += n
                assert self.at <= ARN, self.at
                return AR[:, o:o + n]

        def ident(n=128):
            return con("ident", 0, n, 0, n)

        def act(out, in_, func, *tok, **kw):
            return AC.op(lambda: A.activation(out, in_, func, **kw), *tok)

        def acopy(out, in_, *tok, scale=1.0):
            return AC.op(lambda: A.activation(out, in_, ACT.Copy, scale=scale), *tok)

        def tt(out, a, b, op, *tok):
            return DV.op(lambda: V.tensor_tensor(out, a, b, op), *tok)

        def ts(out, a, s1, s2, op0, op1, *tok):
            return DV.op(lambda: V.tensor_scalar(out, a, s1, s2, op0, op1), *tok)

        def stt(out, a, s, b, op0, op1, *tok):
            return DV.op(lambda: V.scalar_tensor_tensor(out=out, in0=a, scalar=s, in1=b, op0=op0, op1=op1), *tok)

        def ptt(out, a, b, op, *tok):
            return GP.op(lambda: G.tensor_tensor(out, a, b, op), *tok)

        def vcopy(out, in_, *tok):
            return DV.op(lambda: V.tensor_copy(out, in_), *tok)

        def mm(out, l, r, start, stop, *tok, inc=False):
            fn = lambda: T.matmul(out, l, r, start=start, stop=stop)
            return PE.op(fn, *tok) if inc else PE.quiet(fn, *tok)

        def tp(out, in_, idn, *tok, inc=False):
            fn = lambda: T.transpose(out, in_, idn)
            return PE.op(fn, *tok) if inc else PE.quiet(fn, *tok)

        free = [None] * 8

        class Ring:
            def __init__(self, banks):
                self.banks, self.i = banks, 0

            def take(self):
                b = self.banks[self.i % len(self.banks)]
                self.i += 1
                return b, free[b]

        PR = Ring([0, 1])
        TR = Ring([5, 6])
        SB = [2, 3, 4]
        OB = 7

        order = unit_order()
        loaded, split_done, used = [], [], {}
        started = [0]

        def raw_unit(i):
            return order[i][0] in ("w1k", "w1v")

        def load_more(most=1000):
            while len(loaded) < len(order) and most > 0:
                most -= 1
                i = len(loaded)
                if i < NR:
                    waits = []
                elif raw_unit(i - NR):
                    if i - NR not in used:
                        return
                    waits = [used[i - NR]]
                elif i - NR < len(split_done):
                    waits = split_done[i - NR]
                else:
                    return
                k = order[i][3]
                loaded.append(SP.dma(lambda i=i, k=k: nc.sync.dma_start(RAW[:, i % NR, 0:k * 128],
                                                                        wst_d[i, :, 0:k * 128]),
                                     s_raw[i % NR], *waits))

        def split_next():
            i = len(split_done)
            if i >= len(order):
                return
            if raw_unit(i):
                split_done.append([loaded[i]])
                return
            k = order[i][3]
            raw, hi, lo = RAW[:, i % NR, 0:k * 128], WH[:, i % NW, 0:k * 128], WL[:, i % NW, 0:k * 128]
            gone = used.get(i - NW)
            th = acopy(hi, raw, loaded[i], gone)
            low = ptt if i % 2 and order[i][0] in BUSY_DVE else tt
            tl = low(lo, raw, f(hi), ALU.subtract, loaded[i], th, gone)
            split_done.append([th, tl])
            load_more()

        def open_unit(key):
            i = started[0]
            started[0] += 1
            assert order[i] == key, (order[i], key)
            while len(split_done) < min(i + NW, len(order)) and len(split_done) - NW < len(used):
                split_next()
            return i

        class Filler:

            def __init__(self, gens, points):
                self.gens, self.total, self.points = list(gens), 4 * len(gens), points
                self.acc = self.done = 0

            def step(self):
                while self.gens:
                    try:
                        next(self.gens[0])
                        return
                    except StopIteration:
                        self.gens.pop(0)

            def __call__(self, w=1):
                self.acc += w * self.total / self.points
                while self.done < int(self.acc + 1e-6):
                    self.step()
                    self.done += 1

            def drain(self, pend=True):
                while self.gens:
                    self.step()
                if pend:
                    flush(True)

        last_unit = [None]
        pending = []
        hooks = []

        def flush(all_=False):
            n = len(pending)
            for _ in range(n):
                pending.pop(0)()
            if all_ and pending:
                flush(True)

        def together(*gens):
            gens = list(gens)
            while gens:
                for g in list(gens):
                    try:
                        next(g)
                    except StopIteration:
                        gens.remove(g)

        def behind_norm(a, b, c, squares=None):
            for _ in range(4):
                if squares:
                    next(squares, None)
                next(a)
                next(b)
            next(c)
            next(c)
            hooks.pop(0)()
            run(a)
            flush(True)
            run(b)
            run(c)

        def run(gen):
            try:
                while True:
                    next(gen)
            except StopIteration as e:
                return e.value

        def proj(*a):
            return run(gproj(*a))

        def gproj(name, j, X, xtok, k0=0, nk=8):
            i = open_unit((name, j, k0, nk))
            b, fr = PR.take()
            XH, XL = X
            PE.wait(fr, split_done[i])
            t = None
            for k in range(nk):
                if k == nk - 2 and len(hooks) == 2:
                    hooks.pop(0)()
                wh, wl = WH[:, i % NW, k * 128:(k + 1) * 128], WL[:, i % NW, k * 128:(k + 1) * 128]
                mm(PS[:, b, :], wh, XH[:, k, :], k == 0, False, xtok[k])
                mm(PS[:, b, :], wh, XL[:, k, :], False, False)
                t = mm(PS[:, b, :], wl, XH[:, k, :], False, k == nk - 1, inc=(k == nk - 1))
                if k % 2 and k < nk - 1:
                    if k == nk // 2 - 1:
                        flush()
                    yield
            used[i] = t
            last_unit[0] = t
            flush()
            if hooks:
                yield
            return b, t

        def split_from(bank_or_sb, XH, XL, j, *tok):
            th = acopy(XH[:, j, :], bank_or_sb, *tok)
            tl = tt(XL[:, j, :], bank_or_sb, f(XH[:, j, :]), ALU.subtract, th, *tok)
            return [th, tl]

        s_col = AC.dma(lambda: nc.scalar.dma_start(COL[:, :], col_d), d_col)
        xtok = []
        for j, n in ((0, 1), (1, 1), (2, 2), (4, 2), (6, 2)):
            t = SP.dma(lambda j=j, n=n: nc.sync.dma_start(XT[:, j:j + n, :], xT_d[:, j:j + n, :]), d_x[len(xtok)])
            xtok += [t] * n
            if j < 4:
                load_more(1)
        s_c = SP.dma(lambda: nc.sync.dma_start(C[:, :], con_d), d_con)
        tab, oh, vecs = AR[:, 0:24], AR[:, 24:1944], AR[:, 1944:3864]
        t_oh = SP.dma(lambda: nc.sync.dma_start(tab[0:32, :], relb_d), d_vec)
        t_oh = SP.dma(lambda: nc.sync.dma_start(oh[0:33, :], oh_d), d_vec)

        def fence():
            F = [PE.last(), AC.last(), DV.last(), GP.last()]
            GP.wait(*F)
            AC.wait(*F)
            DV.wait(*F)
            return F

        class Stats:

            def __init__(self, sq, acc):
                self.sq, self.acc, self.n, self.last, self.t, self.rest = sq, acc, 0, [None, None], None, None

            def add(self, src, *tok, scale=1.0):
                q = self.n % 2
                dst = self.acc if self.n == 0 else self.sq[q]
                t1 = act(dst, src, ACT.Square, *tok, self.last[q], scale=scale)
                if self.n == 7:
                    self.rest = (dst, t1)
                else:
                    self.t = t1 if self.n == 0 else ptt(self.acc, self.acc, dst, ALU.add, t1, self.t)
                    self.last[q] = None if self.n == 0 else self.t
                self.n += 1
                return t1

            def fold(self):
                b, fr = TR.take()
                for m, (src, tk) in enumerate(((self.acc, self.t), self.rest)):
                    for q in range(4):
                        t = mm(PS[:, b, q:q + 1], src[:, q * 128:(q + 1) * 128], con("mean", 0, 1), m + q == 0,
                               m + q == 4, tk, fr, s_c, inc=(m + q == 4))
                return b, t

        RBT = [None]

        def broadcast(dst, c, *tok, gone=None):
            b, fr = TR.take()
            for q in range(4):
                x = c[:, q:q + 1]
                x = bass.AP(x.tensor, x.offset, [list(x.ap[0]), [0, 128]])
                t = mm(PS[:, b, q * 128:(q + 1) * 128], x, ident(), True, True, *tok, fr, s_c, inc=(q == 3))
            if dst is None:
                return b, t
            free[b] = acopy(dst, PS[:, b, :], t, gone)
            return free[b]

        def inverse_root(c, src, *tok):
            t = ts(c, src, EPS, None, ALU.add, ALU.bypass, *tok)
            return t, ptt(c, c, col("nhalf", 0, n=4), ALU.pow, t)

        def norm_hooks(stats, *gone):
            tr = [None]

            def one():
                b, tm = stats.fold()
                free[b], tr[0] = inverse_root(RC[:, 0:4], PS[:, b, 0:4], tm, PE.last())

            def two():
                RBT[0] = broadcast(RB, RC[:, 0:4], tr[0], gone=[DV.last(), GP.last()])
            return [one, two]

        def power(dst, src, scale, *tok, n=1):
            t = GP.op(lambda: G.tensor_scalar(dst, src, scale, EPS, ALU.mult, ALU.add), *tok)
            return ptt(dst, dst, col("nhalf", 0, n=n), ALU.pow, t)

        def scaled(dst, b, t, *tok, p0=0, p1=128, scale=None):
            if scale is None:
                return tt(dst, PS[p0:p1, b, :], RB[p0:p1, :], ALU.mult, t, RBT[0], *tok)
            return stt(dst, PS[p0:p1, b, :], scale, RB[p0:p1, :], ALU.mult, ALU.mult, t, RBT[0], *tok)

        def operand(j, src, g, X, *tok):
            th = act(X[0][:, j, :], src, ACT.Copy, *tok, scale=g)
            tl = stt(X[1][:, j, :], src, g, f(X[0][:, j, :]), ALU.mult, ALU.subtract, th, *tok)
            return [th, tl]

        st0 = Stats([AR[:, 14336:14848], AR[:, 14848:15360]], AR[:, 15360:15872])
        GG = COL[:, COLS["pre2"]:COLS["pre2"] + 8]
        AC.wait(s_col)
        DV.wait(s_col)
        GP.wait(s_col)
        tgg = tt(GG, COL[:, COLS["final_g"]:COLS["final_g"] + 8], COL[:, COLS["pre2"]:COLS["pre2"] + 8], ALU.mult)
        htok = []
        for j in range(8):
            htok.append(operand(j, XT[:, j, :], col("mix_g", j), HX, xtok[j]))
            st0.add(XT[:, j, :], xtok[j])
            if j in (1, 3):
                split_next()
        AC.wait(s_c)
        DV.wait(s_c)
        hooks.extend(norm_hooks(st0))
        SLOT = [AR[:, 4608 * i:4608 * (i + 1)] for i in range(2)]
        ar = Arena(4608)
        hq = [ar(1024), ar(1024)]
        hk = [ar(1024), ar(1024)]
        hv = [ar(1028), ar(1028)]
        so = ar(1024)
        xc = ar(516)
        yc = ar(512)
        th_ = ar(512)
        Mb = ar(512)
        Md = ar(128)
        Et = [ar(512), ar(512)]
        WT = ar(1280)
        hm = ar(1024)
        yf = ar(512)
        acol, ecol = ar(16), ar(16)
        stat = ar(64)
        g4 = [ar(512) for _ in range(4)]

        xc_zero = DV.op(lambda: V.memset(xc[:, 0:4], 0.0))
        mq = {}
        last_att = {-2: None, -1: None}
        conv_free = [None, None]

        def conv(name, h, j):
            b, t = yield from gproj(name, 2 * h + j, HX, htok)
            c = (0 if name == "qm" else 8) + 2 * h + j
            dst = (hq if name == "qm" else hk)[h % 2][:, j * 512:(j + 1) * 512]
            t1 = scaled(xc[:, 4:516], b, t, conv_free[0])
            free[b] = t1
            t3 = ts(yc, xc[:, 1:513], col("conv_w", 4 * c), col("conv_b", c), ALU.mult, ALU.add, t1, xc_zero,
                    conv_free[1])
            for q in range(1, 4):
                t3 = stt(yc, xc[:, 1 + q:513 + q], col("conv_w", 4 * c + q), yc, ALU.mult, ALU.add, t3)
            conv_free[0] = t3
            def silu():
                t4 = act(th_, yc, ACT.Tanh, t3, conv_free[1], scale=0.5)

                def end():
                    mq[(h, name, j)] = conv_free[1] = stt(dst, th_, 1.0, yc, ALU.add, ALU.mult, t4,
                                                          last_att.get(h - 2))
                pending.append(end)
            pending.append(silu)
            yield

        vt_free = [None]

        def to_tokens(src, dst3, tsrc, *tok):
            b, fr = TR.take()
            for t_ in range(4):
                x = tp(PS[:, b, t_ * 128:(t_ + 1) * 128], src[:, t_ * 128:(t_ + 1) * 128], ident(), tsrc, fr,
                       inc=(t_ == 3))
            free[b] = vcopy(dst3, PS[:, b, :].rearrange("p (t e) -> p t e", t=4), x, *tok)
            return x, free[b]

        def vproj(h, j):
            b, t = yield from gproj("vm", 2 * h + j, HX, htok)
            t1 = scaled(yf, b, t, vt_free[0])
            free[b] = t1

            def end():
                x, y = to_tokens(yf, hv[h % 2].rearrange("p (t e) -> p t e", t=4)[:, :, j * 128:(j + 1) * 128], t1,
                                 last_att.get(h - 2))
                vt_free[0] = x
                mq[(h, "vm", j)] = y
            pending.append(end)
            yield

        def sig_tile(done, dst, b, t, *tok):
            t0 = scaled(dst, b, t, *tok)
            free[b] = t0
            t1 = act(dst, dst, ACT.Tanh, t0, scale=0.5)
            pending.append(lambda: done(ts(dst, dst, 0.5, 0.5, ALU.mult, ALU.add, t1)))

        so_free = [None, None]

        def oproj(h, j):
            b, t = yield from gproj("om", 2 * h + j, HX, htok)
            sig_tile(lambda x: mq.update({(h, "om", j): x}), so[:, j * 512:(j + 1) * 512], b, t, so_free[j])
            yield

        def head_units(h):
            return [conv("qm", h, 0), conv("qm", h, 1), vproj(h, 0), conv("km", h, 0), conv("km", h, 1), vproj(h, 1)]

        pair_tok = {}
        pair_last = {}
        pv_free = [None]
        ptmp = xc[:, 0:512]

        def pair_units(hp, tmp, tmpfree):
            sl = SLOT[hp % 2]

            def one(g, kind):
                b, t = yield from gproj(("qa", "ka", "va")[kind], 4 * g + hp, HX, htok)
                o = (3 * g + kind) * 512
                gone = pair_last.get(hp - 2)
                if kind < 2:
                    tk = scaled(sl[:, o:o + 512], b, t, gone, scale=0.125 if kind == 0 else None)
                    free[b] = tk
                else:
                    t1 = scaled(tmp, b, t, tmpfree[0])
                    free[b] = t1

                    def end():
                        x, tk = to_tokens(tmp, sl[:, o:o + 512].rearrange("p (t e) -> p t e", t=4), t1, gone)
                        tmpfree[0] = x
                        pair_tok[hp].append(tk)
                    pending.append(end)
                if kind < 2:
                    pair_tok.setdefault(hp, []).append(tk)
                yield
            return [one(g, k) for g in range(3) for k in range(3)]

        hu = head_units(0)
        PR.banks = [0, 1, 2, 3]
        if_ = []

        def if_unit():
            if_.extend((yield from gproj("if", 0, HX, htok)))

        behind_norm(hu[0], hu[1], if_unit())
        r = [x[0:4, :] for x in g4]
        gtk = {}

        def gates(b, t):
            t1 = scaled(r[0], b, t, p0=0, p1=4)
            t2 = scaled(r[1], b, t, p0=32, p1=36)
            free[b] = t2
            t1 = ts(r[0], r[0], col("bif", 0, 0, 4), None, ALU.add, ALU.bypass, t1)
            t2 = ts(r[1], r[1], col("bif", 1, 0, 4), None, ALU.add, ALU.bypass, t2)
            t3 = stt(r[2], r[1], -1.0, r[1], ALU.mult, ALU.max, t2)
            t4 = act(r[2], r[2], ACT.Exp, t3, scale=-1.0)
            t5 = act(r[2], r[2], ACT.Ln, t4, bias=col("one", 0, 0, 4))
            t7 = DV.op(lambda: V.memset(r[3], 1.0))
            yield
            yield
            yield
            t6 = stt(r[1], r[1], 0.0, r[2], ALU.min, ALU.subtract, t5, t2)
            t8 = DV.op(lambda: V.tensor_tensor_scan(r[2], r[3], r[1], 0.0, ALU.mult, ALU.add), t6, t7)
            gtk["a"] = tt(r[0], r[0], r[2], ALU.subtract, t8)
            gtk["M"] = DV.op(lambda: V.tensor_tensor_scan(r[1], r[3], r[0], 0.0, ALU.mult, ALU.max), gtk["a"])
            t11 = tt(r[2], r[2], r[1], ALU.add, gtk["M"])
            gtk["e"] = act(r[2], r[2], ACT.Exp, t11, scale=-1.0)

        ya_tok = [None] * 8
        tone = [DV.op(lambda i=i: V.memset(hv[i][:, :].rearrange("p (t e) -> p t e", t=4)[:, :, 256:257], 1.0))
                for i in range(2)][-1]

        together(hu[2], gates(*if_))
        t1 = DV.op(lambda: V.memset(tab[32:33, :], NEG))
        for g in range(3):
            run(hu[3 + g])
            for a, n in ((0, 512), (512, 128)):
                b, fr = TR.take()
                tm = mm(PS[0:24, b, 0:n], tab[0:33, :], oh[0:33, g * 640 + a:g * 640 + a + n], True, True,
                        t_oh, t1, fr, inc=True)
                free[b] = tv = acopy(vecs[0:24, g * 640 + a:g * 640 + a + n], PS[0:24, b, 0:n], tm)
        tvec = SP.dma(lambda: nc.sync.dma_start(scr_d.rearrange("g h i -> h g i"),
                                                vecs[0:24, :].rearrange("p (g i) -> p g i", g=3)), d_vec, tv)
        t9, tM, t12 = gtk["a"], gtk["M"], gtk["e"]
        b, fr = TR.take()
        for s in range(4):
            tp(PS[:, b, 4 * s:4 * s + 4], r[0][:, s * 128:(s + 1) * 128], ident(4), t9, fr)
            tc = tp(PS[:, b, 16 + 4 * s:20 + 4 * s], r[2][:, s * 128:(s + 1) * 128], ident(4), t12, inc=(s == 3))
        tcol = vcopy(acol, PS[:, b, 0:16], tc)
        tcol = vcopy(ecol, PS[:, b, 16:32], tc)
        free[b] = tcol
        PR.banks = [0, 1]
        mb_free = [None]
        e_free = [None, None]
        wt_free = [None]
        hm_free = [None]
        ya, ya_free = [VT[:, :], hm[:, 0:512]], [None, None]
        for h in range(4):
            if h < 3:
                units = head_units(h + 1)
                units[1:1] = [oproj(h, 0)]
                units[5:5] = [oproj(h, 1)]
            else:
                units = [oproj(h, j) for j in (0, 1)] + pair_units(0, ptmp, conv_free)
            filler = Filler(units, 15)

            q, k, v = hq[h % 2], hk[h % 2], hv[h % 2]
            b, fr = TR.take()
            t = mm(PS[:, b, :], con("sel", 128 * h, 128 * h + 128, 0, 4), r[1], True, True, tM, fr, inc=True)
            tmb = acopy(Mb, PS[:, b, :], t, mb_free[0])
            free[b] = tmb
            filler()
            tw = []
            wo = [0, 512, 896, 1152]
            for s in range(4):
                n = 512 - 128 * s
                b = SB[s % 3]
                for c in (0, 1):
                    t = mm(PS[:, b, 0:n], k[:, c * 512 + s * 128:c * 512 + s * 128 + 128],
                           q[:, c * 512 + s * 128:c * 512 + 512], c == 0, c == 1,
                           mq[(h, "qm", c)], mq[(h, "km", c)], free[b], inc=(c == 1))
                E = Et[s % 2]
                t1 = tt(Md, Mb[:, s * 128:(s + 1) * 128], con("big"), ALU.add, tmb, e_free[0])
                t2 = act(E[:, 0:128], Md, ACT.Exp, t1, tcol, e_free[s % 2], scale=-1.0,
                         bias=acol[:, 4 * s + h:4 * s + h + 1])
                e_free[0] = t2 if s % 2 else e_free[0]
                md_free = t2
                if n > 128:
                    t2 = act(E[:, 128:n], Mb[:, (s + 1) * 128:512], ACT.Exp, tmb, scale=-1.0,
                             bias=acol[:, 4 * s + h:4 * s + h + 1])
                t3 = stt(WT[:, wo[s]:wo[s] + n], PS[:, b, 0:n], 1.0 / 64.0, E[:, 0:n], ALU.mult, ALU.mult, t, t2,
                         wt_free[0])
                e_free = [t3, t3]
                free[b] = t3
                tw.append(t3)
                filler()
                DV.wait(md_free)
            mb_free[0] = md_free if n <= 128 else t2
            mb_free[0] = AC.last()
            hv3 = v.rearrange("p (t e) -> p t e", t=4)
            hmt = []
            var = stat[:, 33:40:2]
            rs = stat[:, 40:44]

            def normed(i, tp_):
                hmv = hm[:, i * 256:(i + 1) * 256]
                return ts(hmv, hmv, stat[:, 32 + 2 * i:33 + 2 * i], rs[:, i:i + 1], ALU.subtract, ALU.mult, tp_)

            for t_ in range(4):
                b = (OB, SB[0], SB[1], SB[2])[t_]
                fr = free[b]
                for s in range(t_ + 1):
                    o = wo[s] + (t_ - s) * 128
                    t = mm(PS[:, b, 0:257], WT[:, o:o + 128], hv3[:, s, :], s == 0, s == t_, tw[s],
                           mq[(h, "vm", 0)], mq[(h, "vm", 1)], tone, fr, inc=(s == t_))
                d = stat[:, t_:t_ + 1]
                t1 = stt(d, PS[:, b, 256:257], -1.0, ecol[:, 4 * t_ + h:4 * t_ + h + 1], ALU.mult, ALU.max, t, tcol,
                         hm_free[0])
                t1 = tt(d, d, PS[:, b, 256:257], ALU.max, t1)
                t2 = DV.op(lambda d=d: V.reciprocal(d, d), t1)
                hmv = hm[:, t_ * 256:(t_ + 1) * 256]
                t3 = AC.op(lambda hmv=hmv, b=b, d=d: A.activation(hmv, PS[:, b, 0:256], ACT.Copy, scale=d),
                           t2, hm_free[0])
                free[b] = t3
                st6 = stat[:, 8 + 6 * t_:14 + 6 * t_]
                t4 = DV.op(lambda hmv=hmv, st6=st6: V.bn_stats(st6, hmv), t3)
                mv = stat[:, 32 + 2 * t_:34 + 2 * t_]
                t5 = DV.op(lambda mv=mv, st6=st6: V.bn_aggr(mv, st6), t4)
                hmt.append(t5)
                if t_ == 2:
                    t3p = power(rs[:, 0:3], var[:, 0:3], 1.0, hmt[2], n=3)
                if t_ == 3:
                    wt_free[0] = t
                    last_att[h] = t
                    for i in range(3):
                        normed(i, t3p)
                filler()
            t2 = normed(3, power(rs[:, 3:4], var[:, 3:4], 1.0, hmt[3]))
            filler(4)
            tb = []
            for j in (0, 1):
                b, fr = TR.take()
                for t_ in range(4):
                    t = tp(PS[:, b, t_ * 128:(t_ + 1) * 128], hm[:, t_ * 256 + j * 128:t_ * 256 + j * 128 + 128],
                           ident(), t2, fr, inc=(t_ == 3))
                tb.append((b, t))
            t3 = []
            for j, (b, t) in enumerate(tb):
                t3.append(stt(ya[j], PS[:, b, :], col("mnorm", 2 * h + j), so[:, j * 512:(j + 1) * 512], ALU.mult,
                              ALU.mult, t, mq[(h, "om", j)], ya_free[j]))
                free[b] = t3[j]
                so_free[j] = t3[j]
            filler()
            for j in (0, 1):
                ya_free[j] = ya_tok[2 * h + j] = split_from(ya[j], AH, AL, 2 * h + j, t3[j])
            hm_free[0] = ya_free[1]
            filler()
            filler.drain(h == 3)
        F = fence()
        SP.wait(*F)

        PR.banks = [0, 1, 2, 3]
        AC.wait(tvec)
        DV.wait(tvec)
        ar = Arena(9216)
        MG = ar(4096)
        MG3 = MG.rearrange("p (j t) -> p j t", j=8)
        BI = [ar(1280), ar(1280)]
        SS = [ar(1280), ar(1280)]
        PT = ar(1280)
        yb = ar(512)
        st = ar(32)

        bias_tok = {}
        bias_free = {-2: None, -1: None}

        def load_bias(h):
            t = BI[h % 2]
            SP.wait(bias_free[h - 2])
            for g in (1, 2):
                src = bass.AP(scr_d.tensor, scr_d.offset + (g * 24 + g * 8 + h) * 640, [[1, 128], [1, 512]])
                SP.dma(lambda g=g, src=src: nc.sync.dma_start(t[:, (g - 1) * 512:g * 512], src), d_bias[h % 2])
            src0 = bass.AP(scr_d.tensor, scr_d.offset + h * 640, [[1, 128], [1, 256]])
            bias_tok[h] = SP.dma(lambda: nc.sync.dma_start(t[:, 1024:1280], src0), d_bias[h % 2])

        load_bias(0)
        load_bias(1)

        def rev(ap, start, n, outer=None):
            dims = [list(ap.ap[0])] + ([list(outer)] if outer else []) + [[-1, n]]
            return bass.AP(ap.tensor, ap.offset + start, dims)

        sgt = SS[0][:, 0:512]
        sg_free = None
        mtok = []
        for j in range(8):
            b, t = proj("ga", j, HX, htok)
            st_ = []
            sig_tile(st_.append, sgt, b, t, sg_free)
            b, t = proj("pa", j, AX_, ya_tok)
            t2 = tt(MG3[:, j, :], sgt, PS[:, b, :], ALU.mult, t, st_)
            free[b] = t2
            sg_free = t2
            mtok.append(t2)
        PR.banks = [0, 1]
        ss_free = [sg_free, None]
        pt_free = [None]
        yb_free = [None]
        yb_tok = [None] * 4
        sc_free = [None, None]

        def att_a(it):
            hp, i, n = it
            h = 2 * hp + i
            par = ORD_N.index(n) % 2
            sl = SLOT[hp % 2]
            W = 128 * (n + 1)
            k0 = max(0, n - 1)
            W0 = 128 * (n + 1 - k0)
            p = slice(64 * i, 64 * i + 64)
            toks = []
            for g, bnk, ka, w in ((1, SB[0], 0, W), (2, SB[1], 0, W), (0, SB[2], k0 * 128, W0)):
                o = 3 * g * 512
                toks.append(mm(PS[:, bnk, 0:w], sl[p, o + n * 128:o + n * 128 + 128],
                               sl[p, o + 512 + ka:o + 512 + ka + w], True, True, pair_tok[hp], free[bnk], inc=True))
            return lambda: att_s(it, toks)

        def att_s(it, toks):
            hp, i, n = it
            h = 2 * hp + i
            par = ORD_N.index(n) % 2
            W = 128 * (n + 1)
            W0 = 128 * min(2, n + 1)
            Sx = SS[par]
            bi = BI[h % 2]
            t1 = tt(Sx[:, 0:2 * W].rearrange("p (g k) -> p g k", g=2), PS[:, SB[0]:SB[0] + 2, 0:W],
                    rev(bi, W - 1, W, (512, 2)), ALU.add, toks[1], bias_tok[h], ss_free[par])
            free[SB[0]] = free[SB[1]] = t1
            t2 = tt(Sx[:, 2 * W:2 * W + W0], PS[:, SB[2], 0:W0], rev(bi, 1024 + W0 - 1, W0), ALU.add, toks[2])
            free[SB[2]] = t2
            if n == LAST_N:
                bias_free[h] = t2
                if h + 2 < 8:
                    load_bias(h + 2)
            nm, l = st[:, par:par + 1], st[:, 2 + par:3 + par]
            N = 2 * W + W0
            t3 = DV.op(lambda: V.tensor_reduce(nm, Sx[:, 0:N], AX, ALU.max, negate=True), t1, t2, sc_free[par])
            t4 = AC.op(lambda: A.activation(Sx[:, 0:N], Sx[:, 0:N], ACT.Exp, bias=nm, accum_out=l), t3)
            return t4, (par, N, l)

        def transposes(Sx, nblk, tS, filler, first):
            out = []
            m = 0
            while m < nblk:
                if m == 8:
                    filler()
                c = min(4, nblk - m)
                b, fr = TR.take()
                for q in range(c):
                    t = tp(PS[:, b, q * 128:(q + 1) * 128], Sx[:, (m + q) * 128:(m + q + 1) * 128], ident(), tS, fr,
                           inc=(q == c - 1))
                e = acopy if (m // 4 + first) % 2 else vcopy
                free[b] = e(PT[:, m * 128:(m + c) * 128], PS[:, b, 0:c * 128], t, pt_free[0])
                out.append(free[b])
                m += c
            return t, out

        LAST_N = 2
        WORK = (1.3, 1.1, 0.9, 0.7)
        ORD_N = (0, 3, 1, 2)

        def att_b(it, tS, info, fill, softmax):
            hp, i, n = it
            par, N, l = info
            Sx = SS[par]
            sl = SLOT[hp % 2]
            nb = N // 128
            tl, ev = transposes(Sx, nb, tS, fill, 0)
            ss_free[par] = tl
            nxt = softmax() if softmax else None
            fill()
            keys = [(1, j) for j in range(n + 1)] + [(2, j) for j in range(n + 1)] + \
                   [(0, j) for j in range(max(0, n - 1), n + 1)]
            for m, (g, j) in enumerate(keys):
                o = (3 * g + 2) * 512 + j * 128 + 64 * i
                t = mm(PS[:, OB, 0:64], PT[:, m * 128:(m + 1) * 128], sl[:, o:o + 64], m == 0, m == nb - 1,
                       ev, pair_tok[hp], free[OB], inc=(m == nb - 1))
            pt_free[0] = t
            t1 = DV.op(lambda: V.reciprocal(l, l), tS)
            o = n * 128 + 64 * i
            t2 = ts(yb[:, o:o + 64], PS[:, OB, 0:64], l, None, ALU.mult, ALU.bypass, t, t1, yb_free[0])
            free[OB] = t2
            sc_free[par] = t2
            return t, t2, nxt

        def run_pair(hp, units):
            items = [(hp, i, n) for i in (0, 1) for n in ORD_N]
            fill = Filler(units, 26)
            nxt = att_a(items[0])()
            for m, it in enumerate(items):
                part = lambda w=WORK[it[2]]: fill(w)
                part()
                cur = nxt
                sm = att_a(items[m + 1]) if m + 1 < len(items) else None
                part()
                t, t2, nxt = att_b(it, *cur, part, sm)
            pair_last[hp] = t
            fill.drain(hp == 3)
            b, fr = TR.take()
            for n in range(4):
                t = tp(PS[:, b, n * 128:(n + 1) * 128], yb[:, n * 128:(n + 1) * 128], ident(), t2, fr, inc=(n == 3))
            yb_free[0] = t
            yb_tok[hp] = split_from(PS[:, b, :], AH, AL, hp, t, pa_done)
            free[b] = yb_tok[hp]

        pa_done = last_unit[0]
        vtmp_free = [None]
        for hp in range(3):
            run_pair(hp, pair_units(hp + 1, VT[:, :], vtmp_free))
        gb3 = SLOT[0][:, 0:4096].rearrange("p (j t) -> p j t", j=8)
        gtok = [None] * 8

        def gbu(j):
            b, t = yield from gproj("gb", j, HX, htok)
            sig_tile(lambda x: gtok.__setitem__(j, x), gb3[:, j, :], b, t, pair_last[2])
            yield
        run_pair(3, [gbu(j) for j in range(8)])
        PR.banks = [0, 1, 2, 3]
        mt = []
        for j in range(8):
            b, t = proj("pb", j, AX_, yb_tok, 0, 4)
            t1 = tt(gb3[:, j, :], gb3[:, j, :], PS[:, b, :], ALU.mult, t, gtok[j])
            free[b] = t1
            t2 = tt(MG3[:, j, :], MG3[:, j, :], gb3[:, j, :], ALU.add, t1, mtok[j])
            pending.append(lambda j=j, t2=t2: mt.append(split_from(MG3[:, j, :], HH, HL, j, t2)))
        flush(True)
        xtok = []
        pb_done = last_unit[0]
        nst = Stats([SS[0][:, 0:512], SS[0][:, 512:1024]], SS[1][:, 0:512])
        GP.wait(DV.last(), AC.last(), PE.last())
        htok = []
        for j in range(8):
            b, t = proj("out", j, HX, mt)
            t1 = tt(XT[:, j, :], XT[:, j, :], PS[:, b, :], ALU.add, t)
            free[b] = t1
            xtok.append(t1)
            htok.append(operand(j, XT[:, j, :], col("ffn_g", j), AX_, t1, pb_done))
            nst.add(XT[:, j, :], t1)
        out_done = last_unit[0]
        hooks.extend(norm_hooks(nst))

        def ffn(sfx, X, Y, htok, ar, dst3, dtok, accumulate, ydone, finished, first=None):
            sg = [ar(512), ar(512)]
            sr = [ar(512), ar(512)]
            pf = [ar(512), ar(512)]
            sgf, srf, pff = [None, None], [None, None], [None, None]
            down_done = ydone
            out = list(dtok)
            for a, e in FFN_PARTS:
                tk = []

                def gate(t_):
                    q = t_ % 2
                    b, t = yield from gproj("gate" + sfx, t_, X, htok)
                    t1 = scaled(sg[q], b, t, sgf[q])
                    free[b] = t1
                    t2 = act(sg[q], sg[q], ACT.Silu, t1)
                    sgf[q] = srf[q] = ptt(sr[q], sg[q], RB, ALU.mult, t2, RBT[0], pff[q])
                    yield

                def up(t_):
                    q = t_ % 2
                    b, t = yield from gproj("up" + sfx, t_, X, htok)
                    t2 = tt(pf[q], sr[q], PS[:, b, :], ALU.mult, t, srf[q], pff[q])
                    free[b] = t2
                    t3 = split_from(pf[q], Y[0], Y[1], t_ - a, t2, down_done)
                    pff[q] = t3
                    tk.append(t3)
                    yield

                rest = [u(t_) for t_ in range(a, e) for u in (gate, up)]
                if a == 0:
                    behind_norm(*rest[0:3], first)
                    rest = rest[3:]
                for u in rest:
                    run(u)
                up_done = last_unit[0]
                for j in range(8):
                    b, t = proj("down" + sfx, j, Y, tk, a, e - a)
                    if accumulate or a > 0:
                        out[j] = tt(dst3[:, j, :], dst3[:, j, :], PS[:, b, :], ALU.add, t, out[j])
                    else:
                        out[j] = vcopy(dst3[:, j, :], PS[:, b, :], t)
                    free[b] = out[j]
                    if e == 22:
                        finished(j, out[j], up_done)
                down_done = last_unit[0]
            return out

        arF = Arena(0)
        nst1 = Stats([arF(512), arF(512)], arF(512))
        nst2 = Stats([arF(512), arF(512)], arF(512))
        R1 = VT[:, :]
        htok2, sqt = [], []
        fence()

        def end1(j, t, up_done):
            htok2.append(operand(j, XT[:, j, :], GG[:, j:j + 1], AX_, t, up_done, tgg))
            nst1.add(XT[:, j, :], t)
            sqt.append(nst2.add(XT[:, j, :], t, scale=col("final_g", j)))

        xtok = ffn("", AX_, HX, htok, arF, XT, xtok, True, out_done, end1)
        def two_norms():
            r1, r2, r12 = RC[:, 0:4], RC[:, 4:8], RC[:, 8:12]
            b, tm = nst1.fold()
            free[b], t1 = inverse_root(r1, PS[:, b, 0:4], tm)
            b, tm = nst2.fold()
            t = tt(r2, PS[:, b, 0:4], r1, ALU.mult, tm, t1)
            free[b] = t
            t = tt(r2, r2, r1, ALU.mult, t)
            t = inverse_root(r2, r2, t)[1]
            t12[0] = tt(r12, r1, r2, ALU.mult, t)
            r1t[0] = t1

        def spread():
            RBT[0] = broadcast(RB, RC[:, 8:12], t12[0], gone=[DV.last(), GP.last()])
            r1t[0] = broadcast(R1, RC[:, 0:4], r1t[0])

        r1t, t12 = [None], [None]
        hooks.extend([two_norms, spread])
        htok = htok2
        down_done = last_unit[0]
        F = fence()
        SP.wait(*F)

        ar = Arena(0)
        EB, ENB, EKD = [ar(512), ar(512)], [ar(512), ar(512)], [ar(512), ar(512)]
        BLK = [AR[:, 0:992], AR[:, 1024:2016]]
        NQ = [ar(512) for _ in range(4)]
        NKC, NVC, NKS, NKW, NVS, NVW = [ar(512) for _ in range(6)]
        nsa_at = ar.at
        qe = [ar(512), ar(512)]
        ke = [ar(512), ar(512)]
        kdt = [ar(512), ar(512)]
        gv = [ar(1024), ar(1024)]
        kd, vtm = ar(512), ar(512)
        rr = ar(1024)
        St = [ar(256), ar(256)]
        on = ar(1024)
        gst = ar(32)
        yf = ar(512)
        th2 = ar(512)
        wa2 = ar(512)
        alr = ar(512)
        attn = alr
        dec = ar(32)
        reset = ar(512)
        kcT, vcs = AR[:, 2080:2112], AR[:, 2112:2240]
        hid, th3, w2s = ar(64), ar(64), ar(256)
        gts = kd
        t0 = SP.dma(lambda: nc.sync.dma_start(wa2[0:16, :], wa2_d), d_b2)
        tw2 = SP.dma(lambda: nc.sync.dma_start(w2s, w2_d), d_w2)
        t_rs = DV.op(lambda: V.memset(reset, 1.0))
        t_rs = DV.op(lambda: V.memset(reset.rearrange("p (n c) -> p n c", c=64)[:, :, 0:1], 0.0), t_rs)
        gq = {}
        g_last = {-2: None, -1: None}
        vt_free = [None]
        kd_free = [None]
        small = {}
        XO = AX_

        def small_unit():
            b, t = yield from gproj("small2", 0, XO, htok)
            small["a"] = scaled(alr[0:16, :], b, t, p0=0, p1=16)
            t1 = scaled(gts[0:24, :], b, t, p0=32, p1=56)
            free[b] = t1
            t2 = act(gts[0:24, :], gts[0:24, :], ACT.Tanh, t1, scale=0.5)

            def end():
                b, fr = TR.take()
                for n in range(4):
                    t = tp(PS[:, b, 24 * n:24 * n + 24], gts[0:24, n * 128:(n + 1) * 128], ident(24), t2, fr,
                           inc=(n == 3))
                small["g"] = ts(GT[:, :], PS[:, b, 0:96], 0.5, 0.5, ALU.mult, ALU.add, t)
                free[b] = small["g"]
                kd_free[0] = t
            pending.append(end)
            yield

        ZZ = [EB[0]] + NQ[0:3]
        EE = [ENB[0], NKS, NKW, NVS]

        def log_sigmoids():
            t3, t5 = [], []
            for h in range(4):
                b, fr = PR.take()
                t = mm(PS[:, b, :], wa2[0:16, h * 128:(h + 1) * 128], alr[0:16, :], True, True, t0, small["a"], fr,
                       inc=True)
                t3.append(ts(ZZ[h], PS[:, b, :], col("balpha", h), None, ALU.add, ALU.bypass, t))
                free[b] = t3[h]
                t4 = stt(EE[h], ZZ[h], -1.0, ZZ[h], ALU.mult, ALU.max, t3[h])
                t5.append(act(EE[h], EE[h], ACT.Exp, t4, scale=-1.0))
            for h in range(4):
                t5[h] = act(EE[h], EE[h], ACT.Ln, t5[h], bias=col("one"))

            def finish():
                small["attn"] = DV.op(lambda: V.memset(attn, 0.0), t)
                for h in range(4):
                    small[("ls", h)] = stt(ZZ[h], ZZ[h], 0.0, EE[h], ALU.min, ALU.subtract, t5[h], t3[h])
                run(decays(0))
            pending.append(finish)
            return
            yield

        def decays(h):
            gone = gq.get((h - 2, "k"))
            z, e, w = EB[h % 2], ENB[h % 2], EKD[h % 2]
            w3 = w.rearrange("p (n c) -> p n c", c=64)
            t7 = DV.op(lambda: V.tensor_tensor_scan(w, reset, ZZ[h], 0.0, ALU.mult, ALU.add), small[("ls", h)],
                       t_rs, gone)
            small[("b", h)] = t7
            t8 = act(z, w, ACT.Exp, t7, gone, scale=1.0 / 16)
            t9 = act(e, w, ACT.Exp, t7, gone, scale=-1.0 / 16)

            def scale():
                td = vcopy(dec[:, 8 * h:8 * h + 8], z.rearrange("p (n c) -> p n c", c=64)[:, :, 63:64], t8)
                t10 = tt(w3, w3[:, :, 63:64].to_broadcast([128, 8, 64]), w3, ALU.subtract, t8, t9, t7)
                t11 = act(w, w, ACT.Exp, t10, scale=1.0 / 16)
                small[("eb", h)] = tt(z, z, RB, ALU.mult, t8, td, RBT[0])
                small[("enb", h)] = tt(e, e, RB, ALU.mult, t9, RBT[0])

                def rest():
                    small[("ekd", h)] = tt(w, w, RB, ALU.mult, t11, RBT[0])
                pending.append(rest)
            pending.append(scale)
            return
            yield

        def gla_unit(h, what):
            if what == 0:
                b, t = yield from gproj("gq", h, XO, htok)
                gq[(h, 0)] = free[b] = stt(qe[h % 2], PS[:, b, :], float(128 ** -0.5), EB[h % 2], ALU.mult, ALU.mult,
                                           t, small[("eb", h)], g_last[h - 2])
            elif what == 1:
                b, t = yield from gproj("gk", h, XO, htok)
                gq[(h, 1)] = tt(ke[h % 2], PS[:, b, :], ENB[h % 2], ALU.mult, t, small[("enb", h)], g_last[h - 2])
                t2 = tt(kd, PS[:, b, :], EKD[h % 2], ALU.mult, small[("ekd", h)], kd_free[0])
                free[b] = gq[(h, "k")] = t2

                def end():
                    x, gq[(h, 2)] = to_tokens(kd, kdt[h % 2].rearrange("p (t e) -> p t e", t=4), t2, g_last[h - 2])
                    kd_free[0] = x
                pending.append(end)
            else:
                j = what - 2
                b, t = yield from gproj("gv", 2 * h + j, XO, htok)
                t1 = scaled(vtm, b, t, vt_free[0])
                free[b] = t1

                def end():
                    x, gq[(h, 3 + j)] = to_tokens(vtm, gv[h % 2].rearrange("p (t e) -> p t e", t=4)
                                                  [:, :, j * 128:(j + 1) * 128], t1, g_last[h - 2])
                    vt_free[0] = x
                pending.append(end)
            yield

        ntok = {}

        def nsa_unit(name, i):
            b, t = yield from gproj(name, i, XO, htok)
            if name == "nq":
                ntok[("nq", i)] = free[b] = scaled(NQ[i], b, t, small[("b", 3)], scale=0.125)
            elif name in ("vs", "vw"):
                t1 = scaled(vtm, b, t, vt_free[0])
                free[b] = t1

                def end():
                    x, ntok[name] = to_tokens(vtm, {"vs": NVS, "vw": NVW}[name].rearrange("p (t e) -> p t e", t=4), t1)
                    vt_free[0] = x
                pending.append(end)
            else:
                ntok[name] = free[b] = scaled({"kc": NKC, "vc": NVC, "ks": NKS, "kw": NKW}[name], b, t)
            yield

        def compress_blocks(c):
            src, pe_ = ((NKC, "pek"), (NVC, "pev"))[c]
            win = bass.AP(src.tensor, src.offset, [list(src.ap[0]), [1, 32], [16, 31]])
            pex = COL[:, COLS[pe_]:COLS[pe_] + 32]
            peb = bass.AP(pex.tensor, pex.offset, [list(pex.ap[0]), [1, 32], [0, 31]])
            ntok[("blk", c)] = tt(BLK[c].rearrange("p (l n) -> p l n", l=32), win, peb, ALU.add,
                                  ntok[("kc", "vc")[c]], gq[(3, 0)], gq[(3, 1)], gq[(3, "k")])
            return
            yield

        def compress_1(c):
            b, fr = PR.take()
            for m in range(4):
                i = open_unit((("w1k", "w1v")[c], m, 0, 8))
                for l in range(8):
                    L = 8 * m + l
                    t = mm(PS[:, b, 0:31], RAW[:, i % NR, l * 128:(l + 1) * 128], BLK[c][:, 31 * L:31 * L + 31],
                           L == 0, L == 31, split_done[i], ntok[("blk", c)], fr, inc=(l == 7))
                used[i] = t
                load_more()
                yield
            h_, x_ = hid[:, 32 * c:32 * c + 31], th3[:, 32 * c:32 * c + 31]
            t2 = act(x_, PS[:, b, 0:31], ACT.Tanh, t, scale=0.5)
            t3 = ts(x_, x_, 0.5, 0.5, ALU.mult, ALU.add, t2)
            free[b] = ntok[("hid", c)] = tt(h_, x_, PS[:, b, 0:31], ALU.mult, t3)

        def compress_2(c):
            h_ = hid[:, 32 * c:32 * c + 31]
            b, fr = TR.take()
            if c == 0:
                t = mm(PS[:, b, 0:31], w2s[:, 0:128], h_, True, True, ntok[("hid", 0)], tw2, fr, inc=True)
                ntok["kcT"] = free[b] = vcopy(kcT[:, 0:31], PS[:, b, 0:31], t)
            else:
                t = mm(PS[0:31, b, 0:128], h_, w2s[:, 128:256], True, True, ntok[("hid", 1)], tw2, fr, inc=True)
                ntok["vcs"] = free[b] = vcopy(vcs[0:31, :], PS[0:31, b, 0:128], t)
            return
            yield

        def gla_units(h):
            return [gla_unit(h, 2), gla_unit(h, 3), gla_unit(h, 0), gla_unit(h, 1)]

        r_free = [None, None]
        th_free = [None]

        def gla_r(h, j):
            b, t = yield from gproj("gr", 2 * h + j, XO, htok)
            rj = rr[:, j * 512:(j + 1) * 512]
            t0_ = scaled(rj, b, t, r_free[j])
            free[b] = t0_
            t1 = act(th2, rj, ACT.Tanh, t0_, th_free[0], scale=0.5)

            def end():
                gq[(h, "r", j)] = th_free[0] = stt(rj, th2, 1.0, rj, ALU.add, ALU.mult, t1)
            pending.append(end)
            yield

        gu = gla_units(0)
        PR.banks = [0, 1, 2, 3]
        behind_norm(small_unit(), gu[0], gu[1])
        for u in [log_sigmoids(), gla_r(0, 0), gla_r(0, 1)] + gu[2:]:
            run(u)
        flush(True)

        def final_norm(j):
            xtok[j] = stt(XT[:, j, :], XT[:, j, :], col("final_g", j), R1, ALU.mult, ALU.mult, xtok[j], htok2[j],
                          r1t[0], sqt[j])
            if j < 7:
                pending.append(lambda: final_norm(j + 1))

        pending.append(lambda: final_norm(0))
        att_free = [small["attn"]]
        st_free = [None, None]
        on_free = [None]
        yg_tok = [None] * 8
        yf, yf_free = [yf, wa2], [small["attn"], small["attn"]]
        glam = con("glam").bitcast(i32)
        for h in range(4):
            PR.banks = [0, 1]
            units = [gla_r(h, j) for j in (0, 1)] if h else []
            if h < 3:
                units += [decays(h + 1)] + gla_units(h + 1)
            else:
                units += [nsa_unit("kc", 0), nsa_unit("vc", 0), compress_blocks(0), compress_blocks(1),
                          compress_1(0)]
                units += [nsa_unit("nq", i) for i in range(4)] + [compress_1(1), compress_2(0)]
                units += [nsa_unit(n, 0) for n in ("ks", "kw", "vs", "vw")] + [compress_2(1)]
            fill = Filler(units, 20)
            q_, k_, kt_, v_ = qe[h % 2], ke[h % 2], kdt[h % 2], gv[h % 2]
            v3 = v_.rearrange("p (t e) -> p t e", t=4)
            b = SB[0]
            for T_ in range(4):
                o = T_ * 128
                t = mm(PS[:, b, o:o + 128], k_[:, o:o + 128], q_[:, o:o + 128], True, True, gq[(h, 0)], gq[(h, 1)],
                       free[b], inc=(T_ == 3))
            mask3 = bass.AP(glam.tensor, glam.offset, [list(glam.ap[0]), [0, 4], [1, 128]])
            ta = DV.op(lambda b=b: V.copy_predicated(attn.rearrange("p (t c) -> p t c", t=4), mask3,
                                                     PS[:, b, :].rearrange("p (t c) -> p t c", t=4)),
                       t, att_free[0])
            free[b] = ta
            tst = None
            fill(2)
            for T_ in range(4):
                ob = (OB, SB[0])[T_ % 2]
                up_ = {}
                for n in (2 * T_, 2 * T_ + 1):
                    if n == 7:
                        continue
                    pb = 64 * (n % 2)
                    ub = SB[1 + n % 2]
                    up_[n] = (ub, mm(PS[:, ub, 0:256], kt_[pb:pb + 64, T_ * 128:(T_ + 1) * 128], v3[pb:pb + 64, T_, :],
                                     True, True, gq[(h, 2)], gq[(h, 3)], gq[(h, 4)], free[ub], inc=True))
                fill()
                if T_:
                    scale_o()
                for p0, p1, whole in ((0, 128, False),) if T_ else ((0, 64, True), (64, 128, False)):
                    t = mm(PS[p0:p1, ob, 0:256], attn[:, T_ * 128 + p0:T_ * 128 + p1], v3[:, T_, :], True, whole,
                           ta, free[ob], inc=True)
                for n in (2 * T_, 2 * T_ + 1):
                    pb = 64 * (n % 2)
                    if n > 0:
                        t = mm(PS[pb:pb + 64, ob, 0:256], q_[:, n * 64:n * 64 + 64], St[(n - 1) % 2], False, True,
                               tst, inc=True)
                        st_free[(n - 1) % 2] = t
                    if n < 7:
                        ub, tu = up_[n]
                        if n == 0:
                            tst = vcopy(St[0], PS[:, ub, 0:256], tu, st_free[0])
                        else:
                            tst = stt(St[n % 2], St[(n - 1) % 2], dec[:, 8 * h + n:8 * h + n + 1],
                                      PS[:, ub, 0:256], ALU.mult, ALU.add, tu, tst, st_free[n % 2])
                        free[ub] = tst
                    fill()
                ss, rs = gst[:, T_:T_ + 1], gst[:, 8 + T_:9 + T_]
                onv = on[:, T_ * 256:(T_ + 1) * 256]
                t1 = AC.op(lambda onv=onv, ss=ss, ob=ob: A.activation(onv, PS[:, ob, 0:256], ACT.Square, accum_out=ss),
                           t, on_free[0])
                t2 = power(rs, ss, 1.0 / 256, t1)

                def scale_o(onv=onv, ob=ob, rs=rs, t2=t2):
                    free[ob] = ts(onv, PS[:, ob, 0:256], rs, 0.5, ALU.mult, ALU.mult, t2)
                    return free[ob]
            g_last[h] = t
            att_free[0] = t
            t3 = scale_o()
            fill(3)
            tb = []
            for j in (0, 1):
                b, fr = TR.take()
                for t_ in range(4):
                    t = tp(PS[:, b, t_ * 128:(t_ + 1) * 128], on[:, t_ * 256 + j * 128:t_ * 256 + j * 128 + 128],
                           ident(), t3, fr, inc=(t_ == 3))
                tb.append((b, t))
            t4 = []
            for j, (b, t) in enumerate(tb):
                t4.append(stt(yf[j], PS[:, b, :], col("glag", j), rr[:, j * 512:(j + 1) * 512], ALU.mult, ALU.mult, t,
                              gq[(h, "r", j)], yf_free[j]))
                free[b] = t4[j]
                r_free[j] = t4[j]
            on_free[0] = t
            fill()
            for j in (0, 1):
                yf_free[j] = yg_tok[2 * h + j] = split_from(yf[j], HH, HL, 2 * h + j, t4[j], down_done)
            fill()
            fill.drain(h == 3)
        F = fence()
        tkc, tvc, tg2 = ntok["kcT"], ntok["vcs"], small["g"]
        ar = Arena(0)
        yb = ar(2048)
        st = ar(32)
        ar = Arena(nsa_at)
        MGN = ar(8192)
        MG3 = MGN[:, 0:4096].rearrange("p (j t) -> p j t", j=8)
        SN3 = MGN[:, 4096:8192].rearrange("p (j t) -> p j t", j=8)
        SS = [ar(1056), ar(1056)]
        PT = ar(1280)
        yb3 = yb.rearrange("p (n c) -> p n c", n=4)
        ss_free = [None, None]
        pt_free = [None]
        sc_free = [None, None]
        mtok, stok = [None] * 8, [None] * 8
        sgt_free = [None]
        SGT = VT[:, :]

        def merge_units(j):
            def a():
                b, t = yield from gproj("mg", j, XO, htok)
                sig_tile(lambda x: sgt_free.__setitem__(0, x), SGT, b, t, sgt_free[0], xtok[7])
                yield

            def c():
                b, t = yield from gproj("pg", j, HX, yg_tok)
                mtok[j] = tt(MG3[:, j, :], SGT, PS[:, b, :], ALU.mult, t, sgt_free[0])
                free[b] = mtok[j]
                sgt_free[0] = mtok[j]
                yield

            def d():
                b, t = yield from gproj("mn", j, XO, htok)
                sig_tile(lambda x: stok.__setitem__(j, x), SN3[:, j, :], b, t)
                yield
            return [a(), c(), d()]

        fill = []
        for j in range(8):
            fill += merge_units(j)

        def nsa_a(it):
            h, n = it
            par = ORD_N.index(n) % 2
            i = h % 4
            p = slice(64 * (h // 4), 64 * (h // 4) + 64)
            W = 128 * (n + 1)
            qv = NQ[i][p, n * 128:(n + 1) * 128]
            ta_ = mm(PS[:, SB[0], 0:W], qv, NKS[p, 0:W], True, True, ntok[("nq", i)], ntok["ks"], free[SB[0]], inc=True)
            tb_ = mm(PS[:, SB[1], 0:W], qv, NKW[p, 0:W], True, True, ntok["kw"], free[SB[1]], inc=True)
            tc_ = mm(PS[:, SB[2], 0:31], qv, kcT[p, 0:31], True, True, tkc, free[SB[2]], inc=True)
            return lambda: nsa_s(it, tb_, tc_)

        def nsa_s(it, tb_, tc_):
            h, n = it
            par = ORD_N.index(n) % 2
            W = 128 * (n + 1)
            slope = float(2.0 ** (-8.0 * (h + 1) / 8))
            Sx = SS[par]
            ba = con("ba", 128 * (3 - n), 512)
            ba2 = bass.AP(ba.tensor, ba.offset, [list(ba.ap[0]), [0, 2], [1, W]])
            t1 = stt(Sx[:, 0:2 * W].rearrange("p (g k) -> p g k", g=2), ba2, slope, PS[:, SB[0]:SB[0] + 2, 0:W],
                     ALU.mult, ALU.add, tb_, ss_free[par])
            free[SB[0]] = free[SB[1]] = t1
            Sc = Sx[:, 1024:1055]
            t2 = stt(Sc, con("bc", 31 * n, 31 * n + 31), slope, PS[:, SB[2], 0:31], ALU.mult, ALU.add, tc_)
            free[SB[2]] = t2
            nm, l = st[:, 3 * par:3 * par + 3], st[:, 8 + 3 * par:11 + 3 * par]
            t3 = DV.op(lambda: V.tensor_reduce(nm[:, 1:3], Sx[:, 0:2 * W].rearrange("p (g k) -> p g k", g=2), AX,
                                               ALU.max, negate=True), t1, sc_free[par])
            t3 = DV.op(lambda: V.tensor_reduce(nm[:, 0:1], Sc, AX, ALU.max, negate=True), t2)
            AC.op(lambda: A.activation(Sc, Sc, ACT.Exp, bias=nm[:, 0:1], accum_out=l[:, 0:1]), t3)
            AC.op(lambda: A.activation(Sx[:, 0:W], Sx[:, 0:W], ACT.Exp, bias=nm[:, 1:2], accum_out=l[:, 1:2]))
            t4 = AC.op(lambda: A.activation(Sx[:, W:2 * W], Sx[:, W:2 * W], ACT.Exp, bias=nm[:, 2:3],
                                            accum_out=l[:, 2:3]))
            return t4, (par, l)

        def nsa_b(it, tS, info, fill, softmax):
            h, n = it
            par, l = info
            Sx = SS[par]
            W = 128 * (n + 1)
            g_ = h // 4
            Sc = Sx[:, 1024:1055]
            t5 = tt(Sc, Sc, con("m01", 31 * n, 31 * n + 31), ALU.mult, tS)
            tl, ev = transposes(Sx, 2 * (n + 1), tS, lambda: None, 1)
            b, fr = TR.take()
            tl = tp(PS[0:31, b, 0:128], Sc, ident(), t5, fr, inc=True)
            e2 = free[b] = acopy(PT[0:31, 1024:1152], PS[0:31, b, 0:128], tl, pt_free[0])
            ss_free[par] = tl
            t6 = DV.op(lambda: V.reciprocal(l, l), tS)
            t6 = tt(l, l, GT[:, 24 * n + 3 * h:24 * n + 3 * h + 3], ALU.mult, t6, tg2)
            nxt = softmax() if softmax else None
            fill()
            for br, (vv, c0) in enumerate(((NVS, 64), (NVW, 128))):
                for j in range(n + 1):
                    m = br * (n + 1) + j
                    mm(PS[:, OB, c0:c0 + 64], PT[:, m * 128:(m + 1) * 128],
                       vv[:, j * 128 + 64 * g_:j * 128 + 64 * g_ + 64], j == 0, j == n, ev, ntok["vs"], ntok["vw"],
                       free[OB])
            t = mm(PS[:, OB, 0:64], PT[0:31, 1024:1152], vcs[0:31, 64 * g_:64 * g_ + 64], True, True, e2, tvc,
                   inc=True)
            pt_free[0] = t
            y = yb3[:, n, 64 * h:64 * h + 64]
            t7 = ts(y, PS[:, OB, 0:64], l[:, 0:1], None, ALU.mult, ALU.bypass, t, t6)
            t7 = stt(y, PS[:, OB, 64:128], l[:, 1:2], y, ALU.mult, ALU.add, t7)
            t7 = stt(y, PS[:, OB, 128:192], l[:, 2:3], y, ALU.mult, ALU.add, t7)
            free[OB] = t7
            sc_free[par] = t7
            return t7, nxt

        items = [(h, n) for h in range(8) for n in ORD_N]
        fill = Filler(fill, 3 * len(items))
        nxt = nsa_a(items[0])()
        for m, it in enumerate(items):
            part = lambda w=WORK[it[1]]: fill(w)
            part()
            cur = nxt
            sm = nsa_a(items[m + 1]) if m + 1 < len(items) else None
            part()
            t7, nxt = nsa_b(it, *cur, part, sm)
        fill.drain()
        PR.banks = [0, 1, 2, 3]
        pg_done = last_unit[0]
        yn_tok = []
        for j in range(4):
            b, fr = TR.take()
            for n in range(4):
                t = tp(PS[:, b, n * 128:(n + 1) * 128], yb3[:, n, j * 128:(j + 1) * 128], ident(), t7, fr,
                       inc=(n == 3))
            x = split_from(PS[:, b, :], HH, HL, j, t, pg_done)
            free[b] = x
            yn_tok.append(x)
        mt = []
        for j in range(8):
            b, t = proj("pn", j, HX, yn_tok, 0, 4)
            t1 = tt(SN3[:, j, :], SN3[:, j, :], PS[:, b, :], ALU.mult, t, stok[j])
            free[b] = t1
            t2 = tt(MG3[:, j, :], MG3[:, j, :], SN3[:, j, :], ALU.add, t1, mtok[j])
            pending.append(lambda j=j, t2=t2: mt.append(split_from(MG3[:, j, :], AH, AL, j, t2, pg_done)))
        flush(True)
        pn_done = last_unit[0]

        def post(name, src3, stats, ar, then, both=()):
            b, tm = stats.fold()
            free[b], t = inverse_root(RC[:, 0:4], PS[:, b, 0:4], tm, PE.last())
            b1, te = broadcast(None, RC[:, 0:4], t)
            tmp = [ar(512), ar(512)]
            last = [None, None]
            for j in range(9):
                if j < 8:
                    t = stt(tmp[j % 2], src3[:, j, :], col(name, j), PS[:, b1, :], ALU.mult, ALU.mult, te,
                            last[j % 2])
                    free[b1] = t
                if j:
                    then(j - 1, last[(j - 1) % 2])
                if j < 8:
                    add = tt if j in both else ptt
                    last[j % 2] = add(XT[:, j, :], XT[:, j, :], tmp[j % 2], ALU.add, t, xtok[j])

        ar = Arena(0)
        ost = Stats([ar(512), ar(512)], ar(512))
        F = [PE.last()]
        ar = Arena(nsa_at + 8192)
        ptm = ar
        OT = MG3
        ost.last = [F, F]
        AC.wait(F)
        GP.wait(F)
        for j in range(8):
            b, t = proj("out2", j, AX_, mt)
            free[b] = vcopy(OT[:, j, :], PS[:, b, :], ost.add(PS[:, b, :], t), mt[7])
        out2_done = last_unit[0]
        htok, sqt = [], []

        def then2(j, t):
            htok.append(operand(j, XT[:, j, :], col("fpre2", j), HX, t, pn_done))
            sqt.append(act(SN3[:, j, :], XT[:, j, :], ACT.Square, t))
            xtok[j] = t

        post("post2", OT, ost, ptm, then2, (0,))

        def squares():
            b, fr = TR.take()
            for j in range(8):
                for q in range(4):
                    t = mm(PS[:, b, q:q + 1], SN3[:, j, q * 128:(q + 1) * 128], con("mean", 0, 1), j + q == 0, j + q == 10,
                           sqt[j], fr, inc=(j == 7 and q == 3))
                if j % 2 and j < 7:
                    yield
            free[b], t = inverse_root(RC[:, 0:4], PS[:, b, 0:4], t)

            def spread2():
                RBT[0] = broadcast(RB, RC[:, 0:4], t, gone=[DV.last(), GP.last()])
            hooks.append(spread2)

        ar = Arena(0)
        OT = ar(4096).rearrange("p (j t) -> p j t", j=8)
        fst = Stats([ar(512), ar(512)], ar(512))

        def end2(j, t, up_done):
            fst.add(OT[:, j, :], t)

        ffn("2", HX, AX_, htok, ar, OT, [None] * 8, False, out2_done, end2, squares())

        def store(j, t):
            q, e = ((SP, nc.sync), (AC, nc.scalar))[j % 2]
            store.t.append(q.dma(lambda: e.dma_start(out_d[:, j, :], XT[:, j, :]), d_out[j % 2], t))

        store.t = []
        post("fpost2", OT, fst, ar, store, (2, 5, 7))
        SP.wait(store.t[-2], store.t[-1])

        assert len(used) == len(order)
        block = ctx.enter_context(nc.Block())

        @block.sync
        def _(eng):
            SP.replay(eng)

        @block.scalar
        def _(eng):
            AC.replay(eng)

        @block.gpsimd
        def _(eng):
            GP.replay(eng)

        @block.vector
        def _(eng):
            DV.replay(eng)

        @block.tensor
        def _(eng):
            PE.replay(eng)


def constant_tables():
    con = np.zeros((128, NCON), np.float32)
    p = np.arange(128)
    con[:, CON["ident"]:CON["ident"] + 128] = np.eye(128)
    con[:, CON["big"]:CON["big"] + 128] = np.where(p[None, :] < p[:, None], 1e30, 0.0)
    con[:, CON["mean"]:CON["mean"] + 128] = 1.0 / 1024
    for h in range(4):
        con[h, CON["sel"] + 128 * h:CON["sel"] + 128 * h + 128] = 1.0
    dist = 384 + p[:, None] - np.arange(512)[None, :]
    con[:, CON["ba"]:CON["ba"] + 512] = np.where(dist >= 0, -dist, NEG)
    end = 16 * np.arange(31) + 31
    for n in range(4):
        t = 128 * n + p[:, None]
        ok = end[None, :] <= t
        con[:, CON["bc"] + 31 * n:CON["bc"] + 31 * n + 31] = np.where(ok, -(t - end[None, :]), NEG)
        con[:, CON["m01"] + 31 * n:CON["m01"] + 31 * n + 31] = ok
    con[:, CON["glam"]:CON["glam"] + 128] = (p[:, None] <= p[None, :]) & (p[:, None] // 64 == p[None, :] // 64)
    oh = np.zeros((33, 3, 640), np.float32)
    for g, (win, dil) in enumerate(((128, 1), (512, 4), (2048, 16))):
        for i in range(640):
            d = i - 127
            if d < 0 or d > win or d % dil:
                oh[32, g, i] = 1.0
                continue
            if d < 16:
                bkt = d
            else:
                bkt = min(31, 16 + int(np.float32(np.log(np.float32(d) / np.float32(16)) / np.float32(np.log(128.0))
                                                  * np.float32(16))))
            oh[bkt, g, i] = 1.0
    return con, oh.reshape(33, 1920)


def pack_units(inputs):
    w_in, w_in2 = inputs["w_in"][0], inputs["w_in_2"][0]
    pts = np.cumsum([0, 1024, 1024, 1024, 8, 1024, 1536, 1536, 1536, 1024, 1024])
    names = ["qm", "km", "vm", "if_", "om", "qa", "ka", "va", "ga", "gb"]
    m = {n: w_in[:, pts[i]:pts[i + 1]] for i, n in enumerate(names)}
    z = np.zeros((1024, 128), np.float32)
    z[:, 0:4] = m["if_"][:, 0:4]
    z[:, 32:36] = m["if_"][:, 4:8]
    m["if"] = z
    pts = np.cumsum([0, 512, 512, 1024, 1024, 16, 512, 128, 128, 128, 128, 128, 128, 24, 1024, 1024])
    names = ["gq", "gk", "gv", "gr", "al", "nq_", "kc", "vc", "ks", "vs", "kw", "vw", "gt", "mg", "mn"]
    m.update({n: w_in2[:, pts[i]:pts[i + 1]] for i, n in enumerate(names)})
    z = np.zeros((1024, 128), np.float32)
    z[:, 0:16] = m["al"]
    z[:, 32:56] = m["gt"]
    m["small2"] = z
    q = m["nq_"].reshape(1024, 2, 4, 64)
    m["nq"] = np.ascontiguousarray(q.transpose(0, 2, 1, 3)).reshape(1024, 512)
    m.update({"pa": inputs["w_proj_a"][0], "pb": inputs["w_proj_b"][0], "out": inputs["w_out"][0],
              "gate": inputs["w_gate"][0], "up": inputs["w_up"][0], "down": inputs["w_down"][0],
              "pg": inputs["w_proj_gla_2"][0], "pn": inputs["w_proj_nsa_2"][0], "out2": inputs["w_out_2"][0],
              "gate2": inputs["w_ffn_gate_2"][0], "up2": inputs["w_ffn_up_2"][0], "down2": inputs["w_ffn_down_2"][0]})
    order = unit_order()
    w = np.zeros((len(order), 128, 1024), np.float32)
    for n, k in (("w1k", "nsa_cmp_w1_k_2"), ("w1v", "nsa_cmp_w1_v_2")):
        x = inputs[k][0].reshape(32, 64, 64).transpose(1, 0, 2)
        bd = np.zeros((128, 32, 128), np.float32)
        bd[0:64, :, 0:64] = x
        bd[64:128, :, 64:128] = x
        m[n] = bd
    for i, (name, j, k0, nk) in enumerate(order):
        if name in ("w1k", "w1v"):
            w[i] = m[name][:, 8 * j:8 * j + 8, :].reshape(128, 1024)
            continue
        blk = m[name][k0 * 128:(k0 + nk) * 128, j * 128:(j + 1) * 128]
        w[i, :, 0:nk * 128] = blk.reshape(nk, 128, 128).transpose(1, 0, 2).reshape(128, nk * 128)
    return w


def pack_cols(inputs):
    c = np.zeros((128, NCOL), np.float32)

    def put(name, vec):
        v = vec.reshape(-1, 128).T
        c[:, COLS[name]:COLS[name] + v.shape[1]] = v

    put("mix_g", inputs["norm_mix_g"][0])
    cw = inputs["conv_w"][0]
    c[:, COLS["conv_w"]:COLS["conv_w"] + 64] = cw.reshape(4, 16, 128).transpose(2, 1, 0).reshape(128, 64)
    put("conv_b", inputs["conv_b"][0])
    put("mnorm", inputs["mlstm_norm_g"][0])
    put("ffn_g", inputs["norm_ffn_g"][0])
    put("final_g", inputs["norm_final_g"])
    put("pre2", inputs["norm_mix_pre_2"][0])
    put("post2", inputs["norm_mix_post_2"][0])
    put("fpre2", inputs["norm_ffn_pre_2"][0])
    put("fpost2", inputs["norm_ffn_post_2"][0])
    put("balpha", inputs["gla_b_alpha_2"][0])
    put("glag", inputs["gla_norm_g_2"][0])
    b = inputs["b_gate_if"][0]
    c[0:4, COLS["bif"]] = b[0:4]
    c[0:4, COLS["bif"] + 1] = b[4:8]
    c[:, COLS["eps"]] = EPS
    c[:, COLS["one"]] = 1.0
    c[:, COLS["nhalf"]:COLS["nhalf"] + 4] = -0.5
    for n, k in (("pek", "nsa_cmp_pe_k_2"), ("pev", "nsa_cmp_pe_v_2")):
        pe = inputs[k][0].T
        c[0:64, COLS[n]:COLS[n] + 32] = pe
        c[64:128, COLS[n]:COLS[n] + 32] = pe
    return c


def kernel(**inputs):
    import concourse.bacc as bacc
    from concourse.bass_utils import run_bass_kernel_spmd

    inputs = {k: np.asarray(v) for k, v in inputs.items()}
    con, oh = constant_tables()
    x = inputs["x"][0]
    arrays = {
        "xT": np.ascontiguousarray(x.T.reshape(8, 128, 512).transpose(1, 0, 2)),
        "wst": pack_units(inputs),
        "con": con,
        "col": pack_cols(inputs),
        "relb": np.ascontiguousarray(inputs["rel_bias"]),
        "oh": oh,
        "wa2": np.ascontiguousarray(inputs["gla_w_alpha2_2"][0]),
    }
    w2 = np.zeros((128, 256), np.float32)
    for i, k in enumerate(("nsa_cmp_w2_k_2", "nsa_cmp_w2_v_2")):
        w2[0:64, 128 * i:128 * i + 64] = inputs[k][0]
        w2[64:128, 128 * i + 64:128 * i + 128] = inputs[k][0]
    arrays["w2"] = w2

    nc = bacc.Bacc("TRN2", target_bir_lowering=False, num_devices=1)
    f32 = mybir.dt.float32
    aps = [nc.dram_tensor(n, arrays[n].shape, f32, kind="ExternalInput").ap()
           for n in ("xT", "wst", "con", "col", "relb", "oh", "wa2", "w2")]
    out = nc.dram_tensor("out", (128, 8, 512), f32, kind="ExternalOutput").ap()
    scr = nc.dram_tensor("scr", (3, 24, 640), f32, kind="Internal").ap()
    build(nc, *aps, out, scr)
    r = run_bass_kernel_spmd(nc, [arrays], core_ids=[0])
    y = r.results[0]["out"]
    return np.ascontiguousarray(y.transpose(1, 0, 2).reshape(1024, 512).T)[None]
```
